# Optimizing a Trainium2 kernel written in Bass

```python
import math
import jax, jax.numpy as jnp
from jax import lax
import numpy as np

D_MODEL = 1024
BATCH = 1
SEQ = 256
DEPTH = 1

N_META = 16
BLOCK = 128
PAD_FRONT = BLOCK - N_META
N_HEADS = 8
QK_NOPE = 64
QK_ROPE = 32
V_DIM = 64
Q_LORA = 256
KV_LORA = 128
ROPE_THETA = 10000.0
ATTN_SCALE = (QK_NOPE + QK_ROPE) ** -0.5
ATTN_WIDTH = N_HEADS * V_DIM
CONV_DIM = 512
CONV_GROUPS = 8
CONV_W = 3
MIX_WIDTH = ATTN_WIDTH + CONV_DIM
IN_COLS = Q_LORA + KV_LORA + QK_ROPE + 3 * CONV_DIM
SPLITS = [Q_LORA, Q_LORA + KV_LORA, Q_LORA + KV_LORA + QK_ROPE,
          Q_LORA + KV_LORA + QK_ROPE + CONV_DIM, Q_LORA + KV_LORA + QK_ROPE + 2 * CONV_DIM]
N_GROUPS = 4
EXPERTS_PER_GROUP = 8
N_EXPERTS = N_GROUPS * EXPERTS_PER_GROUP
TOP_K = 2
D_FF = 256
EPS = 1e-6
NEG_INF = -1e30


def rms_norm(x, g):
    xf = x.astype(jnp.float32)
    y = xf * lax.rsqrt(jnp.mean(xf * xf, axis=-1, keepdims=True) + EPS)
    return (y * g.astype(jnp.float32)).astype(x.dtype)

def rope_angles(pos):
    inv_freq = 1.0 / (ROPE_THETA ** (jnp.arange(0, QK_ROPE, 2, dtype=jnp.float32) / QK_ROPE))
    ang = pos.astype(jnp.float32)[..., None] * inv_freq
    return jnp.cos(ang), jnp.sin(ang)

def apply_rope(x, cos, sin):
    xf = x.astype(jnp.float32)
    x1, x2 = jnp.split(xf, 2, axis=-1)
    return jnp.concatenate([x1 * cos - x2 * sin, x2 * cos + x1 * sin], axis=-1).astype(x.dtype)

def causal_block_attention(q_nope, q_rope, k_nope, k_rope, v):
    bsz, plen = q_nope.shape[0], q_nope.shape[1]
    nb = plen // BLOCK
    qn = q_nope.reshape(bsz, nb, BLOCK, N_HEADS, QK_NOPE).transpose(1, 0, 2, 3, 4)
    qr = q_rope.reshape(bsz, nb, BLOCK, N_HEADS, QK_ROPE).transpose(1, 0, 2, 3, 4)
    starts = jnp.arange(nb, dtype=jnp.int32) * BLOCK
    k_idx = jnp.arange(plen, dtype=jnp.int32)

    def one_block(args):
        qn_b, qr_b, s0 = args
        s = (jnp.einsum('bqhd,bkhd->bhqk', qn_b, k_nope, preferred_element_type=jnp.float32)
             + jnp.einsum('bqhr,bkr->bhqk', qr_b, k_rope, preferred_element_type=jnp.float32)) * ATTN_SCALE
        q_idx = s0 + jnp.arange(BLOCK, dtype=jnp.int32)
        mask = (k_idx[None, :] >= PAD_FRONT) & (k_idx[None, :] <= q_idx[:, None])
        s = jnp.where(mask[None, None], s, NEG_INF)
        p = jax.nn.softmax(s, axis=-1).astype(v.dtype)
        return jnp.einsum('bhqk,bkhd->bqhd', p, v)

    out = lax.map(one_block, (qn, qr, starts))
    return out.transpose(1, 0, 2, 3, 4).reshape(bsz, plen, N_HEADS * V_DIM)

def hybrid_mixer(h, cos, sin, w_in, q_norm, w_uq, kv_norm, w_ukv, conv_w,
                 attn_out_norm, conv_out_norm, w_out):
    bsz = h.shape[0]
    hp = jnp.pad(h, ((0, 0), (PAD_FRONT, 0), (0, 0)))
    plen = hp.shape[1]
    z = hp @ w_in
    c_q, c_kv, k_pe, gate_b, gate_c, x_in = jnp.split(z, SPLITS, axis=-1)

    q = (rms_norm(c_q, q_norm) @ w_uq).reshape(bsz, plen, N_HEADS, QK_NOPE + QK_ROPE)
    q_nope = q[..., :QK_NOPE]
    q_rope = apply_rope(q[..., QK_NOPE:], cos[:, :, None, :], sin[:, :, None, :])
    kv = (rms_norm(c_kv, kv_norm) @ w_ukv).reshape(bsz, plen, N_HEADS, QK_NOPE + V_DIM)
    k_nope, v = kv[..., :QK_NOPE], kv[..., QK_NOPE:]
    k_rope = apply_rope(k_pe, cos, sin)
    attn = causal_block_attention(q_nope, q_rope, k_nope, k_rope, v)

    u = gate_c * x_in
    u_pad = jnp.pad(u, ((0, 0), (CONV_W - 1, 0), (0, 0)))
    y = sum(conv_w[k] * u_pad[:, k:k + plen] for k in range(CONV_W))
    conv = gate_b * y

    merged = jnp.concatenate([rms_norm(attn[:, PAD_FRONT:], attn_out_norm),
                              rms_norm(conv[:, PAD_FRONT:], conv_out_norm)], axis=-1)
    return merged @ w_out

def hier_moe(h, w_group_router, b_group_router, w_expert_router, b_expert_router,
             w_gate, w_up, w_down, w_sh_gate, w_sh_up, w_sh_down):
    bsz, slen, d = h.shape
    t = h.reshape(-1, d)
    g_prob = jax.nn.softmax((t @ w_group_router).astype(jnp.float32) + b_group_router.astype(jnp.float32), axis=-1)
    g_w, g_idx = lax.top_k(g_prob, 1)
    e_logits = ((t @ w_expert_router).astype(jnp.float32) + b_expert_router.astype(jnp.float32))
    e_logits = e_logits.reshape(-1, N_GROUPS, EXPERTS_PER_GROUP)
    e_logits = jnp.take_along_axis(e_logits, g_idx[:, :, None], axis=1)[:, 0]
    e_prob = jax.nn.softmax(e_logits, axis=-1)
    e_w, e_idx = lax.top_k(e_prob, TOP_K)
    e_w = e_w / jnp.sum(e_w, axis=-1, keepdims=True)
    weights = g_w * e_w
    eid = g_idx * EXPERTS_PER_GROUP + e_idx
    combine = jnp.einsum('nk,nke->ne', weights,
                         jax.nn.one_hot(eid, N_EXPERTS, dtype=jnp.float32)).astype(t.dtype)
    a = jnp.einsum('nd,edf->nef', t, w_gate)
    b = jnp.einsum('nd,edf->nef', t, w_up)
    hid = jax.nn.silu(a) * b * combine[:, :, None]
    routed = jnp.einsum('nef,efd->nd', hid, w_down)
    shared = (jax.nn.silu(t @ w_sh_gate) * (t @ w_sh_up)) @ w_sh_down
    return (routed + shared).reshape(bsz, slen, d)

def first_inputs(seed: int = 0) -> dict:
    key = jax.random.key(seed)
    ks = jax.random.split(key, 32)
    f32 = jnp.float32

    def nrm(k, shape, fan_in):
        return jax.random.normal(k, shape, f32) * (fan_in ** -0.5)

    def gain(k, shape):
        return 1.0 + 0.05 * jax.random.normal(k, shape, f32)

    L = DEPTH
    return {
        "x": jax.random.normal(ks[0], (BATCH, SEQ, D_MODEL), f32),
        "positions": jnp.broadcast_to(jnp.arange(SEQ, dtype=jnp.int32), (BATCH, SEQ)),
        "meta_tokens": jax.random.normal(ks[1], (N_META, D_MODEL), f32),
        "pre_mix_norm": gain(ks[2], (L, D_MODEL)),
        "w_in": nrm(ks[3], (L, D_MODEL, IN_COLS), D_MODEL),
        "q_norm": gain(ks[4], (L, Q_LORA)),
        "w_uq": nrm(ks[5], (L, Q_LORA, N_HEADS * (QK_NOPE + QK_ROPE)), Q_LORA),
        "kv_norm": gain(ks[6], (L, KV_LORA)),
        "w_ukv": nrm(ks[7], (L, KV_LORA, N_HEADS * (QK_NOPE + V_DIM)), KV_LORA),
        "conv_w": nrm(ks[8], (L, CONV_W, CONV_DIM), CONV_W),
        "attn_out_norm": gain(ks[9], (L, ATTN_WIDTH)),
        "conv_out_norm": gain(ks[10], (L, CONV_DIM)),
        "w_out": nrm(ks[11], (L, MIX_WIDTH, D_MODEL), MIX_WIDTH),
        "post_mix_norm": gain(ks[12], (L, D_MODEL)),
        "pre_ffn_norm": gain(ks[13], (L, D_MODEL)),
        "w_group_router": nrm(ks[14], (L, D_MODEL, N_GROUPS), D_MODEL),
        "b_group_router": 0.01 * jax.random.normal(ks[15], (L, N_GROUPS), f32),
        "w_expert_router": nrm(ks[16], (L, D_MODEL, N_EXPERTS), D_MODEL),
        "b_expert_router": 0.01 * jax.random.normal(ks[17], (L, N_EXPERTS), f32),
        "w_gate": nrm(ks[18], (L, N_EXPERTS, D_MODEL, D_FF), D_MODEL),
        "w_up": nrm(ks[19], (L, N_EXPERTS, D_MODEL, D_FF), D_MODEL),
        "w_down": nrm(ks[20], (L, N_EXPERTS, D_FF, D_MODEL), D_FF),
        "w_sh_gate": nrm(ks[21], (L, D_MODEL, D_FF), D_MODEL),
        "w_sh_up": nrm(ks[22], (L, D_MODEL, D_FF), D_MODEL),
        "w_sh_down": nrm(ks[23], (L, D_FF, D_MODEL), D_FF),
        "post_ffn_norm": gain(ks[24], (L, D_MODEL)),
    }

def first_block(x, positions, meta_tokens, pre_mix_norm, w_in, q_norm, w_uq, kv_norm, w_ukv, conv_w,
              attn_out_norm, conv_out_norm, w_out, post_mix_norm, pre_ffn_norm,
              w_group_router, b_group_router, w_expert_router, b_expert_router,
              w_gate, w_up, w_down, w_sh_gate, w_sh_up, w_sh_down, post_ffn_norm):
    bsz = x.shape[0]
    meta = jnp.broadcast_to(meta_tokens[None].astype(x.dtype), (bsz, N_META, D_MODEL))
    h = jnp.concatenate([meta, x], axis=1)
    rope_pos = jnp.concatenate([
        jnp.zeros((bsz, PAD_FRONT), jnp.int32),
        jnp.broadcast_to(jnp.arange(N_META, dtype=jnp.int32), (bsz, N_META)),
        positions.astype(jnp.int32) + N_META], axis=1)
    cos, sin = rope_angles(rope_pos)

    for l in range(DEPTH):
        mix = hybrid_mixer(rms_norm(h, pre_mix_norm[l]), cos, sin, w_in[l], q_norm[l], w_uq[l],
                           kv_norm[l], w_ukv[l], conv_w[l], attn_out_norm[l], conv_out_norm[l], w_out[l])
        h = h + rms_norm(mix, post_mix_norm[l])
        ffn = hier_moe(rms_norm(h, pre_ffn_norm[l]), w_group_router[l], b_group_router[l],
                       w_expert_router[l], b_expert_router[l], w_gate[l], w_up[l], w_down[l],
                       w_sh_gate[l], w_sh_up[l], w_sh_down[l])
        h = h + rms_norm(ffn, post_ffn_norm[l])

    return h[:, N_META:]


CHUNK = 64
Q_BLOCK = 128

DA_HEADS = 4
DA_HEAD_DIM = 64
DA_V_DIM = 2 * DA_HEAD_DIM
DA_WIDTH = DA_HEADS * DA_V_DIM
ALIBI_MAX = 8.0

RET_HEADS = 4
RET_QK_DIM = 64
RET_V_DIM = 128
RET_WIDTH = RET_HEADS * RET_V_DIM

MIX_WIDTH_2 = DA_WIDTH + RET_WIDTH

DA_Q_COLS = DA_HEADS * 2 * DA_HEAD_DIM
DA_K_COLS = DA_HEADS * 2 * DA_HEAD_DIM
DA_V_COLS = DA_WIDTH
RET_Q_COLS = RET_HEADS * RET_QK_DIM
RET_K_COLS = RET_HEADS * RET_QK_DIM
RET_V_COLS = RET_WIDTH
RET_G_COLS = RET_WIDTH
IN_COLS_2 = DA_Q_COLS + DA_K_COLS + DA_V_COLS + RET_Q_COLS + RET_K_COLS + RET_V_COLS + RET_G_COLS
IN_SPLITS = (DA_Q_COLS,
             DA_Q_COLS + DA_K_COLS,
             DA_Q_COLS + DA_K_COLS + DA_V_COLS,
             DA_Q_COLS + DA_K_COLS + DA_V_COLS + RET_Q_COLS,
             DA_Q_COLS + DA_K_COLS + DA_V_COLS + RET_Q_COLS + RET_K_COLS,
             DA_Q_COLS + DA_K_COLS + DA_V_COLS + RET_Q_COLS + RET_K_COLS + RET_V_COLS)

MOE_GROUPS = 4
MOE_EXPERTS_PER_GROUP = 8
MOE_EXPERTS = MOE_GROUPS * MOE_EXPERTS_PER_GROUP
MOE_TOP_K = 2
MOE_HIDDEN = 512
MOE_BLOCK = 128


def rmsnorm(x, g):
    xf = x.astype(jnp.float32)
    y = xf * lax.rsqrt(jnp.mean(xf * xf, axis=-1, keepdims=True) + EPS)
    return (y * g.astype(jnp.float32)).astype(x.dtype)

def head_rmsnorm(x):
    xf = x.astype(jnp.float32)
    return xf * lax.rsqrt(jnp.mean(xf * xf, axis=-1, keepdims=True) + EPS)

def alibi_slopes(n_heads):
    return jnp.exp2(-ALIBI_MAX * jnp.arange(1, n_heads + 1, dtype=jnp.float32) / n_heads)

def diff_attention(q, k, v, lam, subln_g, lambda_init):
    B, S = q.shape[0], q.shape[1]
    nb = S // Q_BLOCK
    scale = DA_HEAD_DIM ** -0.5
    slopes = alibi_slopes(DA_HEADS)
    k_pos = jnp.arange(S)
    k_chunk = k_pos // CHUNK
    qb = q.reshape(B, nb, Q_BLOCK, DA_HEADS, 2, DA_HEAD_DIM).transpose(1, 0, 2, 3, 4, 5)

    def one_block(args):
        i, q_blk = args
        q_pos = i * Q_BLOCK + jnp.arange(Q_BLOCK)
        s = jnp.einsum('bqhmd,bkhmd->bhmqk', q_blk, k,
                       preferred_element_type=jnp.float32) * scale
        dist = jnp.abs(q_pos[:, None] - k_pos[None, :]).astype(jnp.float32)
        bias = -slopes[:, None, None, None] * dist[None, None]
        allowed = k_chunk[None, :] <= (q_pos // CHUNK)[:, None]
        s = jnp.where(allowed, s + bias, -jnp.inf)
        p = jax.nn.softmax(s, axis=-1)
        a = p[:, :, 0] - lam * p[:, :, 1]
        return jnp.einsum('bhqk,bkhe->bqhe', a.astype(v.dtype), v)

    o = lax.map(one_block, (jnp.arange(nb), qb))
    o = o.transpose(1, 0, 2, 3, 4).reshape(B, S, DA_HEADS, DA_V_DIM)
    o = rmsnorm(o, subln_g) * (1.0 - lambda_init)
    return o.reshape(B, S, DA_WIDTH)

def retention(q, k, v, g):
    B, S = q.shape[0], q.shape[1]
    nc = S // CHUNK
    f32 = jnp.float32
    log_gamma = jnp.log1p(-jnp.exp2(-5.0 - jnp.arange(RET_HEADS, dtype=f32)))
    qc = q.astype(f32).reshape(B, nc, CHUNK, RET_HEADS, RET_QK_DIM)
    kc = (k.astype(f32) * RET_QK_DIM ** -0.5).reshape(B, nc, CHUNK, RET_HEADS, RET_QK_DIM)
    vc = v.astype(f32).reshape(B, nc, CHUNK, RET_HEADS, RET_V_DIM)
    pos = jnp.arange(CHUNK, dtype=f32)
    rel = pos[:, None] - pos[None, :]
    intra_decay = jnp.where(rel >= 0, jnp.exp(log_gamma[:, None, None] * jnp.maximum(rel, 0.0)), 0.0)
    s = jnp.einsum('bnchd,bnshd->bnhcs', qc, kc) * intra_decay
    intra = jnp.einsum('bnhcs,bnshe->bnche', s, vc)
    k_decay = jnp.exp(log_gamma[:, None] * (CHUNK - 1 - pos)[None, :])
    kv = jnp.einsum('bnshd,hs,bnshe->bnhde', kc, k_decay, vc)
    chunk_decay = jnp.exp(log_gamma * CHUNK)[:, None, None]

    def step(state, kv_n):
        return state * chunk_decay + kv_n, state

    init = jnp.zeros((B, RET_HEADS, RET_QK_DIM, RET_V_DIM), f32)
    _, prev = lax.scan(step, init, kv.transpose(1, 0, 2, 3, 4))
    prev = prev.transpose(1, 0, 2, 3, 4)
    q_decay = jnp.exp(log_gamma[:, None] * (pos + 1.0)[None, :])
    cross = jnp.einsum('bnchd,hc,bnhde->bnche', qc, q_decay, prev)
    o = head_rmsnorm((intra + cross).reshape(B, S, RET_HEADS, RET_V_DIM))
    o = jax.nn.silu(g.astype(f32)) * o
    return o.reshape(B, S, RET_WIDTH).astype(q.dtype)

def hier_moe_2(xn, wg, bg, we, be, w_gate, w_up, w_down):
    B, S, D = xn.shape
    T = B * S
    f32 = jnp.float32
    xt = xn.reshape(T, D)
    g_prob = jax.nn.softmax((xt @ wg + bg).astype(f32), axis=-1)
    g_top_p, g_top_i = lax.top_k(g_prob, 1)
    grp = g_top_i[:, 0]
    e_logits = (xt @ we + be).astype(f32).reshape(T, MOE_GROUPS, MOE_EXPERTS_PER_GROUP)
    idx = jnp.broadcast_to(grp[:, None, None], (T, 1, MOE_EXPERTS_PER_GROUP))
    e_logits = jnp.take_along_axis(e_logits, idx, axis=1)[:, 0]
    top_val, top_idx = lax.top_k(e_logits, MOE_TOP_K)
    weights = g_top_p * jax.nn.softmax(top_val, axis=-1)
    expert_id = grp[:, None] * MOE_EXPERTS_PER_GROUP + top_idx

    N = T * MOE_TOP_K
    e_flat = expert_id.reshape(N).astype(jnp.int32)
    w_flat = weights.reshape(N)
    tok_flat = jnp.repeat(jnp.arange(T, dtype=jnp.int32), MOE_TOP_K)
    order = jnp.argsort(e_flat)
    sorted_e = e_flat[order]
    counts = jnp.zeros((MOE_EXPERTS,), jnp.int32).at[e_flat].add(1)
    start = jnp.cumsum(counts) - counts
    padded = (counts + MOE_BLOCK - 1) // MOE_BLOCK * MOE_BLOCK
    pad_end = jnp.cumsum(padded)
    pad_start = pad_end - padded
    dest = pad_start[sorted_e] + jnp.arange(N, dtype=jnp.int32) - start[sorted_e]
    n_blocks = (N + MOE_BLOCK - 1) // MOE_BLOCK + MOE_EXPERTS
    nbuf = n_blocks * MOE_BLOCK
    buf_tok = jnp.full((nbuf,), T, jnp.int32).at[dest].set(tok_flat[order])
    buf_w = jnp.zeros((nbuf,), f32).at[dest].set(w_flat[order])
    block_e = jnp.minimum(jnp.searchsorted(pad_end, jnp.arange(n_blocks, dtype=jnp.int32) * MOE_BLOCK,
                                           side='right'), MOE_EXPERTS - 1)
    x_pad = jnp.concatenate([xt, jnp.zeros((1, D), xt.dtype)], axis=0)
    xb = x_pad[buf_tok].reshape(n_blocks, MOE_BLOCK, D)

    def expert_block(args):
        xblk, e = args
        h = jax.nn.silu(xblk @ w_gate[e]) * (xblk @ w_up[e])
        return h @ w_down[e]

    yb = lax.map(expert_block, (xb, block_e)).reshape(nbuf, D)
    y = jnp.zeros((T + 1, D), f32).at[buf_tok].add(yb.astype(f32) * buf_w[:, None])[:T]
    return y.reshape(B, S, D).astype(xn.dtype)

def second_inputs(seed: int = 0) -> dict:
    key = jax.random.key(seed)
    ks = jax.random.split(key, 20)
    f32 = jnp.float32
    L, D = DEPTH, D_MODEL

    def nrm(k, shape, scale):
        return jax.random.normal(k, shape, f32) * scale

    return {
        "x": nrm(ks[0], (BATCH, SEQ, D), 1.0),
        "attn_norm_g": 1.0 + nrm(ks[1], (L, D), 0.02),
        "w_in": nrm(ks[2], (L, D, IN_COLS_2), D ** -0.5),
        "da_lambda_q1": nrm(ks[3], (L, DA_HEAD_DIM), 0.1),
        "da_lambda_k1": nrm(ks[4], (L, DA_HEAD_DIM), 0.1),
        "da_lambda_q2": nrm(ks[5], (L, DA_HEAD_DIM), 0.1),
        "da_lambda_k2": nrm(ks[6], (L, DA_HEAD_DIM), 0.1),
        "da_subln_g": 1.0 + nrm(ks[7], (L, DA_V_DIM), 0.02),
        "w_out": nrm(ks[8], (L, MIX_WIDTH_2, D), MIX_WIDTH_2 ** -0.5),
        "ffn_norm_g": 1.0 + nrm(ks[9], (L, D), 0.02),
        "router_group_w": nrm(ks[10], (L, D, MOE_GROUPS), D ** -0.5),
        "router_group_b": nrm(ks[11], (L, MOE_GROUPS), 0.01),
        "router_expert_w": nrm(ks[12], (L, D, MOE_EXPERTS), D ** -0.5),
        "router_expert_b": nrm(ks[13], (L, MOE_EXPERTS), 0.01),
        "expert_w_gate": nrm(ks[14], (L, MOE_EXPERTS, D, MOE_HIDDEN), D ** -0.5),
        "expert_w_up": nrm(ks[15], (L, MOE_EXPERTS, D, MOE_HIDDEN), D ** -0.5),
        "expert_w_down": nrm(ks[16], (L, MOE_EXPERTS, MOE_HIDDEN, D), MOE_HIDDEN ** -0.5),
        "final_norm_g": 1.0 + nrm(ks[17], (D,), 0.02),
    }

def second_block(x, attn_norm_g, w_in, da_lambda_q1, da_lambda_k1, da_lambda_q2, da_lambda_k2,
              da_subln_g, w_out, ffn_norm_g, router_group_w, router_group_b, router_expert_w,
              router_expert_b, expert_w_gate, expert_w_up, expert_w_down, final_norm_g):
    B, S, _ = x.shape
    h = x
    for l in range(DEPTH):
        xn = rmsnorm(h, attn_norm_g[l])
        proj = xn @ w_in[l]
        q_da, k_da, v_da, q_r, k_r, v_r, g_r = jnp.split(proj, IN_SPLITS, axis=-1)
        lambda_init = 0.8 - 0.6 * math.exp(-0.3 * l)
        lam = (jnp.exp(jnp.sum(da_lambda_q1[l].astype(jnp.float32) * da_lambda_k1[l].astype(jnp.float32)))
               - jnp.exp(jnp.sum(da_lambda_q2[l].astype(jnp.float32) * da_lambda_k2[l].astype(jnp.float32)))
               + lambda_init)
        o_da = diff_attention(q_da.reshape(B, S, DA_HEADS, 2, DA_HEAD_DIM),
                              k_da.reshape(B, S, DA_HEADS, 2, DA_HEAD_DIM),
                              v_da.reshape(B, S, DA_HEADS, DA_V_DIM),
                              lam, da_subln_g[l], lambda_init)
        o_r = retention(q_r.reshape(B, S, RET_HEADS, RET_QK_DIM),
                        k_r.reshape(B, S, RET_HEADS, RET_QK_DIM),
                        v_r.reshape(B, S, RET_HEADS, RET_V_DIM),
                        g_r.reshape(B, S, RET_HEADS, RET_V_DIM))
        mix = jnp.concatenate([o_da.astype(h.dtype), o_r.astype(h.dtype)], axis=-1)
        h = h + mix @ w_out[l]
        xn = rmsnorm(h, ffn_norm_g[l])
        h = h + hier_moe_2(xn, router_group_w[l], router_group_b[l], router_expert_w[l],
                         router_expert_b[l], expert_w_gate[l], expert_w_up[l], expert_w_down[l])
    return rmsnorm(h, final_norm_g)


def setup_inputs(seed=0):
    out = dict(first_inputs(seed))
    for name, value in second_inputs(seed + 1).items():
        if name != "x":
            out[name + "_2"] = value
    return out


def reference(
    x, positions, meta_tokens, pre_mix_norm, w_in, q_norm, w_uq, kv_norm, w_ukv, conv_w,
    attn_out_norm, conv_out_norm, w_out, post_mix_norm, pre_ffn_norm, w_group_router,
    b_group_router, w_expert_router, b_expert_router, w_gate, w_up, w_down, w_sh_gate, w_sh_up,
    w_sh_down, post_ffn_norm, attn_norm_g_2, w_in_2, da_lambda_q1_2, da_lambda_k1_2,
    da_lambda_q2_2, da_lambda_k2_2, da_subln_g_2, w_out_2, ffn_norm_g_2, router_group_w_2,
    router_group_b_2, router_expert_w_2, router_expert_b_2, expert_w_gate_2, expert_w_up_2,
    expert_w_down_2, final_norm_g_2,
):
    x = first_block(
        x, positions, meta_tokens, pre_mix_norm, w_in, q_norm, w_uq, kv_norm, w_ukv, conv_w,
        attn_out_norm, conv_out_norm, w_out, post_mix_norm, pre_ffn_norm, w_group_router,
        b_group_router, w_expert_router, b_expert_router, w_gate, w_up, w_down, w_sh_gate,
        w_sh_up, w_sh_down, post_ffn_norm,
    )
    return second_block(
        x, attn_norm_g_2, w_in_2, da_lambda_q1_2, da_lambda_k1_2, da_lambda_q2_2,
        da_lambda_k2_2, da_subln_g_2, w_out_2, ffn_norm_g_2, router_group_w_2, router_group_b_2,
        router_expert_w_2, router_expert_b_2, expert_w_gate_2, expert_w_up_2, expert_w_down_2,
        final_norm_g_2,
    )


_drawn_inputs = setup_inputs


def setup_inputs(seed=0):
    import zlib

    import numpy as np

    out = dict(_drawn_inputs(seed))
    spreads = {}
    factors = {'b_group_router': 3.972,
     'attn_norm_g_2': 2.908,
     'da_lambda_q2_2': 7.501,
     'da_lambda_k2_2': 5.629,
     'da_subln_g_2': 7.81,
     'ffn_norm_g_2': 3.974,
     'router_group_b_2': 8.0,
     'router_expert_b_2': 8.0,
     'final_norm_g_2': 8.045,
     'da_lambda_q1_2': 8.0}
    for name, (base, spread) in spreads.items():
        noise = np.random.default_rng([zlib.crc32(name.encode()), seed]).standard_normal(out[name].shape)
        drawn = base * np.exp(spread * noise) if base else spread * noise
        out[name] = __import__('jax').numpy.asarray(drawn.astype(out[name].dtype))
    for name, factor in factors.items():
        out[name] = (out[name] * factor).astype(out[name].dtype)
    return out
```

```python
from contextlib import ExitStack

import numpy as np

import concourse.bass as bass
from concourse import mybir

ALU = mybir.AluOpType
ACT = mybir.ActivationFunctionType
F32 = mybir.dt.float32
I32 = mybir.dt.int32
F32R = mybir.dt.float32r
AX = mybir.AxisListType.X

P = 128
D = 1024
KC = D // P
TOK = 256
TT = TOK // P
META = 16
COLS = META + TOK
EPS = 1e-6
NEG = -1e30

HEADS, NOPE, ROPE, VD = 8, 64, 32, 64
QK = NOPE + ROPE
QL, KVL = 256, 128
ZC = QL + KVL + ROPE
CONV = 512
CC = CONV // P
A_SCALE = QK ** -0.5

DH = 4
DD = 64
DV = 128
LAMBDA_INIT = 0.2
LN_GAMMA = [float(np.log1p(-np.exp2(-5.0 - h))) for h in range(DH)]
SLOPES = [float(np.exp2(-8.0 * (h + 1) / DH)) for h in range(DH)]

GROUPS, PER_GROUP, EXPERTS = 4, 8, 32
CAP = 64
PAIRS = EXPERTS // 2
MAX_ROUNDS = TOK // CAP

RING = 12
CH = 2048


def stream_of_phase_one(t):
    w_in = t["w_in"][0].rearrange("(p c) n -> p c n", c=KC)
    w_out = t["w_out"][0].rearrange("(c p) n -> p c n", p=P)
    out = []

    def block(w, a, b):
        for k in range(0, KC, 4):
            out.append((w[:, k:k + 4, a:b], (4, b - a)))

    block(w_in, 0, ZC)
    block(w_in, ZC + CONV, ZC + 2 * CONV)
    out.append((t["w_uq"][0].rearrange("(p c) n -> p c n", c=2), (2, HEADS * QK)))
    out.append((t["w_ukv"][0].rearrange("p (c n) -> p c n", c=1), (1, HEADS * (NOPE + VD))))
    block(w_in, ZC + 2 * CONV, ZC + 3 * CONV)
    block(w_in, ZC, ZC + CONV)
    for c in (4, 6, 0, 2):
        out.append((w_out[:, c:c + 2, :], (2, D)))
    for name in ("w_sh_gate", "w_sh_up"):
        out.append((t[name][0].rearrange("(p c) n -> p c n", c=KC), (KC, 256)))
    out.append((t["w_sh_down"][0].rearrange("(p c) n -> p c n", c=2), (2, D)))
    return out


def stream_of_phase_two(t):
    w_in = t["w_in_2"][0].rearrange("(p c) n -> p c n", c=KC)
    w_out = t["w_out_2"][0].rearrange("(c p) n -> p c n", p=P)
    out = []
    for b in range(6):
        for k in range(0, KC, 4):
            out.append((w_in[:, k:k + 4, 512 * b:512 * b + 512], (4, 512)))
    for c in (0, 2, 4, 6):
        out.append((w_out[:, c:c + 2, :], (2, D)))
    return out


def pair_chunks(gate, up, down, ff, pair):
    out = []
    rows = CH // ff
    for w in (gate, up):
        v = w[0].rearrange("e (p c) f -> e p c f", c=KC)
        for k in range(0, KC, rows):
            for e in range(2):
                out.append((v[bass.ds(2 * pair + e, 1), :, k:k + rows, :].rearrange("e p c f -> p (e c) f"), (rows, ff)))
    fc = ff // P
    v = down[0].rearrange("e (p c) f -> e p c f", c=fc)
    for c in range(0, fc, 2):
        for e in range(2):
            out.append((v[bass.ds(2 * pair + e, 1), :, c:c + 2, :].rearrange("e p c f -> p (e c) f"), (2, D)))
    return out


def two_block_kernel(nc, t, out):
    ctx = ExitStack()
    with ctx:
        def sb(name, shape, dt=F32):
            return ctx.enter_context(nc.sbuf_tensor(name, shape, dt))

        events = {}

        SHARED = {
            "conv_sq_ready": ("square_sums", 0), "attn_sq_ready": ("square_sums", 1),
            "dist_i_ready": ("late_iota", 0), "lag_i_ready": ("late_iota", 1),
            "gcp": ("conv_block", 0), "xip": ("conv_block", 4), "gbp": ("conv_block", 8),
            "cqp": ("compressed_turned", 0), "ckvp": ("compressed_turned", 1), "krp": ("compressed_turned", 2),
            "qp": ("expanded", 0), "vp": ("expanded", 2), "kp": ("expanded", 5),
            "pcp": ("projected", 0), "pap": ("projected", 1), "out2p": ("projected", 2),
            "qdp": ("block2", 0), "kdp": ("block2", 4), "vdp": ("block2", 8), "rp": ("block2", 10),
            "vrp": ("block2", 14), "grp": ("block2", 16),
            "kr_ready": ("keys_ready", 0), "kT_ready": ("keys_ready", 1),
            "kd_ready": ("taken2", 0), "vd_ready": ("taken2", 4), "r_ready": ("taken2", 6), "vr_ready": ("taken2", 10),
            "gr_ready": ("taken2", 12),
            "sin_ready": ("sines", 0), "cos_ready": ("sines", 1),
            "pexp": ("exps", 0), "pexp2": ("exps", 16),
            "nmax": ("row_max", 0), "nmax2": ("row_max", 4),
            "cqT_ready": ("compressed_ready", 0), "ckvT_ready": ("compressed_ready", 2),
            "biased0": ("biased", 0), "biased1": ("biased", 2),
            "mixed1": ("h_ready", 0), "h_two": ("h_ready", 2), "mixed2": ("h_ready", 4), "h_four": ("h_ready", 6),
        }

        def ev(name):
            name = SHARED[name][0] if name in SHARED else name
            if name not in events:
                events[name] = ctx.enter_context(nc.semaphore(name))
            return events[name]

        def nth(name, n):
            return ev(name), (SHARED[name][1] if name in SHARED else 0) + n

        ring = sb("ring", [P, RING, CH])
        h = sb("h", [P, TT, D])
        xs = sb("xs", [P, TT, D])
        xT = sb("xT", [P, KC, COLS])
        gain_row = sb("gain_row", [P, D])
        ident = sb("ident", [P, P])
        ones = sb("ones", [P, P])
        before = sb("before", [P, P])
        gk = sb("gk", [P, 4, KC])
        gq = sb("gq", [P, 2])
        gkv = sb("gkv", [P, 1])
        rows = sb("rows", [21, P])
        cols = sb("cols", [P, 21])
        lams = sb("lams", [P, 4, DD])
        iota_i = sb("iota_i", [P, CAP], I32)
        iota = sb("iota", [P, CAP])
        slot_no = sb("slot_no", [P, CAP])
        wr = sb("wr", [P, KC, 36])
        br = sb("br", [36, 1])
        rounds_i = sb("rounds_i", [P, 2], I32)
        small = sb("small", [P, 640])
        ps = ctx.enter_context(nc.psum_tensor("ps", [P, 8, 512], F32))

        def carve(tensor):
            at = [0]

            def take(*shape, start=None):
                if start is not None:
                    at[0] = start
                n = int(np.prod(shape))
                v = tensor[:, at[0]:at[0] + n]
                at[0] += n
                assert at[0] <= tensor.shape[1], at[0]
                if len(shape) == 2:
                    v = v.rearrange("p (a b) -> p a b", b=shape[1])
                if len(shape) == 3:
                    v = v.rearrange("p (a b c) -> p a b c", b=shape[1], c=shape[2])
                return v
            return take

        tiny = carve(small)
        eps = tiny(1)
        half_pi = tiny(1)
        mean_sq = tiny(3)
        root = tiny(3)
        rstd = tiny(3)
        zss = tiny(5)
        zroot = tiny(5)
        zr = tiny(5)
        fine = tiny(2, 2)
        fine_root = tiny(4)
        fine_r = tiny(2, 2)
        freq = tiny(16)
        posf = tiny(3)
        inv512 = tiny(1)
        nmax = tiny(8)
        psum_row = tiny(8)
        prow = tiny(8)
        lam = tiny(1)
        lam_a = tiny(2)
        lam_b = tiny(2)
        rnd = tiny(4)
        r_gmax = tiny(2)
        r_gsum = tiny(2)
        r_gw = tiny(2)
        r_gi = tiny(2)
        r_m1 = tiny(2)
        r_i1 = tiny(2)
        r_m2 = tiny(2)
        r_i2 = tiny(2)
        r_dd = tiny(2)
        r_e = tiny(2)
        r_e1 = tiny(2)
        r_w1 = tiny(2)
        r_w2 = tiny(2)
        r_c = tiny(1)
        r_gd = tiny(2, 4)
        r_ge = tiny(2, 4)
        r_geq = tiny(2, 4)
        r_gt = tiny(2, 4)
        r_gm = tiny(2, 4)
        r_pen = tiny(2, 4)
        hss = tiny(2, 8)
        hroot = tiny(2, 8)
        hrs = tiny(2, 8)
        pos_i = sb("pos_i", [P, 4], I32)
        with nc.sbuf_tensor("work", [P, 17664], F32) as work:
            pass
        sb("under_parts", [P, 12288])
        parts = sb("parts", [P, 2 * D + TT * P])

        a = carve(work)
        zq = a(3, 384)
        sq = a(3, TOK, start=0)
        kr = a(3, ROPE, start=1152)
        cqT = a(2, TOK)
        ckvT = a(COLS)
        qs = a(TT, HEADS, QK)
        kT = a(HEADS, COLS)
        mix = a(TT, D)
        qT = mix.rearrange("p t (h c) -> p (t h) c", c=TOK)
        vtok = a(3, 512)
        pr = a(2, 4, COLS)
        attnT = a(CC, TOK)
        gc = a(CC, COLS)
        u = a(CC, COLS)
        conv = a(CC, TOK)
        cs = a(3, ROPE)
        sn = a(3, ROPE)
        ang = a(3, ROPE // 2)
        turns_ = a(3, ROPE // 2)
        rtmp = a(HEADS, ROPE)
        mask = a(COLS)
        pT = qs.rearrange("p t h d -> p (t h d)").rearrange("p (k h c) -> p k h c", k=3, h=4)
        meta = attnT.rearrange("p c t -> p (c t)")[0:META, :]
        metan = conv.rearrange("p c t -> p (c t)")[0:META, :]

        m = carve(work)
        xgT = m(KC, P)
        sil = m(512)
        hs = m(512)
        hT = m(4, P)
        y = m(D)
        onehot = m(TT, P)
        wonehot = m(TT, P)
        comb = m(TT, EXPERTS)
        posm = m(TT, EXPERTS)
        routed = m(TT, EXPERTS)
        mask1 = m(TT, EXPERTS)
        mask2 = m(TT, EXPERTS)
        em = m(TT, EXPERTS)
        e_t = m(TT, EXPERTS)
        lg = m(TT, 36)
        lgT = m(TOK)
        assert 1024 + 512 * 3 + 1024 + 768 + 7 * 64 + 72 + 256 <= 5632
        slot_weight = m(1)
        exact = carve(parts)
        y_high = exact(D)
        y_low = exact(D)
        scat = exact(TT, P)
        b = carve(work)
        bias = b(DH, TOK, start=5632)
        decay = b(DH, TOK)
        dist = b(TOK)
        dist_i = work[:, 5632 + 2048 + 256:5632 + 2048 + 512].bitcast(I32)
        spare = carve(work)(2, CH, start=8192)
        qdT = b(DH, TOK, start=8192)
        kdT = b(DH, TOK)
        rT = b(4, TOK)
        vda = b(TT, 512)
        vr = b(TT, 512)
        gr = b(TT, 512)
        sd1 = b(8, TOK)
        sd0 = b(8, P)
        on_da = qdT.rearrange("p h t -> p (h t)").rearrange("p (t n) -> p t n", t=TT)
        on_r = kdT.rearrange("p h t -> p (h t)").rearrange("p (t n) -> p t n", t=TT)
        b2 = carve(work)
        aT = b2(3, DH, P, start=0)
        sTm = b2(DH, 384)
        mixT = b2(KC, TOK)

        landed = [ctx.enter_context(nc.semaphore(f"landed{s}")) for s in range(RING)]
        chunk_used = ev("chunk_used")
        phase_one = stream_of_phase_one(t)
        phase_two = stream_of_phase_two(t)
        moes = [
            dict(tag="m1", gate=t["w_gate"], up=t["w_up"], down=t["w_down"], ff=256, gains=1, unroll=2),
            dict(tag="m2", gate=t["expert_w_gate_2"], up=t["expert_w_up_2"], down=t["expert_w_down_2"], ff=512,
                 gains=3, unroll=1),
        ]
        TURN = {"m1": 1, "m2": 2}
        EARLIER = {"m1": 0, "m2": PAIRS}
        n = len(phase_one)
        for cfg, after in zip(moes, (phase_two, [])):
            cfg["per"] = len(pair_chunks(cfg["gate"], cfg["up"], cfg["down"], cfg["ff"], 0))
            cfg["base"] = n
            assert cfg["per"] * cfg["unroll"] % RING == 0
            n += PAIRS * cfg["per"]
            cfg["next"] = n
            n += len(after)

        def chunk_view(slot, shape):
            return ring[:, slot, 0:shape[0] * shape[1]].rearrange("p (a b) -> p a b", b=shape[1])

        def loops(cfg):
            u_ = cfg["unroll"]
            return [(0, 2, 1), (2, u_, (PAIRS - 2 - u_) // u_), (PAIRS - u_, u_, 1)]

        def extra_rounds(eng, tag):
            extra = eng.value_load(rounds_i[0:1, TURN[tag] - 1:TURN[tag]], min_val=0, max_val=MAX_ROUNDS - 1)
            if tag == "m1":
                return extra, 0
            first = eng.value_load(rounds_i[0:1, 0:1], min_val=0, max_val=MAX_ROUNDS - 1)
            return extra, first * PAIRS

        block = ctx.enter_context(nc.Block())

        @block.sync
        def _(sp):
            def load(n0, spec, turn, per_turn, addr=None):
                src, shape = spec
                n_free = n0 - RING + 1
                if not isinstance(turn, int) or n_free + turn * per_turn > 0:
                    sp.wait_ge(chunk_used, turn * per_turn + n_free)
                sp.dma_start(chunk_view(n0 % RING, shape), src).then_inc(landed[n0 % RING], 16)

            for tt in range(TT):
                sp.dma_start(h[:, tt, :], t["x"][0, tt * P:(tt + 1) * P, :]).then_inc(ev(f"x_in{tt}"), 16)
            sp.dma_start(meta, t["meta_tokens"][:, :]).then_inc(ev("meta_in"), 16)
            for j, spec in enumerate(phase_one):
                load(j, spec, 0, 0)
            for cfg, rest in zip(moes, (phase_two, [])):
                tag = cfg["tag"]
                for p0, body, turns in loops(cfg):
                    if turns == 1:
                        for k in range(body):
                            for j, spec in enumerate(pair_chunks(cfg["gate"], cfg["up"], cfg["down"], cfg["ff"], p0 + k)):
                                load(cfg["base"] + (p0 + k) * cfg["per"] + j, spec, 0, 0)
                        continue
                    with sp.Fori(0, turns) as i:
                        for k in range(body):
                            specs = pair_chunks(cfg["gate"], cfg["up"], cfg["down"], cfg["ff"], i * body + (p0 + k))
                            for j, spec in enumerate(specs):
                                load(cfg["base"] + (p0 + k) * cfg["per"] + j, spec, i, body * cfg["per"])
                sp.wait_ge(ev("rounds"), TURN[tag])
                extra, earlier_x = extra_rounds(sp, tag)
                with sp.If(extra > 0):
                    with sp.Fori(0, extra) as r:
                        with sp.Fori(0, PAIRS) as q:
                            specs = pair_chunks(cfg["gate"], cfg["up"], cfg["down"], cfg["ff"], q)
                            for j, (src, shape) in enumerate(specs):
                                if j % 2 == 0:
                                    sp.wait_ge(ev(f"{tag}_x_used"), (r * PAIRS + q) * cfg["per"] + j)
                                dst = spare[:, j % 2, 0:shape[0] * shape[1]].rearrange("p (a b) -> p a b", b=shape[1])
                                sp.dma_start(dst, src).then_inc(ev(f"{tag}_x_landed{j % 2}"), 16)
                for j, spec in enumerate(rest):
                    load(cfg["next"] + j, spec, 0, 0)
            for tt in range(TT):
                sp.wait_ge(ev("result"), tt + 1)
                sp.dma_start(out[0, tt * P:(tt + 1) * P, :], xs[:, tt, :]).then_inc(ev("stored"), 16)
            sp.wait_ge(ev("stored"), 16 * TT)

        @block.gpsimd
        def _(pool):
            def keep_where(v, op, fill, base, pattern, mult):
                return pool.affine_select(out=v, in_=v, compare_op=op, fill=fill, base=base, pattern=pattern,
                                          channel_multiplier=mult)

            pool.memset(ident[:, :], 0.0).then_inc(ev("g0"), 1)
            pool.memset(ones[:, :], 1.0).then_inc(ev("tables_ready"), 1)
            pool.memset(before[:, :], 1.0).then_inc(ev("g0"), 1)
            pool.memset(mask, 0.0).then_inc(ev("g0"), 1)
            pool.wait_ge(ev("g0"), 3)
            keep_where(ident[:, :], ALU.not_equal, 1.0, 0, [[-1, P]], 1).then_inc(ev("tables_ready"), 1)
            keep_where(before[:, :], ALU.is_ge, 0.0, -1, [[1, P]], -1).then_inc(ev("tables_ready"), 1)
            keep_where(mask, ALU.is_ge, NEG, META + P, [[-1, COLS]], 1).then_inc(ev("tables_ready"), 1)
            pool.iota(iota_i[:, :], pattern=[[1, CAP]], base=0, channel_multiplier=0).then_inc(ev("tables_ready"), 1)
            pool.iota(pos_i[:, 3:4], pattern=[[1, 1]], base=0, channel_multiplier=1).then_inc(ev("tables_ready"), 1)
            for j in range(ROPE // 2):
                f = np.float32(1.0) / np.float32(10000.0) ** np.float32(2.0 * j / ROPE)
                pool.memset(freq[:, j:j + 1], float(f)).then_inc(ev("tables_ready"), 1)

            def squares_sum(src, dst, waits, tag, done):
                n = 0 if tag == "conv" else 2 * CC - 2
                for c in range(CC):
                    pool.wait_ge(*waits[c])
                    pool.tensor_tensor(sq[:, 2, :] if c else dst, src[:, c, :], src[:, c, :], ALU.mult)\
                        .then_inc(ev("sq_step"), 1)
                    n += 1
                    pool.wait_ge(ev("sq_step"), n)
                    if c:
                        add = pool.tensor_tensor(dst, dst, sq[:, 2, :], ALU.add)
                        if c == CC - 1:
                            add.then_inc(ev(done), 1)
                            pool.wait_ge(*nth(done, 1))
                        else:
                            add.then_inc(ev("sq_step"), 1)
                            n += 1
                            pool.wait_ge(ev("sq_step"), n)

            squares_sum(conv, sq[:, 0, :], [(ev("conv_ready"), c + 1) for c in range(CC)], "conv", "conv_sq_ready")
            squares_sum(attnT, sq[:, 1, :], [(ev("attnT_raw"), TT)] * CC, "attn", "attn_sq_ready")

            pool.wait_ge(*nth("mixed1", TT))
            pool.iota(dist_i, pattern=[[-1, TOK]], base=P, channel_multiplier=1).then_inc(ev("dist_i_ready"), 1)
            pool.wait_ge(ev("dist_ready"), 1)
            pool.iota(dist_i, pattern=[[1, TOK]], base=0, channel_multiplier=-1).then_inc(ev("lag_i_ready"), 1)
            pool.wait_ge(ev("decay_raw"), DH)
            keep_where(decay, ALU.is_ge, 0.0, 0, [[0, DH], [1, TOK]], -1).then_inc(ev("decay_ready"), 1)

        def products_done(cfg, n, j, sfx=""):
            if sfx:
                return ev(f"{cfg['tag']}_x_used"), n * cfg["per"] + j
            return chunk_used, n * cfg["per"] + (cfg["base"] + j)

        def moe_scalar(act, cfg):
            tag, ff, per = cfg["tag"], cfg["ff"], cfg["per"]
            gates = KC * ff // CH * 2

            def pair(n, m, sfx=""):
                act.wait_ge(*products_done(cfg, m, gates, sfx))
                act.activation(sil[:, 0:ff], ps[:, 4, 0:ff], ACT.Silu).then_inc(ev(f"sil{sfx}"), 1)
                act.wait_ge(ev(f"hTp{sfx}"), n + 1)
                act.activation(hT[:, 0:ff // P, :], ps[:, 6, 0:ff].rearrange("p (c s) -> p c s", s=P), ACT.Copy)\
                    .then_inc(ev(f"hT{sfx}"), 1)
                act.wait_ge(*products_done(cfg, m, per, sfx))
                act.activation(y[:, 512:1024], ps[:, 7, :], ACT.Copy, scale=slot_weight).then_inc(ev(f"y1{sfx}"), 1)

            for p0, body, turns in loops(cfg):
                first = EARLIER[tag] + p0
                if turns == 1:
                    for k in range(body):
                        pair(first + k, p0 + k)
                else:
                    with act.Fori(0, turns) as i:
                        for k in range(body):
                            pair(i * body + (first + k), i * body + (p0 + k))
            act.wait_ge(ev("rounds"), TURN[tag])
            extra, earlier_x = extra_rounds(act, tag)
            with act.If(extra > 0):
                with act.Fori(0, extra) as r:
                    with act.Fori(0, PAIRS) as q:
                        pair(earlier_x + (r * PAIRS + q), r * PAIRS + q, "_x")
            act.wait_ge(ev("experts_summed"), earlier_x + extra * PAIRS + TURN[tag])

        def moe_vector(dve, cfg):
            tag, ff, per = cfg["tag"], cfg["ff"], cfg["per"]
            ups = KC * ff // CH * 4

            def expert_cols(v, pair):
                return v[:, :, bass.ds(2 * pair, 2)].unsqueeze(3).broadcast_to([P, TT, 2, CAP])

            def slots():
                return slot_no[:, :].unsqueeze(1).unsqueeze(1).broadcast_to([P, TT, 2, CAP])

            def four(v):
                return v.rearrange("p t (e s) -> p t e s", e=2)

            def build_onehot(pair, n, sfx=""):
                if not isinstance(n, int) or n > 0:
                    dve.wait_ge(ev(f"xgp{sfx}"), n * 2)
                dve.tensor_tensor(four(onehot), expert_cols(posm, pair), slots(), ALU.is_equal)\
                    .then_inc(ev(f"onehot{sfx}"), 1)

            def build_weighted(pair, n, sfx=""):
                if not isinstance(n, int) or n > 0:
                    dve.wait_ge(ev(f"scatp{sfx}"), n)
                dve.tensor_tensor(four(wonehot), expert_cols(posm, pair), slots(), ALU.is_equal)\
                    .then_inc(ev(f"wraw{sfx}"), 1)
                dve.wait_ge(ev(f"wraw{sfx}"), n + 1)
                dve.tensor_tensor(four(wonehot), four(wonehot), expert_cols(comb, pair), ALU.mult)\
                    .then_inc(ev(f"wonehot{sfx}"), 1)

            def take_gathered(n, sfx=""):
                for half in range(2):
                    dve.wait_ge(ev(f"xgp{sfx}"), n * 2 + (half + 1))
                    gain = gk[:, cfg["gains"], 4 * half:4 * half + 4].unsqueeze(2).broadcast_to([P, 4, P])
                    dve.tensor_tensor(xgT[:, 4 * half:4 * half + 4, :],
                                      ps[:, 6 + half, :].rearrange("p (c s) -> p c s", s=P),
                                      gain, ALU.mult).then_inc(ev(f"xg{sfx}"), 1)

            def hidden(n, m, sfx=""):
                dve.wait_ge(ev(f"sil{sfx}"), n + 1)
                dve.wait_ge(*products_done(cfg, m, ups, sfx))
                dve.tensor_tensor(hs[:, 0:ff], sil[:, 0:ff], ps[:, 5, 0:ff], ALU.mult).then_inc(ev(f"h{sfx}"), 1)

            def take_scatter(n, sfx=""):
                dve.wait_ge(ev(f"scatp{sfx}"), n + 1)
                dve.tensor_reduce(slot_weight, ps[:, 7, 0:256], AX, ALU.max).then_inc(ev(f"scat{sfx}"), 1)
                dve.tensor_scalar(scat.bitcast(F32R), ps[:, 7, 0:256].rearrange("p (t s) -> p t s", s=P), 0.0, None, ALU.is_gt)\
                    .then_inc(ev(f"scat{sfx}"), 1)

            def take_y(n, sfx=""):
                dve.wait_ge(ev(f"y0p{sfx}"), n + 1)
                dve.wait_ge(ev(f"scat{sfx}"), n * 2 + 2)
                dve.tensor_scalar(y[:, 0:512], ps[:, 6, :], slot_weight, None, ALU.mult).then_inc(ev(f"y0{sfx}"), 1)
                for half in range(2):
                    v, high, low = (u_[:, 512 * half:512 * half + 512] for u_ in (y, y_high, y_low))
                    dve.wait_ge(ev(f"y{half}{sfx}"), n + 1)
                    dve.tensor_copy(high.bitcast(F32R), v).then_inc(ev(f"y_parts{sfx}"), 1)
                    dve.wait_ge(ev(f"y_parts{sfx}"), n * 4 + (2 * half + 1))
                    dve.tensor_tensor(low.bitcast(F32R), v, high, ALU.subtract).then_inc(ev(f"y_parts{sfx}"), 1)

            def pair(p, last):
                n = p + EARLIER[tag]
                build_weighted(p, n)
                if not last:
                    build_onehot(p + 1, n + 1)
                hidden(n, p)
                if not last:
                    take_gathered(n + 1)
                take_scatter(n)
                take_y(n)

            build_onehot(0, EARLIER[tag])
            take_gathered(EARLIER[tag])
            for p0, body, turns in loops(cfg):
                if turns == 1:
                    for k in range(body):
                        pair(p0 + k, p0 + k == PAIRS - 1)
                else:
                    with dve.Fori(0, turns) as i:
                        for k in range(body):
                            pair(i * body + (p0 + k), False)
            dve.wait_ge(ev("experts_summed"), TURN[tag])
            extra, earlier_x = extra_rounds(dve, tag)
            with dve.If(extra > 0):
                with dve.Fori(0, extra) as r:
                    dve.tensor_scalar(slot_no[:, :], slot_no[:, :], float(CAP), None, ALU.add)\
                        .then_inc(ev(f"{tag}_slots"), 1)
                    with dve.Fori(0, PAIRS) as q:
                        dve.wait_ge(ev(f"{tag}_slots"), r + 1)
                        n = earlier_x + (r * PAIRS + q)
                        build_onehot(q, n, "_x")
                        build_weighted(q, n, "_x")
                        take_gathered(n, "_x")
                        hidden(n, r * PAIRS + q, "_x")
                        take_scatter(n, "_x")
                        take_y(n, "_x")
            dve.wait_ge(ev("experts_summed"), earlier_x + extra * PAIRS + TURN[tag])

        def moe_tensor(pe, cfg):
            tag, ff, per = cfg["tag"], cfg["ff"], cfg["per"]
            fc = ff // P
            rows_ = CH // ff

            def gather(n, sfx="", free=None):
                pe.wait_ge(ev(f"onehot{sfx}"), n + 1)
                if free is not None:
                    pe.wait_ge(ev("y0"), free + 1)
                    pe.wait_ge(ev("y1"), free + 1)
                for half in range(2):
                    for c in range(4):
                        for tt in range(TT):
                            mm = pe.matmul(ps[:, 6 + half, c * P:(c + 1) * P], xs[:, tt, 4 * half + c::KC],
                                           onehot[:, tt, :], start=(tt == 0), stop=(tt == TT - 1))
                    mm.then_inc(ev(f"xgp{sfx}"), 1)

            def gates_and_ups(get, used, n, sfx=""):
                pe.wait_ge(ev(f"xg{sfx}"), n * 2 + 2)
                j = 0
                for which in range(2):
                    for k0 in range(0, KC, rows_):
                        chunks = get(j, (rows_, ff))
                        for k in range(rows_):
                            for e in range(2):
                                mm = pe.matmul(ps[CAP * e:CAP * e + CAP, 4 + which, 0:ff],
                                               xgT[:, k0 + k, CAP * e:CAP * e + CAP], chunks[e][:, k, :],
                                               start=(k0 + k == 0), stop=(k0 + k == KC - 1), skip_group_check=True)
                                if k == rows_ - 1:
                                    mm.then_inc(used, 1)
                        j += 2
                return j

            def turn_hidden(n, sfx=""):
                pe.wait_ge(ev(f"h{sfx}"), n + 1)
                for c in range(fc):
                    tr = pe.transpose(ps[:, 6, c * P:(c + 1) * P], hs[:, c:ff:fc], ident[:, :])
                tr.then_inc(ev(f"hTp{sfx}"), 1)

            def turn_weights(n, sfx=""):
                pe.wait_ge(ev(f"wonehot{sfx}"), n + 1)
                for tt in range(TT):
                    tr = pe.transpose(ps[:, 7, tt * P:(tt + 1) * P], wonehot[:, tt, :], ident[:, :])
                tr.then_inc(ev(f"scatp{sfx}"), 1)

            def down(get, used, j, n, sfx=""):
                pe.wait_ge(ev(f"hT{sfx}"), n + 1)
                for c0 in range(0, fc, 2):
                    chunks = get(j, (2, D))
                    for half in range(2):
                        if half == 1 and c0 == 0:
                            pe.wait_ge(ev(f"scat{sfx}"), n * 2 + 2)
                        for k in range(2):
                            for e in range(2):
                                mm = pe.matmul(ps[CAP * e:CAP * e + CAP, 6 + half, :],
                                               hT[:, c0 + k, CAP * e:CAP * e + CAP],
                                               chunks[e][:, k, 512 * half:512 * half + 512],
                                               start=(c0 + k == 0), stop=(c0 + k == fc - 1), skip_group_check=True)
                                if half == 1 and k == 1:
                                    mm.then_inc(used, 1)
                        if half == 0 and c0 + 2 == fc:
                            mm.then_inc(ev(f"y0p{sfx}"), 1)
                    j += 2

            def scatter(n, half, first, last, sfx=""):
                pe.wait_ge(ev(f"y_parts{sfx}"), n * 4 + (2 * half + 2))
                for part, v in enumerate((y_high, y_low)):
                    for tt in range(TT):
                        mm = pe.matmul(ps[:, 2 * tt + half, :], scat[:, tt, :].bitcast(F32R),
                                       v[:, 512 * half:512 * half + 512].bitcast(F32R),
                                       start=first and part == 0, stop=last and part == 1, skip_group_check=True)
                return mm

            def pair(p, p_first, turn, first, last):
                n0 = cfg["base"] + p_first * per

                def get(j, shape):
                    views = []
                    for e in range(2):
                        slot, lap = (n0 + j + e) % RING, (n0 + j + e) // RING
                        pe.wait_ge(landed[slot], turn * (16 * (cfg["unroll"] * per // RING)) + 16 * (lap + 1))
                        views.append(chunk_view(slot, shape))
                    return views

                n = p + EARLIER[tag]
                j = gates_and_ups(get, chunk_used, n)
                opens = tag == "m2" and isinstance(p, int) and p == 1
                if not last:
                    gather(n + 1, free=None if first else n - 1)
                if not first:
                    scatter(n - 1, 0, opens, False)
                if not last:
                    pe.wait_ge(ev("xg"), n * 2 + 4)
                turn_hidden(n)
                if not first:
                    scatter(n - 1, 1, opens, False)
                turn_weights(n)
                down(get, chunk_used, j, n)

            gather(EARLIER[tag])
            for p0, body, turns in loops(cfg):
                if turns == 1:
                    for k in range(body):
                        pair(p0 + k, p0 + k, 0, p0 + k == 0, p0 + k == PAIRS - 1)
                else:
                    with pe.Fori(0, turns) as i:
                        for k in range(body):
                            pair(i * body + (p0 + k), p0 + k, i, False, False)
            for half in range(2):
                mm = scatter(EARLIER[tag] + PAIRS - 1, half, False, True)
            mm.then_inc(ev("experts_summed"), 1)

            pe.wait_ge(ev("rounds"), TURN[tag])
            extra, earlier_x = extra_rounds(pe, tag)
            with pe.If(extra > 0):
                with pe.Fori(0, extra) as r:
                    with pe.Fori(0, PAIRS) as q:
                        n = earlier_x + (r * PAIRS + q)

                        def get(j, shape):
                            for e in range(2):
                                pe.wait_ge(ev(f"{tag}_x_landed{e}"), ((r * PAIRS + q) * (per // 2) + (j // 2 + 1)) * 16)
                            return [spare[:, e, 0:shape[0] * shape[1]].rearrange("p (a b) -> p a b", b=shape[1])
                                    for e in range(2)]

                        used = ev(f"{tag}_x_used")
                        gather(n, "_x")
                        j = gates_and_ups(get, used, n, "_x")
                        turn_hidden(n, "_x")
                        turn_weights(n, "_x")
                        down(get, used, j, n, "_x")
                        for half in range(2):
                            mm = scatter(n, half, False, True, "_x")
                        mm.then_inc(ev("experts_summed"), 1)

        def route(dve, tag, chain):
            A = lg[:, :, 0:GROUPS]
            E = lg[:, :, GROUPS:36]

            def over(v, n):
                return v.unsqueeze(2).broadcast_to([P, TT, n])

            def first_of(values, top, hit, ids, lowest, mask_out, n):
                chain(dve.tensor_tensor(hit, values, over(top, n), ALU.is_ge))
                chain(dve.scalar_tensor_tensor(hit, hit, -64.0, ids, ALU.mult, ALU.add))
                chain(dve.tensor_reduce(lowest, hit, AX, ALU.min))
                chain(dve.tensor_tensor(mask_out, hit, over(lowest, n), ALU.is_equal))

            ids4 = iota[:, 0:GROUPS].unsqueeze(1).broadcast_to([P, TT, GROUPS])
            ids32 = iota[:, 0:EXPERTS].unsqueeze(1).broadcast_to([P, TT, EXPERTS])
            dve.wait_ge(ev("router_pe"), 3 * TURN[tag] - 1)
            chain(dve.tensor_copy(lg, ps[:, 7, 0:72].rearrange("p (t e) -> p t e", t=TT)))
            chain(dve.tensor_reduce(r_gmax, A, AX, ALU.max))
            dve.tensor_tensor(r_gd, A, over(r_gmax, GROUPS), ALU.subtract).then_inc(ev("router_diff"), 1)
            first_of(A, r_gmax, r_geq, ids4, r_gi, r_gm, GROUPS)
            chain(dve.tensor_scalar(r_pen, r_gm, 1.0, 1e30, ALU.subtract, ALU.mult))

            def grouped(v):
                return v.rearrange("p t (g e) -> p t g e", g=GROUPS)

            def per_group(v):
                return v.unsqueeze(3).broadcast_to([P, TT, GROUPS, PER_GROUP])

            chain(dve.tensor_tensor(grouped(em), grouped(E), per_group(r_gm), ALU.mult))
            chain(dve.tensor_tensor(grouped(em), grouped(em), per_group(r_pen), ALU.add))
            chain(dve.tensor_reduce(r_m1, em, AX, ALU.max))
            first_of(em, r_m1, e_t, ids32, r_i1, mask1, EXPERTS)
            chain(dve.scalar_tensor_tensor(em, mask1, -2e30, em, ALU.mult, ALU.add))
            chain(dve.tensor_reduce(r_m2, em, AX, ALU.max))
            dve.tensor_tensor(r_dd, r_m2, r_m1, ALU.subtract).then_inc(ev("router_diff"), 1)
            first_of(em, r_m2, e_t, ids32, r_i2, mask2, EXPERTS)
            dve.tensor_tensor(routed, mask1, mask2, ALU.add).then_inc(ev("routed"), 1)
            dve.wait_ge(ev("router_exp"), 2 * TURN[tag] - 1)
            chain(dve.tensor_reduce(r_gsum, r_ge, AX, ALU.add))
            chain(dve.reciprocal(r_gw, r_gsum))
            dve.wait_ge(ev("router_exp"), 2 * TURN[tag])
            chain(dve.tensor_scalar(r_e1, r_e, 1.0, None, ALU.add))
            chain(dve.reciprocal(r_w1, r_e1))
            chain(dve.tensor_tensor(r_w1, r_w1, r_gw, ALU.mult))
            chain(dve.tensor_tensor(r_w2, r_w1, r_e, ALU.mult))
            chain(dve.tensor_tensor(comb, mask1, over(r_w1, EXPERTS), ALU.mult))
            chain(dve.tensor_tensor(e_t, mask2, over(r_w2, EXPERTS), ALU.mult))
            chain(dve.tensor_tensor(comb, comb, e_t, ALU.add))

        def place(dve, tag, chain):
            dve.wait_ge(ev("router_pe"), 3 * TURN[tag])
            pos = ps[:, 7, 128:192].rearrange("p (t e) -> p t e", t=TT)
            chain(dve.scalar_tensor_tensor(posm, pos, 1.0, routed, ALU.add, ALU.mult))
            chain(dve.tensor_scalar(posm, posm, -1.0, None, ALU.add))
            chain(dve.tensor_reduce(r_c, ps[:, 7, 192:224], AX, ALU.max))
            for k in range(1, MAX_ROUNDS):
                chain(dve.tensor_scalar(rnd[:, k - 1:k], r_c, float(CAP * k), None, ALU.is_gt))
            chain(dve.tensor_reduce(rnd[:, 3:4], rnd[:, 0:3], AX, ALU.add))
            chain(dve.tensor_copy(slot_no[:, :], iota[:, :]))
            dve.tensor_copy(rounds_i[:, TURN[tag] - 1:TURN[tag]], rnd[:, 3:4]).then_inc(ev("rounds"), 1)
            dve.wait_ge(ev("rounds"), TURN[tag])

        def route_scalar(act, tag):
            act.wait_ge(ev("router_pe"), 3 * TURN[tag] - 2)
            act.activation(lgT[0:36, :], ps[0:36, 6, 0:TOK], ACT.Identity, bias=br[:, :]).then_inc(ev("lgT"), 1)
            act.wait_ge(ev("router_diff"), 2 * TURN[tag] - 1)
            act.activation(r_ge, r_gd, ACT.Exp).then_inc(ev("router_exp"), 1)
            act.wait_ge(ev("router_diff"), 2 * TURN[tag])
            act.activation(r_e, r_dd, ACT.Exp).then_inc(ev("router_exp"), 1)

        def logits(pe, tag):
            pe.wait_ge(ev("wr"), 32 * TURN[tag])
            for k in range(KC):
                mm = pe.matmul(ps[0:36, 6, 0:TOK], wr[:, k, :], xT[:, k, META:COLS], start=(k == 0), stop=(k == KC - 1))
            mm.then_inc(ev("router_pe"), 1)

        def turn_logits(pe, tag):
            pe.wait_ge(ev("lgT"), TURN[tag])
            for tt in range(TT):
                tr = pe.transpose(ps[:, 7, 36 * tt:36 * tt + 36], lgT[0:36, tt * P:(tt + 1) * P], ident[0:36, 0:36])
            tr.then_inc(ev("router_pe"), 1)

        def positions_of(pe, tag):
            pe.wait_ge(ev("routed"), TURN[tag])
            r0, r1 = routed[:, 0, :], routed[:, 1, :]
            pe.matmul(ps[:, 7, 128:160], before[:, :], r0, start=True, stop=True)
            pe.matmul(ps[:, 7, 160:192], before[:, :], r1, start=True, stop=False)
            pe.matmul(ps[:, 7, 160:192], ones[:, :], r0, start=False, stop=True)
            pe.matmul(ps[:, 7, 192:224], ones[:, :], r0, start=True, stop=False)
            pe.matmul(ps[:, 7, 192:224], ones[:, :], r1, start=False, stop=True).then_inc(ev("router_pe"), 1)

        STAGES_ROWS = {"n0": 0, "o1": 3, "n1": 5, "o2": 7, "n2": 9, "n3": 11, "o4": 13}
        STAGES_XS = {"n0": 0, "n1": 3, "n2": 5, "n3": 7}
        STAGES_TURNED = {"n0": 0, "n1": KC, "n2": 2 * KC, "n3": 3 * KC}

        def mean_square(act, tag, tt, src, junk, wait, parts=P):
            act.wait_ge(*wait)
            act.activation(junk, src, ACT.Square, scale=D ** -0.5, accum_out=mean_sq[0:parts, tt:tt + 1])\
                .then_inc(ev("mean_sq"), 1)
            act.wait_ge(ev("mean_sq"), STAGES_ROWS[tag] + tt + 1)
            act.activation(root[0:parts, tt:tt + 1], mean_sq[0:parts, tt:tt + 1], ACT.Sqrt, bias=eps[0:parts, :])\
                .then_inc(ev("root"), 1)

        def one_over(dve, tag, tt, chain, parts=P):
            dve.wait_ge(ev("root"), STAGES_ROWS[tag] + tt + 1)
            chain(dve.reciprocal(rstd[0:parts, tt:tt + 1], root[0:parts, tt:tt + 1]))

        def turn_tokens(pe, tag, with_meta):
            for tt in range(TT):
                pe.wait_ge(ev("xs_ready"), STAGES_XS[tag] + tt + 1)
                for k in range(KC):
                    tr = pe.transpose(ps[:, k, META + tt * P:META + (tt + 1) * P], xs[:, tt, k::KC], ident[:, :])
                    if tt == TT - 1 and not with_meta:
                        tr.then_inc(ev("turned"), 1)
            if with_meta:
                pe.wait_ge(ev("xs_ready"), STAGES_XS[tag] + TT + 1)
                for k in range(KC):
                    pe.transpose(ps[:, k, 0:META], metan[:, k::KC], ident[0:META, 0:META])\
                        .then_inc(ev("turned"), 1)

        def take_turned(eng, tag, g, with_meta, parity):
            lo = 0 if with_meta else META
            for k in range(parity, KC, 2):
                eng.wait_ge(ev("turned"), STAGES_TURNED[tag] + k + 1)
                if parity:
                    eng.activation(xT[:, k, lo:COLS], ps[:, k, lo:COLS], ACT.Copy, scale=gk[:, g, k:k + 1])\
                        .then_inc(ev("xT_odd"), 1)
                else:
                    eng.tensor_scalar(xT[:, k, lo:COLS], ps[:, k, lo:COLS], gk[:, g, k:k + 1], None, ALU.mult)\
                        .then_inc(ev("xT_even"), 1)

        def turned(pe, tag):
            pe.wait_ge(ev("xT_odd"), (STAGES_TURNED[tag] + KC) // 2)
            pe.wait_ge(ev("xT_even"), (STAGES_TURNED[tag] + KC) // 2)

        TWO_PI_HI = 6.28125
        TWO_PI_MID = 0.0019350051879882812
        TWO_PI_LO = 3.01991598e-07
        ROUNDER = 12582912.0
        SC_KEYS = [META + P, COLS]
        conv_banks = [1, 6, 7, 0]

        @block.scalar
        def _(act):
            for tt in range(TT):
                act.dma_start(pos_i[:, tt:tt + 1], t["positions"][0, tt * P:(tt + 1) * P].rearrange("(p o) -> p o", o=1))\
                    .then_inc(ev("pos_in"), 16)
            for j, name in enumerate(("pre_mix_norm", "pre_ffn_norm", "attn_norm_g_2", "ffn_norm_g_2")):
                act.dma_start(gk[:, j, :], t[name][0].rearrange("(p c) -> p c", c=KC)).then_inc(ev("params_in"), 16)
            act.dma_start(gq[:, :], t["q_norm"][0].rearrange("(p c) -> p c", c=2)).then_inc(ev("params_in"), 16)
            act.dma_start(gkv[:, :], t["kv_norm"][0].rearrange("(p c) -> p c", c=1)).then_inc(ev("params_in"), 16)
            act.dma_start(rows[0:12, :], t["conv_w"][0].rearrange("w (c p) -> (w c) p", p=P)).then_inc(ev("params_in"), 16)
            act.dma_start(rows[12:16, :], t["attn_out_norm"][0].rearrange("(c p) -> c p", p=P)).then_inc(ev("params_in"), 16)
            act.dma_start(rows[16:20, :], t["conv_out_norm"][0].rearrange("(c p) -> c p", p=P)).then_inc(ev("params_in"), 16)
            act.dma_start(rows[20:21, :], t["da_subln_g_2"]).then_inc(ev("params_in"), 16)
            act.dma_start(gain_row[:, :], t["post_mix_norm"].broadcast_to([P, D])).then_inc(ev("gain_row"), 16)
            for j, name in enumerate(("da_lambda_q1_2", "da_lambda_q2_2", "da_lambda_k1_2", "da_lambda_k2_2")):
                act.dma_start(lams[:, j, :], t[name].broadcast_to([P, DD])).then_inc(ev("lams_in"), 16)

            def load_router(tag, wg, bg, we, be):
                act.dma_start(wr[:, :, 0:GROUPS], t[wg][0].rearrange("(p c) e -> p c e", c=KC)).then_inc(ev("wr"), 16)
                act.dma_start(wr[:, :, GROUPS:36], t[we][0].rearrange("(p c) e -> p c e", c=KC)).then_inc(ev("wr"), 16)
                act.dma_start(br[0:GROUPS, :], t[bg][0].rearrange("(e o) -> e o", o=1)).then_inc(ev("br"), 16)
                act.dma_start(br[GROUPS:36, :], t[be][0].rearrange("(e o) -> e o", o=1)).then_inc(ev("br"), 16)

            load_router("m1", "w_group_router", "b_group_router", "w_expert_router", "b_expert_router")

            act.wait_ge(ev("ang_ready"), 2)
            act.activation(sn[:, :, ROPE // 2:ROPE], ang, ACT.Sin).then_inc(ev("sin_ready"), 1)
            act.activation(cs[:, :, 0:ROPE // 2], turns_, ACT.Sin, bias=half_pi, scale=-1.0).then_inc(ev("cos_ready"), 1)

            act.wait_ge(ev("consts"), 1)
            for tt in range(TT):
                mean_square(act, "n0", tt, h[:, tt, :], xs[:, tt, :], (ev(f"x_in{tt}"), 16))
            mean_square(act, "n0", 2, meta, metan, (ev("meta_in"), 16), META)
            act.wait_ge(ev("params_in"), 160)
            take_turned(act, "n0", 0, True, 1)

            for tt in range(TT):
                act.wait_ge(ev("zp"), tt + 1)
                junk = qs.rearrange("p t h d -> p (t h d)")
                act.activation(junk[:, tt * QL:(tt + 1) * QL], ps[:, tt, 0:QL], ACT.Square, scale=QL ** -0.5,
                               accum_out=zss[:, 2 * tt:2 * tt + 1]).then_inc(ev("zss"), 1)
                act.activation(junk[:, (4 + tt) * KVL:(5 + tt) * KVL], ps[:, tt, QL:QL + KVL], ACT.Square, scale=KVL ** -0.5,
                               accum_out=zss[:, 2 * tt + 1:2 * tt + 2]).then_inc(ev("zss"), 1)
            act.wait_ge(ev("zp"), 3)
            act.activation(junk[0:META, 6 * KVL:7 * KVL], ps[0:META, 2, 0:KVL], ACT.Square, scale=KVL ** -0.5,
                           accum_out=zss[0:META, 4:5]).then_inc(ev("zss"), 1)
            act.wait_ge(ev("zss"), 5)
            act.activation(zroot, zss, ACT.Sqrt, bias=eps).then_inc(ev("zroot"), 1)

            for c in range(CC):
                act.wait_ge(*nth("gcp", c + 1))
                act.activation(gc[:, c, :], ps[:, 3 + c, 0:COLS], ACT.Copy).then_inc(ev("gc_ready"), 1)
            act.wait_ge(*nth("krp", 1))
            act.activation(kT[NOPE:QK, :, :], ps[0:ROPE, 1, 0:COLS].unsqueeze(1).broadcast_to([ROPE, HEADS, COLS]),
                           ACT.Copy).then_inc(ev("kr_ready"), 1)
            for hh in range(HEADS):
                act.wait_ge(*nth("kp", hh + 1))
                act.activation(kT[0:NOPE, hh, :], ps[0:NOPE, conv_banks[hh % 4], 0:COLS], ACT.Copy)\
                    .then_inc(ev("kT_ready"), 1)
            for j, bank in enumerate((5, 2, 3, 4)):
                act.wait_ge(ev("qTp"), j + 1)
                tt, h0 = j // 2, 4 * (j % 2)
                act.activation(qT[0:QK, h0:h0 + 4, tt * P:(tt + 1) * P],
                               ps[0:QK, bank, :].rearrange("p (h c) -> p h c", h=4), ACT.Copy)\
                    .then_inc(ev("qT_ready"), 1)
            act.wait_ge(ev("cols_ready"), 1)
            for c in range(CC):
                act.wait_ge(ev("conv_ready"), c + 1)
                act.activation(u[:, c, 0:TOK], conv[:, c, :], ACT.Copy, scale=cols[:, 16 + c:17 + c])\
                    .then_inc(ev("convG_ready"), 1)

            def exps(g):
                act.wait_ge(*nth("nmax", g + 1))
                b_ = g % 2
                for j in range(4):
                    row = pr[:, b_, j, 0:SC_KEYS[g // 2]]
                    act.activation(row, row, ACT.Exp, bias=nmax[:, 4 * b_ + j:4 * b_ + j + 1],
                                   accum_out=prow[:, 4 * b_ + j:4 * b_ + j + 1]).then_inc(ev("pexp"), 1)

            def take_second_block(g):
                if g >= 2:
                    act.wait_ge(ev("pTp"), g + 1)
                    act.activation(pT[:, 1, :, :], ps[:, 7, :].rearrange("p (h c) -> p h c", h=4), ACT.Copy)\
                        .then_inc(ev("pT7"), 1)

            exps(0)
            for g in range(4):
                if g < 3:
                    exps(g + 1)
                take_second_block(g)
            act.wait_ge(ev("attnT_raw"), 2)
            for c in range(CC):
                act.activation(gc[:, c, 0:TOK], attnT[:, c, :], ACT.Copy, scale=cols[:, 12 + c:13 + c])\
                    .then_inc(ev("attnG_ready"), 1)
            act.wait_ge(ev("fine_ms"), 1)
            act.activation(fine_root, ps[:, 1, 0:4], ACT.Sqrt, bias=eps).then_inc(ev("fine_root"), 1)
            act.wait_ge(ev("fine_r"), 1)
            act.wait_ge(*nth("pap", 1))
            for tt in range(TT):
                for half in range(2):
                    act.activation(mix[:, tt, 512 * half:512 * half + 512], ps[:, [6, 7, 0, 1][2 * tt + half], :],
                                   ACT.Copy, scale=fine_r[:, 1, tt:tt + 1]).then_inc(ev("mixa"), 1)
            for tt in range(TT):
                mean_square(act, "o1", tt, mix[:, tt, :], xs[:, tt, :], (ev("mixc"), 2 * tt + 2))
            for tt in range(TT):
                mean_square(act, "n1", tt, h[:, tt, :], xs[:, tt, :], nth("mixed1", tt + 1))
            act.wait_ge(*nth("mixed1", TT))
            act.dma_start(gain_row[:, :], t["post_ffn_norm"].broadcast_to([P, D])).then_inc(ev("gain_row"), 16)
            take_turned(act, "n1", 1, False, 1)
            act.wait_ge(ev("br"), 32)
            route_scalar(act, "m1")
            for tt in range(TT):
                act.wait_ge(chunk_used, 16)
                act.activation(sil[:, 256 * tt:256 * tt + 256], ps[:, 4 + tt, 0:256], ACT.Silu).then_inc(ev("sh_sil"), 1)
            act.wait_ge(ev("sh_hTp"), 1)
            act.activation(hT, ps[:, 6, :].rearrange("p (c s) -> p c s", s=P), ACT.Copy).then_inc(ev("sh_hT"), 1)
            act.wait_ge(ev("lag_ready"), 1)
            for hh in range(DH):
                act.activation(decay[:, hh, :], dist, ACT.Exp, scale=LN_GAMMA[hh]).then_inc(ev("decay_raw"), 1)
            act.wait_ge(ev("lam_a"), 1)
            act.activation(lam_b, lam_a, ACT.Exp).then_inc(ev("lam_b"), 1)
            act.wait_ge(ev("router_pe"), 1)
            load_router("m2", "router_group_w_2", "router_group_b_2", "router_expert_w_2", "router_expert_b_2")
            moe_scalar(act, moes[0])

            for tt in range(TT):
                mean_square(act, "o2", tt, ps[:, 2 * tt:2 * tt + 2, :], xs[:, tt, :].rearrange("p (a b) -> p a b", a=2),
                            (ev("experts_summed"), 1))
            for tt in range(TT):
                mean_square(act, "n2", tt, h[:, tt, :], xs[:, tt, :], nth("h_two", tt + 1))
            act.wait_ge(*nth("h_two", TT))
            act.dma_start(gain_row[:, :], t["final_norm_g_2"].rearrange("(a n) -> a n", a=1).broadcast_to([P, D]))\
                .then_inc(ev("gain_row"), 16)
            take_turned(act, "n2", 2, False, 1)
            for c in range(DH):
                act.wait_ge(*nth("kdp", c + 1))
                act.activation(kdT[:, c, :], ps[:, 4 + c, 0:TOK], ACT.Copy).then_inc(ev("kd_ready"), 1)
            for tt in range(TT):
                act.wait_ge(*nth("vdp", tt + 1))
                act.activation(vda[:, tt, :], ps[:, tt, :], ACT.Copy).then_inc(ev("vd_ready"), 1)

            def exps2(tile, src, n0):
                act.wait_ge(*nth("nmax2", tile + 1))
                for j in range(8):
                    act.activation(src[:, j, :], src[:, j, :], ACT.Exp, bias=nmax[:, j:j + 1],
                                   accum_out=prow[:, j:j + 1]).then_inc(ev("pexp2"), 1)

            exps2(0, sd0, 0)
            for c in range(4):
                act.wait_ge(*nth("rp", c + 1))
                act.activation(rT[:, c, :], ps[:, c, 0:TOK], ACT.Copy).then_inc(ev("r_ready"), 1)
            exps2(1, sd1, 8)
            for tt in range(TT):
                act.wait_ge(*nth("vrp", tt + 1))
                act.activation(vr[:, tt, :], ps[:, 4 + tt, :], ACT.Copy).then_inc(ev("vr_ready"), 1)
            for tt in range(TT):
                act.wait_ge(*nth("grp", tt + 1))
                act.activation(gr[:, tt, :], ps[:, 6 + tt, :], ACT.Silu).then_inc(ev("gr_ready"), 1)
            for j in range(3):
                act.wait_ge(ev("aTp"), j + 1)
                act.activation(aT[:, j, :, :], ps[:, j, :].rearrange("p (h c) -> p h c", h=DH), ACT.Copy)\
                    .then_inc(ev("aT_ready"), 1)
            n = 0
            for tt in range(TT):
                for kind, bank in ((0, 3 + tt), (1, 1 + tt)):
                    act.wait_ge(ev("odp" if kind == 0 else "orp"), tt + 1)
                    for hh in range(DH):
                        act.activation(sd1.rearrange("p a b -> p (a b)")[:, n * DV:(n + 1) * DV], ps[:, bank, hh * DV:(hh + 1) * DV], ACT.Square, scale=DV ** -0.5,
                                       accum_out=hss[:, tt, 4 * kind + hh:4 * kind + hh + 1]).then_inc(ev("hss"), 1)
                        n += 1
                    act.wait_ge(ev("hss"), n)
                    act.activation(hroot[:, tt, 4 * kind:4 * kind + 4], hss[:, tt, 4 * kind:4 * kind + 4], ACT.Sqrt,
                                   bias=eps).then_inc(ev("hroot"), 1)
            for j, (tt, kind) in enumerate(((0, 0), (0, 1), (1, 0), (1, 1))):
                act.wait_ge(ev("mTp"), j + 1)
                dst = mixT[:, 4 * kind:4 * kind + 4, tt * P:(tt + 1) * P]
                src = ps[:, 5 + j if j < 3 else 0, :].rearrange("p (h c) -> p h c", h=DH)
                if kind == 0:
                    act.activation(dst, src, ACT.Copy, scale=cols[:, 20:21]).then_inc(ev("mT_ready"), 1)
                else:
                    act.activation(dst, src, ACT.Copy).then_inc(ev("mT_ready"), 1)
            for tt in range(TT):
                mean_square(act, "n3", tt, h[:, tt, :], xs[:, tt, :], nth("mixed2", tt + 1))
            take_turned(act, "n3", 3, False, 1)
            act.wait_ge(ev("br"), 64)
            route_scalar(act, "m2")
            moe_scalar(act, moes[1])
            for tt in range(TT):
                mean_square(act, "o4", tt, h[:, tt, :], xs[:, tt, :], nth("h_four", tt + 1))

        @block.vector
        def _(dve):
            count = [0]

            def chain(ins):
                count[0] += 1
                ins.then_inc(ev("vector_chain"), 1)
                dve.wait_ge(ev("vector_chain"), count[0])

            chain(dve.memset(eps, EPS))
            chain(dve.memset(half_pi, float(np.pi / 2)))
            chain(dve.memset(zss, 1.0))
            chain(dve.memset(inv512, 1.0 / 512.0))
            dve.memset(mean_sq, 1.0).then_inc(ev("consts"), 1)

            dve.wait_ge(ev("pos_in"), 32)
            chain(dve.tensor_copy(posf[:, 0:2], pos_i[:, 0:2]))
            chain(dve.tensor_scalar(posf[:, 0:2], posf[:, 0:2], float(META), None, ALU.add))
            dve.wait_ge(ev("tables_ready"), 6 + ROPE // 2)
            chain(dve.tensor_copy(posf[:, 2:3], pos_i[:, 3:4]))
            dve.wait_ge(ev("tables_ready"), 6 + ROPE // 2)
            half = ROPE // 2
            chain(dve.tensor_tensor(ang, posf.unsqueeze(2).broadcast_to([P, 3, half]),
                                    freq.unsqueeze(1).broadcast_to([P, 3, half]), ALU.mult))
            chain(dve.tensor_scalar(turns_, ang, float(1 / (2 * np.pi)), None, ALU.mult))
            chain(dve.tensor_scalar(turns_, turns_, ROUNDER, None, ALU.add))
            chain(dve.tensor_scalar(turns_, turns_, ROUNDER, None, ALU.subtract))
            for part in (TWO_PI_HI, TWO_PI_MID, TWO_PI_LO):
                chain(dve.scalar_tensor_tensor(ang, turns_, -part, ang, ALU.mult, ALU.add))
            chain(dve.tensor_scalar(ang, ang, 3.1415925, -3.1415925, ALU.min, ALU.max))
            chain(dve.tensor_scalar(turns_, ang, -1.0, None, ALU.mult))
            dve.tensor_tensor(turns_, turns_, ang, ALU.max).then_inc(ev("ang_ready"), 2)
            dve.wait_ge(*nth("sin_ready", 1))
            chain(dve.tensor_scalar(sn[:, :, 0:half], sn[:, :, half:ROPE], -1.0, None, ALU.mult))
            dve.wait_ge(*nth("cos_ready", 1))
            chain(dve.tensor_copy(cs[:, :, half:ROPE], cs[:, :, 0:half]))
            dve.wait_ge(ev("tables_ready"), 6 + ROPE // 2)
            chain(dve.tensor_copy(iota[:, :], iota_i[:, :]))

            for tt in range(TT):
                one_over(dve, "n0", tt, chain)
                dve.tensor_scalar(xs[:, tt, :], h[:, tt, :], rstd[:, tt:tt + 1], None, ALU.mult).then_inc(ev("xs_ready"), 1)
            one_over(dve, "n0", 2, chain, META)
            dve.tensor_scalar(metan, meta, rstd[0:META, 2:3], None, ALU.mult).then_inc(ev("xs_ready"), 1)
            dve.wait_ge(ev("colsp"), 1)
            dve.tensor_copy(cols[:, :], ps[:, 7, 480:501]).then_inc(ev("cols_ready"), 1)
            dve.wait_ge(ev("cols_ready"), 1)
            chain(dve.tensor_scalar(cols[:, 20:21], cols[:, 20:21], 1.0 - LAMBDA_INIT, None, ALU.mult))
            dve.wait_ge(ev("params_in"), 160)
            take_turned(dve, "n0", 0, True, 0)

            dve.wait_ge(ev("zroot"), 1)
            chain(dve.reciprocal(zr, zroot))
            for tt in range(TT):
                dve.tensor_scalar(zq[:, tt, 0:QL], ps[:, tt, 0:QL], zr[:, 2 * tt:2 * tt + 1], None, ALU.mult)\
                    .then_inc(ev("zq_ready"), 1)
                dve.tensor_scalar(zq[:, tt, QL:QL + KVL], ps[:, tt, QL:QL + KVL], zr[:, 2 * tt + 1:2 * tt + 2], None,
                                  ALU.mult).then_inc(ev("zq_ready"), 1)
            dve.tensor_scalar(zq[0:META, 2, QL:QL + KVL], ps[0:META, 2, 0:KVL], zr[0:META, 4:5], None, ALU.mult)\
                .then_inc(ev("zq_ready"), 1)

            def rotate(dst, src, parts, tile, done):
                n_ = src.shape[1]
                tmp = rtmp[0:parts, 0:n_, :]

                def angles(v):
                    return v[0:parts, tile, :].unsqueeze(1).broadcast_to([parts, n_, v.shape[2]])
                chain(dve.tensor_tensor(dst, src, angles(cs), ALU.mult))
                chain(dve.tensor_tensor(tmp[:, :, 0:half], src[:, :, half:ROPE], angles(sn[:, :, 0:half]), ALU.mult))
                chain(dve.tensor_tensor(tmp[:, :, half:ROPE], src[:, :, 0:half], angles(sn[:, :, half:ROPE]), ALU.mult))
                dve.tensor_tensor(dst, dst, tmp, ALU.add).then_inc(done, 1)

            for tile in range(3):
                parts, bank, at = (P, tile, QL + KVL) if tile < TT else (META, 2, KVL)
                rotate(kr[0:parts, tile:tile + 1, :], ps[0:parts, bank, at:at + ROPE].unsqueeze(1), parts, tile,
                       ev("kr_turned"))
                dve.wait_ge(ev("kr_turned"), tile + 1)
            dve.wait_ge(ev("params_in"), 160)
            dve.wait_ge(*nth("cqp", 1))
            for c in range(2):
                dve.tensor_scalar(cqT[:, c, :], ps[:, 7, c * TOK:(c + 1) * TOK], gq[:, c:c + 1], None, ALU.mult)\
                    .then_inc(ev("cqT_ready"), 1)
            dve.wait_ge(*nth("ckvp", 1))
            dve.tensor_scalar(ckvT, ps[:, 0, 0:COLS], gkv[:, 0:1], None, ALU.mult).then_inc(ev("ckvT_ready"), 1)
            for tt in range(TT):
                dve.wait_ge(*nth("qp", tt + 1))
                src = ps[:, 2 + 2 * tt:4 + 2 * tt, :].rearrange("p a b -> p (a b)")[:, 0:HEADS * QK]\
                    .rearrange("p (h d) -> p h d", h=HEADS)
                dve.tensor_copy(qs[:, tt, :, 0:NOPE], src[:, :, 0:NOPE]).then_inc(ev("qs_ready"), 1)
                rotate(qs[:, tt, :, NOPE:QK], src[:, :, NOPE:QK], P, tt, ev("qs_ready"))
                dve.wait_ge(ev("qs_ready"), 2 * tt + 2)
            for kb in range(3):
                parts = P if kb < 2 else META
                dve.wait_ge(*nth("vp", kb + 1))
                dve.tensor_copy(vtok[0:parts, kb, :], ps[0:parts, [6, 7, 0][kb], :]).then_inc(ev("v_ready"), 1)
            for c in range(CC):
                dve.wait_ge(*nth("xip", c + 1))
                dve.wait_ge(ev("gc_ready"), c + 1)
                dve.tensor_tensor(u[:, c, :], ps[:, conv_banks[c], 0:COLS], gc[:, c, :], ALU.mult).then_inc(ev("u_ready"), 1)
                dve.wait_ge(ev("u_ready"), c + 1)
                chain(dve.tensor_scalar(conv[:, c, :], u[:, c, META - 2:COLS - 2], cols[:, c:c + 1], None, ALU.mult))
                for w in (1, 2):
                    chain(dve.scalar_tensor_tensor(conv[:, c, :], u[:, c, META - 2 + w:COLS - 2 + w],
                                                   cols[:, 4 * w + c:4 * w + c + 1], conv[:, c, :], ALU.mult, ALU.add))
            for c in range(CC):
                dve.wait_ge(*nth("gbp", c + 1))
                dve.tensor_tensor(conv[:, c, :], ps[:, conv_banks[c], META:COLS], conv[:, c, :], ALU.mult)\
                    .then_inc(ev("conv_ready"), 1)

            dve.wait_ge(ev("tables_ready"), 6 + ROPE // 2)

            def mask_and_max(g):
                b_, keys = g % 2, SC_KEYS[g // 2]
                dve.wait_ge(ev("scp"), g + 1)
                if g >= 2:
                    dve.wait_ge(ev("pTp"), g - 1)
                m_ = mask[:, COLS - keys:COLS].unsqueeze(1).broadcast_to([P, 4, keys])
                dve.scalar_tensor_tensor(pr[:, b_, :, 0:keys], ps[:, 2:6, 0:keys], A_SCALE, m_, ALU.mult, ALU.add)\
                    .then_inc(ev("masked"), 1)
                dve.wait_ge(ev("masked"), g + 1)
                dve.tensor_reduce(nmax[:, 4 * b_:4 * b_ + 4], pr[:, b_, :, 0:keys], AX, ALU.max, negate=True)\
                    .then_inc(ev("nmax"), 1)

            mask_and_max(0)
            for g in range(4):
                tt = g // 2
                b_, keys = g % 2, SC_KEYS[tt]
                if g < 3:
                    mask_and_max(g + 1)
                dve.wait_ge(*nth("pexp", 4 * g + 4))
                sums = prow[:, 4 * b_:4 * b_ + 4]
                chain(dve.reciprocal(sums, sums))
                dve.tensor_tensor(pr[:, b_, :, 0:keys], pr[:, b_, :, 0:keys],
                                  sums.unsqueeze(2).broadcast_to([P, 4, keys]), ALU.mult).then_inc(ev("p_ready"), 1)
                dve.wait_ge(ev("pTp"), g + 1)
                dve.tensor_copy(pT[:, 0, :, :], ps[:, 6, :].rearrange("p (h c) -> p h c", h=4)).then_inc(ev("pT_ready"), 1)
                dve.tensor_copy(pT[0:META, 1 + tt, :, :] if tt == 0 else pT[0:META, 2, :, :],
                                ps[0:META, 0, :].rearrange("p (h c) -> p h c", h=4)).then_inc(ev("pT_ready"), 1)
                if g % 2:
                    dve.wait_ge(ev("atp"), tt + 1)
                    dve.tensor_copy(attnT[:, :, tt * P:(tt + 1) * P], ps[:, 1, :].rearrange("p (c t) -> p c t", c=4))\
                        .then_inc(ev("attnT_raw"), 1)
            dve.wait_ge(ev("fine_root"), 1)
            dve.reciprocal(fine_r.rearrange("p a b -> p (a b)"), fine_root).then_inc(ev("fine_r"), 1)
            dve.wait_ge(ev("fine_r"), 1)
            dve.wait_ge(*nth("pcp", 1))
            for j in range(4):
                tt, hf = j // 2, j % 2
                dve.wait_ge(ev("mixa"), j + 1)
                part = mix[:, tt, 512 * hf:512 * hf + 512]
                dve.scalar_tensor_tensor(part, ps[:, 2 + j, :], fine_r[:, 0, tt:tt + 1], part, ALU.mult, ALU.add)\
                    .then_inc(ev("mixc"), 1)
            dve.wait_ge(ev("gain_row"), 16)
            for tt in range(TT):
                one_over(dve, "o1", tt, chain)
                chain(dve.scalar_tensor_tensor(mix[:, tt, :], mix[:, tt, :], rstd[:, tt:tt + 1], gain_row[:, :],
                                               ALU.mult, ALU.mult))
                dve.tensor_tensor(h[:, tt, :], h[:, tt, :], mix[:, tt, :], ALU.add).then_inc(ev("mixed1"), 1)
            for tt in range(TT):
                one_over(dve, "n1", tt, chain)
                dve.tensor_scalar(xs[:, tt, :], h[:, tt, :], rstd[:, tt:tt + 1], None, ALU.mult).then_inc(ev("xs_ready"), 1)
            take_turned(dve, "n1", 1, False, 0)
            route(dve, "m1", chain)
            for tt in range(TT):
                dve.wait_ge(ev("sh_sil"), tt + 1)
                dve.wait_ge(chunk_used, 16)
                dve.tensor_tensor(hs[:, 256 * tt:256 * tt + 256], sil[:, 256 * tt:256 * tt + 256],
                                  ps[:, 4 + tt, 256:512], ALU.mult).then_inc(ev("sh_h"), 1)
            place(dve, "m1", chain)
            dve.wait_ge(*nth("dist_i_ready", 1))
            chain(dve.tensor_copy(dist, dist_i))
            chain(dve.tensor_scalar(decay[:, 0, 0:P], dist[:, 0:P], 1.0, None, ALU.mult))
            chain(dve.tensor_copy(decay[:, 0, P:TOK], dist[:, P:TOK]))
            chain(dve.scalar_tensor_tensor(dist[:, P:TOK], decay[:, 0, P:TOK], -1.0, decay[:, 0, P:TOK], ALU.mult, ALU.max))
            chain(dve.memset(dist[0:64, P + 64:TOK], 1e33))
            for hh in range(DH):
                chain(dve.tensor_scalar(bias[:, hh, :], dist, -SLOPES[hh], None, ALU.mult))
            dve.tensor_copy(rnd[:, 0:1], rnd[:, 1:2]).then_inc(ev("dist_ready"), 1)
            dve.wait_ge(*nth("lag_i_ready", 1))
            dve.tensor_copy(dist, dist_i).then_inc(ev("lag_ready"), 1)
            dve.wait_ge(ev("lams_in"), 64)
            chain(dve.tensor_tensor(lams[:, 0:2, :], lams[:, 0:2, :], lams[:, 2:4, :], ALU.mult))
            dve.tensor_reduce(lam_a, lams[:, 0:2, :], AX, ALU.add).then_inc(ev("lam_a"), 1)
            dve.wait_ge(ev("lam_b"), 1)
            chain(dve.scalar_tensor_tensor(lam, lam_b[:, 0:1], LAMBDA_INIT, lam_b[:, 1:2], ALU.add, ALU.subtract))
            moe_vector(dve, moes[0])

            dve.wait_ge(ev("gain_row"), 32)
            for tt in range(TT):
                one_over(dve, "o2", tt, chain)
                chain(dve.scalar_tensor_tensor(xs[:, tt, :].rearrange("p (a b) -> p a b", a=2), ps[:, 2 * tt:2 * tt + 2, :],
                                               rstd[:, tt:tt + 1], gain_row[:, :].rearrange("p (a b) -> p a b", a=2),
                                               ALU.mult, ALU.mult))
                dve.tensor_tensor(h[:, tt, :], h[:, tt, :], xs[:, tt, :], ALU.add).then_inc(ev("h_two"), 1)
            for tt in range(TT):
                one_over(dve, "n2", tt, chain)
                dve.tensor_scalar(xs[:, tt, :], h[:, tt, :], rstd[:, tt:tt + 1], None, ALU.mult).then_inc(ev("xs_ready"), 1)
            take_turned(dve, "n2", 2, False, 0)
            for c in range(DH):
                dve.wait_ge(*nth("qdp", c + 1))
                dve.tensor_copy(qdT[:, c, :], ps[:, c, 0:TOK]).then_inc(ev("qd_ready"), 1)
            dve.wait_ge(ev("sc2p"), 1)
            for mp in range(2):
                dve.scalar_tensor_tensor(sd0[:, 4 * mp:4 * mp + 4, :], ps[:, 2 + mp, :].rearrange("p (h k) -> p h k", h=DH),
                                         DD ** -0.5, bias[:, :, P:TOK], ALU.mult, ALU.add).then_inc(ev("biased0"), 1)
            dve.wait_ge(*nth("biased0", 2))
            dve.tensor_reduce(nmax, sd0, AX, ALU.max, negate=True).then_inc(ev("nmax2"), 1)
            dve.wait_ge(ev("sc2p"), 2)
            for mp in range(2):
                dve.scalar_tensor_tensor(sd1[:, 4 * mp:4 * mp + 4, :],
                                         ps[:, 4 + 2 * mp:6 + 2 * mp, :].rearrange("p a (h k) -> p (a h) k", h=2),
                                         DD ** -0.5, bias, ALU.mult, ALU.add).then_inc(ev("biased1"), 1)
            dve.wait_ge(*nth("biased1", 2))

            def combine(sd, tile, keys):
                dve.wait_ge(*nth("pexp2", 8 * tile + 8))
                chain(dve.reciprocal(prow, prow))
                chain(dve.tensor_scalar(prow[:, 4:8], prow[:, 4:8], lam, None, ALU.mult))
                chain(dve.tensor_tensor(sd, sd, prow.unsqueeze(2).broadcast_to([P, 8, keys]), ALU.mult))
                dve.tensor_tensor(sd[:, 0:4, :], sd[:, 0:4, :], sd[:, 4:8, :], ALU.subtract).then_inc(ev("a_ready"), 1)
                dve.wait_ge(ev("a_ready"), tile + 1)

            combine(sd0, 0, P)
            dve.tensor_reduce(nmax, sd1, AX, ALU.max, negate=True).then_inc(ev("nmax2"), 1)
            combine(sd1, 1, TOK)
            dve.wait_ge(ev("decay_ready"), 1)
            for hh in range(DH):
                dve.wait_ge(ev("rsp"), hh + 1)
                bank = [5, 6, 7, 0][hh]
                dve.scalar_tensor_tensor(sTm[:, hh, 0:TOK], ps[:, bank, 0:TOK], DD ** -0.5, decay[:, hh, :],
                                         ALU.mult, ALU.mult).then_inc(ev("rs_ready"), 1)
                dve.scalar_tensor_tensor(sTm[:, hh, TOK:384], ps[:, bank, TOK:384], DD ** -0.5, decay[:, hh, 0:P],
                                         ALU.mult, ALU.mult).then_inc(ev("rs_ready"), 1)
            n = 0
            for tt in range(TT):
                for kind, bank in ((0, 3 + tt), (1, 1 + tt)):
                    n += 1
                    dve.wait_ge(ev("hroot"), n)
                    r_ = hrs[:, tt, 4 * kind:4 * kind + 4]
                    chain(dve.reciprocal(r_, hroot[:, tt, 4 * kind:4 * kind + 4]))
                    dst = (on_da, on_r)[kind][:, tt, :]
                    hd = dst.rearrange("p (h e) -> p h e", h=DH)
                    last = dve.tensor_tensor(hd, ps[:, bank, :].rearrange("p (h e) -> p h e", h=DH),
                                             r_.unsqueeze(2).broadcast_to([P, DH, DV]), ALU.mult)
                    if kind:
                        chain(last)
                        dve.wait_ge(*nth("gr_ready", tt + 1))
                        last = dve.tensor_tensor(dst, dst, gr[:, tt, :], ALU.mult)
                    last.then_inc(ev("on_ready"), 1)
            dve.wait_ge(*nth("out2p", 1))
            for tt in range(TT):
                hv = h[:, tt, :].rearrange("p (a b) -> p a b", a=2)
                dve.tensor_tensor(hv, ps[:, 1 + 2 * tt:3 + 2 * tt, :], hv, ALU.add).then_inc(ev("mixed2"), 1)
            for tt in range(TT):
                one_over(dve, "n3", tt, chain)
                dve.tensor_scalar(xs[:, tt, :], h[:, tt, :], rstd[:, tt:tt + 1], None, ALU.mult).then_inc(ev("xs_ready"), 1)
            take_turned(dve, "n3", 3, False, 0)
            route(dve, "m2", chain)
            place(dve, "m2", chain)
            moe_vector(dve, moes[1])
            for tt in range(TT):
                hv = h[:, tt, :].rearrange("p (a b) -> p a b", a=2)
                dve.tensor_tensor(hv, ps[:, 2 * tt:2 * tt + 2, :], hv, ALU.add).then_inc(ev("h_four"), 1)
            dve.wait_ge(ev("gain_row"), 48)
            for tt in range(TT):
                one_over(dve, "o4", tt, chain)
                dve.scalar_tensor_tensor(xs[:, tt, :], h[:, tt, :], rstd[:, tt:tt + 1], gain_row[:, :],
                                         ALU.mult, ALU.mult).then_inc(ev("result"), 1)

        @block.tensor
        def _(pe):
            def chunk(n, spec):
                pe.wait_ge(landed[n % RING], 16 * (n // RING + 1))
                return chunk_view(n % RING, spec[1])

            pe.wait_ge(ev("tables_ready"), 6 + ROPE // 2)
            pe.wait_ge(ev("params_in"), 160)
            pe.transpose(ps[:, 7, 480:501], rows[:, :], ident[0:21, 0:21]).then_inc(ev("colsp"), 1)
            pe.wait_ge(ev("cols_ready"), 1)
            turn_tokens(pe, "n0", True)
            turned(pe, "n0")

            for j in range(2):
                w = chunk(j, phase_one[j])
                for tile in range(3):
                    parts, lo, c0 = (P, META + tile * P, 0) if tile < TT else (META, 0, QL)
                    for k in range(4):
                        mm = pe.matmul(ps[0:parts, tile, 0:ZC - c0], xT[:, 4 * j + k, lo:lo + parts], w[:, k, c0:ZC],
                                       start=(j == 0 and k == 0), stop=(j == 1 and k == 3))
                    if j == 1 and tile < TT:
                        mm.then_inc(ev("zp"), 1)
                mm.then_inc(chunk_used, 1)

            def by_feature(n, banks, cols_, done, before_bank=None, rhs_lo=0):
                ws = [chunk(n, ((), (4, 512))), chunk(n + 1, ((), (4, 512)))]
                for c in range(4):
                    if before_bank:
                        pe.wait_ge(*before_bank(c))
                    for k in range(KC):
                        mm = pe.matmul(ps[:, banks[c], 0:cols_], ws[k // 4][:, k % 4, c * P:(c + 1) * P],
                                       xT[:, k, COLS - cols_:COLS], start=(k == 0), stop=(k == KC - 1))
                        if c == 3 and k == 3:
                            mm.then_inc(chunk_used, 1)
                    if c == 3:
                        mm.then_inc(chunk_used, 1)
                        pe.wait_ge(chunk_used, n + 2)
                        pe.nop().then_inc(done, 1)
                    else:
                        mm.then_inc(done, 1)

            pe.wait_ge(chunk_used, 2)
            pe.nop().then_inc(ev("zp"), 1)
            by_feature(2, [3, 4, 5, 6], COLS, ev("gcp"))
            pe.wait_ge(ev("zq_ready"), 5)
            for c in range(2):
                for tt in range(TT):
                    tr = pe.transpose(ps[:, 7, c * TOK + tt * P:c * TOK + (tt + 1) * P], zq[:, tt, c:QL:2], ident[:, :])
            tr.then_inc(ev("cqp"), 1)
            pe.wait_ge(ev("kr_turned"), 3)
            for tt in range(TT):
                pe.transpose(ps[:, 0, META + tt * P:META + (tt + 1) * P], zq[:, tt, QL:QL + KVL], ident[:, :])
            pe.transpose(ps[:, 0, 0:META], zq[0:META, 2, QL:QL + KVL], ident[0:META, 0:META]).then_inc(ev("ckvp"), 1)
            for tt in range(TT):
                pe.transpose(ps[0:ROPE, 1, META + tt * P:META + (tt + 1) * P], kr[:, tt, :], ident[:, :])
            pe.transpose(ps[0:ROPE, 1, 0:META], kr[0:META, 2, :], ident[0:META, 0:META]).then_inc(ev("krp"), 1)
            w = chunk(4, phase_one[4])
            pe.wait_ge(*nth("cqT_ready", 2))
            pe.wait_ge(ev("gc_ready"), 3)
            for tt in range(TT):
                for lo, hi in ((0, 512), (512, 768)):
                    for k in range(2):
                        mm = pe.matmul(ps[:, 2 + 2 * tt + lo // 512, 0:hi - lo], cqT[:, k, tt * P:(tt + 1) * P],
                                       w[:, k, lo:hi], start=(k == 0), stop=(k == 1))
                if tt == 0:
                    mm.then_inc(ev("qp"), 1)
            mm.then_inc(chunk_used, 1)
            pe.wait_ge(chunk_used, 5)
            pe.nop().then_inc(ev("qp"), 1)
            w = chunk(5, phase_one[5])[:, 0, :].rearrange("p (h d) -> p h d", h=HEADS)
            pe.wait_ge(*nth("ckvT_ready", 1))
            pe.wait_ge(ev("gc_ready"), 4)
            for kb in range(3):
                parts = P if kb < 2 else META
                pe.matmul(ps[0:parts, [6, 7, 0][kb], :], ckvT[:, kb * P:kb * P + parts], w[:, :, NOPE:NOPE + VD],
                          start=True, stop=True).then_inc(ev("vp"), 1)
            for hh in range(HEADS):
                if hh == 0:
                    pe.wait_ge(*nth("kr_ready", 1))
                elif hh < 4:
                    pe.wait_ge(ev("v_ready"), hh)
                else:
                    pe.wait_ge(*nth("kT_ready", hh - 3))
                mm = pe.matmul(ps[0:NOPE, conv_banks[hh % 4], 0:COLS], w[:, hh, 0:NOPE], ckvT, start=True, stop=True)
                if hh < HEADS - 1:
                    mm.then_inc(ev("kp"), 1)
            mm.then_inc(chunk_used, 1)
            pe.wait_ge(chunk_used, 6)
            pe.nop().then_inc(ev("kp"), 1)
            by_feature(6, conv_banks, COLS, ev("xip"), lambda c: nth("kT_ready", 5 + c))
            for j, bank in enumerate((5, 2, 3, 4)):
                tt, h0 = j // 2, 4 * (j % 2)
                if j == 0:
                    pe.wait_ge(ev("qs_ready"), 4)
                for hh in range(4):
                    tr = pe.transpose(ps[0:QK, bank, hh * P:(hh + 1) * P], qs[:, tt, h0 + hh, :], ident[:, :])
                tr.then_inc(ev("qTp"), 1)
            by_feature(8, conv_banks, COLS, ev("gbp"), lambda c: (ev("u_ready"), c + 1))

            def scores(g):
                tt, h0 = g // 2, 4 * (g % 2)
                keys = SC_KEYS[tt]
                if g == 0:
                    pe.wait_ge(ev("qT_ready"), 4)
                else:
                    pe.wait_ge(ev("masked"), g)
                for hh in range(4):
                    mm = pe.matmul(ps[:, 2 + hh, 0:keys], qT[0:QK, h0 + hh, tt * P:(tt + 1) * P],
                                   kT[0:QK, h0 + hh, 0:keys], start=True, stop=True)
                mm.then_inc(ev("scp"), 1)

            def weigh_values(g):
                tt, h0 = g // 2, 4 * (g % 2)
                blocks = [(0, P, 6, 0), (P, META, 0, 1)] if tt == 0 else [(0, P, 6, 0), (P, P, 7, 1), (2 * P, META, 0, 2)]
                pe.wait_ge(ev("p_ready"), g + 1)
                if g == 0:
                    pe.wait_ge(ev("conv_ready"), 4)
                else:
                    pe.wait_ge(ev("pT_ready"), 2 * g)
                    if g == 3:
                        pe.wait_ge(ev("pT7"), 1)
                for lo, n_, bank, _ in blocks:
                    for hh in range(4):
                        tr = pe.transpose(ps[0:n_, bank, hh * P:(hh + 1) * P], pr[:, g % 2, hh, lo:lo + n_], ident[:, :])
                tr.then_inc(ev("pTp"), 1)
                pe.wait_ge(ev("pT_ready"), 2 * g + 2)
                if tt:
                    pe.wait_ge(ev("pT7"), g - 1)
                if g == 2:
                    pe.wait_ge(ev("attnT_raw"), 1)
                for hh in range(4):
                    head = h0 + hh
                    half = NOPE * (head % 2)
                    for b_, (lo, n_, bank, at) in enumerate(blocks):
                        mm = pe.matmul(ps[half:half + VD, 1, (head // 2) * P:(head // 2 + 1) * P],
                                       vtok[0:n_, lo // P, head * VD:(head + 1) * VD], pT[0:n_, at, hh, :],
                                       start=(b_ == 0), stop=(b_ == len(blocks) - 1), skip_group_check=True)
                if g % 2:
                    mm.then_inc(ev("atp"), 1)

            scores(0)
            for g in range(4):
                if g < 3:
                    scores(g + 1)
                weigh_values(g)

            def project(n, lhs, out_bank, done, total):
                for j in range(total // 2):
                    w_ = chunk(n + j, ((), (2, D)))
                    for k in range(2):
                        for tt in range(TT):
                            for half in range(2):
                                mm = pe.matmul(ps[:, out_bank(tt, half), :], lhs[:, 2 * j + k, tt * P:(tt + 1) * P],
                                               w_[:, k, 512 * half:512 * half + 512],
                                               start=(j + k == 0), stop=(2 * j + k == total - 1))
                    mm.then_inc(chunk_used, 1)
                pe.wait_ge(chunk_used, n + total // 2)
                pe.nop().then_inc(done, 1)

            pe.wait_ge(ev("masked"), 4)
            pe.wait_ge(ev("convG_ready"), 4)
            project(10, u, lambda tt, half: 2 + 2 * tt + half, ev("pcp"), 4)
            pe.wait_ge(*nth("conv_sq_ready", 1))
            pe.wait_ge(*nth("attn_sq_ready", 1))
            pe.wait_ge(ev("attnT_raw"), 2)
            for i_ in range(2):
                for tt in range(TT):
                    mm = pe.matmul(ps[:, 1, 2 * i_ + tt:2 * i_ + tt + 1], sq[:, i_, tt * P:(tt + 1) * P], inv512,
                                   start=True, stop=True)
            mm.then_inc(ev("fine_ms"), 1)
            pe.wait_ge(ev("attnG_ready"), 4)
            pe.wait_ge(ev("fine_root"), 1)
            project(12, gc, lambda tt, half: [6, 7, 0, 1][2 * tt + half], ev("pap"), 4)

            pe.wait_ge(ev("mixc"), 4)
            turn_tokens(pe, "n1", False)
            turned(pe, "n1")
            logits(pe, "m1")
            turn_logits(pe, "m1")
            for which in range(2):
                w = chunk(14 + which, phase_one[14 + which])
                for tt in range(TT):
                    for k in range(KC):
                        mm = pe.matmul(ps[:, 4 + tt, 256 * which:256 * which + 256],
                                       xT[:, k, META + tt * P:META + (tt + 1) * P], w[:, k, :],
                                       start=(k == 0), stop=(k == KC - 1))
                mm.then_inc(chunk_used, 1)
            positions_of(pe, "m1")
            pe.wait_ge(ev("sh_h"), 2)
            for tt in range(TT):
                for c in range(2):
                    tr = pe.transpose(ps[:, 6, (2 * tt + c) * P:(2 * tt + c + 1) * P],
                                      hs[:, 256 * tt + c:256 * tt + 256:2], ident[:, :])
            tr.then_inc(ev("sh_hTp"), 1)
            w = chunk(16, phase_one[16])
            pe.wait_ge(ev("sh_hT"), 1)
            for tt in range(TT):
                for half in range(2):
                    for c in range(2):
                        mm = pe.matmul(ps[:, 2 * tt + half, :], hT[:, 2 * tt + c, :], w[:, c, 512 * half:512 * half + 512],
                                       start=(c == 0), stop=False, skip_group_check=True)
            mm.then_inc(chunk_used, 1)
            pe.wait_ge(ev("rounds"), 1)
            moe_tensor(pe, moes[0])

            pe.wait_ge(*nth("h_two", 2))
            turn_tokens(pe, "n2", False)
            turned(pe, "n2")
            base2 = moes[0]["next"]

            def by_token(n, banks, done, wait=None):
                if wait:
                    pe.wait_ge(*wait)
                for j in range(2):
                    w_ = chunk(n + j, ((), (4, 512)))
                    for tt in range(TT):
                        for k in range(4):
                            mm = pe.matmul(ps[:, banks[tt], :], xT[:, 4 * j + k, META + tt * P:META + (tt + 1) * P],
                                           w_[:, k, :], start=(j + k == 0), stop=(j + k == 4 and j == 1 and k == 3))
                        if j and tt == 0:
                            mm.then_inc(done, 1)
                    mm.then_inc(chunk_used, 1)
                pe.wait_ge(chunk_used, n + 2)
                pe.nop().then_inc(done, 1)

            by_feature(base2, [0, 1, 2, 3], TOK, ev("qdp"))
            by_feature(base2 + 2, [4, 5, 6, 7], TOK, ev("kdp"))
            by_token(base2 + 4, [0, 1], ev("vdp"), (ev("qd_ready"), 2))
            pe.wait_ge(ev("qd_ready"), 4)
            pe.wait_ge(*nth("kd_ready", 4))
            for hh in range(DH):
                for mp in range(2):
                    rows_ = slice(DD * mp, DD * mp + DD)
                    mm = pe.matmul(ps[:, 2 + mp, hh * P:(hh + 1) * P], qdT[rows_, hh, 0:P], kdT[rows_, hh, 0:P],
                                   start=True, stop=True)
            mm.then_inc(ev("sc2p"), 1)
            for hh in range(DH):
                for mp in range(2):
                    rows_ = slice(DD * mp, DD * mp + DD)
                    mm = pe.matmul(ps[:, 4 + 2 * mp + hh // 2, (hh % 2) * TOK:(hh % 2 + 1) * TOK],
                                   qdT[rows_, hh, P:TOK], kdT[rows_, hh, :], start=True, stop=True)
            mm.then_inc(ev("sc2p"), 1)
            by_feature(base2 + 6, [0, 1, 2, 3], TOK, ev("rp"),
                       lambda c: nth("vd_ready", c + 1) if c < 2 else nth("biased0", c - 1))
            by_token(base2 + 8, [4, 5], ev("vrp"), nth("biased1", 2))
            by_token(base2 + 10, [6, 7], ev("grp"))
            for j in range(3):
                pe.wait_ge(ev("a_ready"), 1 + (j > 0))
                pe.wait_ge(*nth("r_ready", 4))
                for hh in range(DH):
                    src = sd0[:, hh, :] if j == 0 else sd1[:, hh, (j - 1) * P:j * P]
                    tr = pe.transpose(ps[:, j, hh * P:(hh + 1) * P], src, ident[:, :])
                tr.then_inc(ev("aTp"), 1)
            for hh in range(DH):
                rows_ = slice(DD * (hh % 2), DD * (hh % 2) + DD)
                bank = [5, 6, 7, 0][hh]
                if hh == 0:
                    pe.wait_ge(*nth("vr_ready", 2))
                elif hh < 3:
                    pe.wait_ge(*nth("gr_ready", hh))
                else:
                    pe.wait_ge(ev("aT_ready"), 1)
                pe.matmul(ps[:, bank, 0:TOK], rT[rows_, 2 + hh // 2, 0:P], rT[rows_, hh // 2, :], start=True, stop=True)
                pe.matmul(ps[:, bank, TOK:384], rT[rows_, 2 + hh // 2, P:TOK], rT[rows_, hh // 2, P:TOK],
                          start=True, stop=True).then_inc(ev("rsp"), 1)
            pe.wait_ge(ev("aT_ready"), 3)
            for tt in range(TT):
                for hh in range(DH):
                    ks = [(0, 0)] if tt == 0 else [(1, 0), (2, 1)]
                    for b_, (at, kt) in enumerate(ks):
                        mm = pe.matmul(ps[:, 3 + tt, hh * DV:(hh + 1) * DV], aT[:, at, hh, :],
                                       vda[:, kt, hh * DV:(hh + 1) * DV], start=(b_ == 0), stop=(b_ == len(ks) - 1))
                mm.then_inc(ev("odp"), 1)
                pe.wait_ge(ev("rs_ready"), 8)
                for hh in range(DH):
                    ks = [(0, 0)] if tt == 0 else [(P, 0), (TOK, 1)]
                    for b_, (at, kt) in enumerate(ks):
                        mm = pe.matmul(ps[:, 1 + tt, hh * DV:(hh + 1) * DV], sTm[:, hh, at:at + P],
                                       vr[:, kt, hh * DV:(hh + 1) * DV], start=(b_ == 0), stop=(b_ == len(ks) - 1))
                mm.then_inc(ev("orp"), 1)
            for j, (tt, kind) in enumerate(((0, 0), (0, 1), (1, 0), (1, 1))):
                pe.wait_ge(ev("on_ready"), j + 1)
                src = (on_da, on_r)[kind]
                for c in range(DH):
                    tr = pe.transpose(ps[:, 5 + j if j < 3 else 0, c * P:(c + 1) * P], src[:, tt, c * P:(c + 1) * P],
                                      ident[:, :])
                tr.then_inc(ev("mTp"), 1)
            pe.wait_ge(ev("mT_ready"), 4)
            project(base2 + 12, mixT, lambda tt, half: 1 + 2 * tt + half, ev("out2p"), 8)
            pe.wait_ge(*nth("mixed2", 2))
            turn_tokens(pe, "n3", False)
            turned(pe, "n3")
            logits(pe, "m2")
            turn_logits(pe, "m2")
            positions_of(pe, "m2")
            pe.wait_ge(ev("rounds"), 2)
            moe_tensor(pe, moes[1])


_INS = ['x', 'positions', 'meta_tokens', 'pre_mix_norm', 'w_in', 'q_norm', 'w_uq', 'kv_norm', 'w_ukv', 'conv_w',
        'attn_out_norm', 'conv_out_norm', 'w_out', 'post_mix_norm', 'pre_ffn_norm', 'w_group_router',
        'b_group_router', 'w_expert_router', 'b_expert_router', 'w_gate', 'w_up', 'w_down', 'w_sh_gate', 'w_sh_up',
        'w_sh_down', 'post_ffn_norm', 'attn_norm_g_2', 'w_in_2', 'da_lambda_q1_2', 'da_lambda_k1_2',
        'da_lambda_q2_2', 'da_lambda_k2_2', 'da_subln_g_2', 'w_out_2', 'ffn_norm_g_2', 'router_group_w_2',
        'router_group_b_2', 'router_expert_w_2', 'router_expert_b_2', 'expert_w_gate_2', 'expert_w_up_2',
        'expert_w_down_2', 'final_norm_g_2']
_OUTS = [((1, 256, 1024), 'float32')]


def kernel(**inputs):
    import numpy as _np
    import concourse.bacc as _bacc
    from concourse import mybir as _mybir
    from concourse.bass_utils import run_bass_kernel_spmd as _run

    nc = _bacc.Bacc("TRN2", target_bir_lowering=False, num_devices=1)
    arrays, tensors = {}, {}
    for name in _INS:
        a = _np.ascontiguousarray(inputs[name])
        arrays[f"in_{name}_dram"] = a
        tensors[name] = nc.dram_tensor(f"in_{name}_dram", a.shape, _mybir.dt.from_np(a.dtype), kind="ExternalInput").ap()
    shape, dtype = _OUTS[0]
    result = nc.dram_tensor("out_0_dram", shape, _mybir.dt.from_np(_np.dtype(dtype)), kind="ExternalOutput").ap()
    two_block_kernel(nc, tensors, result)
    r = _run(nc, [arrays], core_ids=[0])
    return r.results[0]["out_0_dram"]
```

```python
from contextlib import ExitStack

import numpy as np

import concourse.bass as bass
from concourse import mybir

ALU = mybir.AluOpType
ACT = mybir.ActivationFunctionType
F32 = mybir.dt.float32
I32 = mybir.dt.int32
F32R = mybir.dt.float32r
AX = mybir.AxisListType.X


P = 128
D = 1024
KC = D // P
TOK = 256
TT = TOK // P
META = 16
COLS = META + TOK
EPS = 1e-6
NEG = -1e30

HEADS, NOPE, ROPE, VD = 8, 64, 32, 64
QK = NOPE + ROPE
QL, KVL = 256, 128
ZC = QL + KVL + ROPE
CONV = 512
CC = CONV // P
A_SCALE = QK ** -0.5

DH = 4
DD = 64
DV = 128
LAMBDA_INIT = 0.2
LN_GAMMA = [float(np.log1p(-np.exp2(-5.0 - h))) for h in range(DH)]
SLOPES = [float(np.exp2(-8.0 * (h + 1) / DH)) for h in range(DH)]

GROUPS, PER_GROUP, EXPERTS = 4, 8, 32
CAP = 64
PAIRS = EXPERTS // 2
MAX_ROUNDS = TOK // CAP

RING = 12
CH = 2048


def stream_of_phase_one(t):
    w_in = t["w_in"][0].rearrange("(p c) n -> p c n", c=KC)
    w_out = t["w_out"][0].rearrange("(c p) n -> p c n", p=P)
    out = []

    def block(w, a, b):
        for k in range(0, KC, 4):
            out.append((w[:, k:k + 4, a:b], (4, b - a)))

    block(w_in, 0, ZC)
    block(w_in, ZC + CONV, ZC + 2 * CONV)
    out.append((t["w_uq"][0].rearrange("(p c) n -> p c n", c=2), (2, HEADS * QK)))
    out.append((t["w_ukv"][0].rearrange("p (c n) -> p c n", c=1), (1, HEADS * (NOPE + VD))))
    block(w_in, ZC + 2 * CONV, ZC + 3 * CONV)
    block(w_in, ZC, ZC + CONV)
    for c in (4, 6, 0, 2):
        out.append((w_out[:, c:c + 2, :], (2, D)))
    for name in ("w_sh_gate", "w_sh_up"):
        out.append((t[name][0].rearrange("(p c) n -> p c n", c=KC), (KC, 256)))
    out.append((t["w_sh_down"][0].rearrange("(p c) n -> p c n", c=2), (2, D)))
    return out


def stream_of_phase_two(t):
    w_in = t["w_in_2"][0].rearrange("(p c) n -> p c n", c=KC)
    w_out = t["w_out_2"][0].rearrange("(c p) n -> p c n", p=P)
    out = []
    for b in range(6):
        for k in range(0, KC, 4):
            out.append((w_in[:, k:k + 4, 512 * b:512 * b + 512], (4, 512)))
    for c in (0, 2, 4, 6):
        out.append((w_out[:, c:c + 2, :], (2, D)))
    return out


def pair_chunks(gate, up, down, ff, pair):
    out = []
    rows = CH // ff
    for w in (gate, up):
        v = w[0].rearrange("e (p c) f -> e p c f", c=KC)
        for k in range(0, KC, rows):
            for e in range(2):
                out.append((v[bass.ds(2 * pair + e, 1), :, k:k + rows, :].rearrange("e p c f -> p (e c) f"),
                            (rows, ff)))
    fc = ff // P
    v = down[0].rearrange("e (p c) f -> e p c f", c=fc)
    for c in range(0, fc, 2):
        for e in range(2):
            out.append((v[bass.ds(2 * pair + e, 1), :, c:c + 2, :].rearrange("e p c f -> p (e c) f"), (2, D)))
    return out


def two_block_kernel(nc, t, out):
    ctx = ExitStack()
    with ctx:
        def sb(name, shape, dt=F32):
            return ctx.enter_context(nc.sbuf_tensor(name, shape, dt))

        events = {}

        SHARED = {
            "conv_sq_ready": ("square_sums", 0), "attn_sq_ready": ("square_sums", 1),
            "dist_i_ready": ("late_iota", 0), "lag_i_ready": ("late_iota", 1),
            "gcp": ("conv_block", 0), "xip": ("conv_block", 3), "gbp": ("conv_block", 6),
            "cqp": ("compressed_turned", 0), "ckvp": ("compressed_turned", 1), "krp": ("compressed_turned", 2),
            "qp": ("expanded", 0), "vp": ("expanded", 1), "kp": ("expanded", 4),
            "pcp": ("projected", 0), "pap": ("projected", 1), "out2p": ("projected", 2),
            "qdp": ("block2", 0), "kdp": ("block2", 3), "vdp": ("block2", 6), "rp": ("block2", 7),
            "vrp": ("block2", 10), "grp": ("block2", 11),
            "kr_ready": ("keys_ready", 0), "kT_ready": ("keys_ready", 1),
            "kd_ready": ("taken2", 0), "vd_ready": ("taken2", 4), "r_ready": ("taken2", 6), "vr_ready": ("taken2", 10),
            "gr_ready": ("taken2", 12),
            "sin_ready": ("sines", 0), "cos_ready": ("sines", 1),
            "pexp": ("exps", 0), "pexp2": ("exps", 16),
            "nmax": ("row_max", 0), "nmax2": ("row_max", 4),
            "cqT_ready": ("compressed_ready", 0), "ckvT_ready": ("compressed_ready", 2),
            "biased0": ("biased", 0), "biased1": ("biased", 2),
            "mixed1": ("h_ready", 0), "h_two": ("h_ready", 2), "mixed2": ("h_ready", 4), "h_four": ("h_ready", 6),
        }

        def ev(name):
            name = SHARED[name][0] if name in SHARED else name
            if name not in events:
                events[name] = ctx.enter_context(nc.semaphore(name))
            return events[name]

        def nth(name, n):
            if (name, n) in LAST_CHUNK:
                return chunk_used, LAST_CHUNK[name, n]
            return ev(name), (SHARED[name][1] if name in SHARED else 0) + n

        ring = sb("ring", [P, RING, CH])
        h = sb("h", [P, TT, D])
        xs = sb("xs", [P, TT, D])
        xT = sb("xT", [P, KC, COLS])
        gain_row = sb("gain_row", [P, D])
        ident = sb("ident", [P, P])
        ones = sb("ones", [P, P])
        before = sb("before", [P, P])
        gk = sb("gk", [P, 4, KC])
        gq = sb("gq", [P, 2])
        gkv = sb("gkv", [P, 1])
        rows = sb("rows", [21, P])
        cols = sb("cols", [P, 21])
        lams = sb("lams", [P, 4, DD])
        iota_i = sb("iota_i", [P, CAP], I32)
        iota = sb("iota", [P, CAP])
        slot_no = sb("slot_no", [P, CAP])
        wr = sb("wr", [P, KC, 36])
        br = sb("br", [36, 1])
        rounds_i = sb("rounds_i", [P, 2], I32)
        small = sb("small", [P, 640])
        ps = ctx.enter_context(nc.psum_tensor("ps", [P, 8, 512], F32))

        def carve(tensor):
            at = [0]

            def take(*shape, start=None):
                if start is not None:
                    at[0] = start
                n = int(np.prod(shape))
                v = tensor[:, at[0]:at[0] + n]
                at[0] += n
                assert at[0] <= tensor.shape[1], at[0]
                if len(shape) == 2:
                    v = v.rearrange("p (a b) -> p a b", b=shape[1])
                if len(shape) == 3:
                    v = v.rearrange("p (a b c) -> p a b c", b=shape[1], c=shape[2])
                return v
            return take

        tiny = carve(small)
        eps = tiny(1)
        half_pi = tiny(1)
        mean_sq = tiny(3)
        root = tiny(3)
        rstd = tiny(3)
        zss = tiny(5)
        zroot = tiny(5)
        zr = tiny(5)
        fine_root = tiny(4)
        fine_r = tiny(2, 2)
        freq = tiny(16)
        posf = tiny(3)
        inv512 = tiny(1)
        nmax = tiny(8)
        prow = tiny(8)
        lam = tiny(1)
        lam_a = tiny(2)
        lam_b = tiny(2)
        rnd = tiny(4)
        r_gmax = tiny(2)
        r_gsum = tiny(2)
        r_gw = tiny(2)
        r_gi = tiny(2)
        r_m1 = tiny(2)
        r_i1 = tiny(2)
        r_m2 = tiny(2)
        r_i2 = tiny(2)
        r_dd = tiny(2)
        r_e = tiny(2)
        r_e1 = tiny(2)
        r_w1 = tiny(2)
        r_w2 = tiny(2)
        r_c = tiny(1)
        slot_weight = tiny(1)
        ahead = tiny(3)
        r_gd = tiny(2, 4)
        r_ge = tiny(2, 4)
        r_geq = tiny(2, 4)
        r_gm = tiny(2, 4)
        r_pen = tiny(2, 4)
        hss = tiny(2, 8)
        hroot = tiny(2, 8)
        hrs = tiny(2, 8)
        pos_i = sb("pos_i", [P, 4], I32)
        with nc.sbuf_tensor("work", [P, 17664], F32) as work:
            pass
        sb("under_parts", [P, 10240])
        parts = sb("parts", [P, 2 * D + TT * P + 2 * TT * D + TT * 2 * P])

        a = carve(work)
        zq = a(3, 384)
        sq = a(3, TOK, start=0)
        kr = a(3, ROPE, start=1152)
        cqT = a(2, TOK)
        ckvT = a(COLS)
        qs = a(TT, HEADS, QK)
        kT = a(HEADS, COLS)
        mix = a(TT, D)
        qT = mix.rearrange("p t (h c) -> p (t h) c", c=TOK)
        vtok = a(3, 512)
        pr = a(2, 4, COLS)
        attnT = a(CC, TOK)
        gc = a(CC, COLS)
        u = a(CC, COLS)
        conv = a(CC, TOK)
        cs = a(3, ROPE)
        sn = a(3, ROPE)
        ang = a(3, ROPE // 2)
        turns_ = a(3, ROPE // 2)
        rtmp = a(HEADS, ROPE)
        mask = a(COLS)
        pT = qs.rearrange("p t h d -> p (t h d)").rearrange("p (k h c) -> p k h c", k=3, h=4)
        meta = attnT.rearrange("p c t -> p (c t)")[0:META, :]
        metan = conv.rearrange("p c t -> p (c t)")[0:META, :]

        m = carve(work)
        xgT = m(KC, 2 * P)
        sil = m(512)
        hs = m(512)
        hT = m(4, P)
        y = m(D)
        wonehot = m(TT, P)
        comb = m(TT, EXPERTS)
        posm = m(TT, EXPERTS)
        routed = m(TT, EXPERTS)
        mask1 = m(TT, EXPERTS)
        mask2 = m(TT, EXPERTS)
        em = m(TT, EXPERTS)
        e_t = m(TT, EXPERTS)
        lg = m(TT, 36)
        assert 2048 + 512 * 3 + 1024 + 256 + 7 * 64 + 72 <= 5632
        lgT = m(TOK, start=17664 - TOK)
        exact = carve(parts)
        y_high = exact(D)
        y_low = exact(D)
        scat = exact(TT, P)
        xs_high = exact(TT, D)
        xs_low = exact(TT, D)
        onehot = exact(TT, 2 * P)
        assert 10240 + parts.shape[1] <= 17664 - TOK
        b = carve(work)
        bias = b(DH, TOK, start=5632)
        decay = b(DH, TOK)
        dist = b(TOK)
        dist_i = work[:, 5632 + 2048 + 256:5632 + 2048 + 512].bitcast(I32)
        spare = (xT[:, :, :].rearrange("p c t -> p (c t)")[:, 0:CH], work[:, 8192:8192 + CH])
        qdT = b(DH, TOK, start=8192)
        kdT = b(DH, TOK)
        rT = b(4, TOK)
        vda = b(TT, 512)
        vr = b(TT, 512)
        gr = b(TT, 512)
        sd1 = b(8, TOK)
        sd0 = b(8, P)
        on_da = qdT.rearrange("p h t -> p (h t)").rearrange("p (t n) -> p t n", t=TT)
        on_r = kdT.rearrange("p h t -> p (h t)").rearrange("p (t n) -> p t n", t=TT)
        b2 = carve(work)
        aT = b2(3, DH, P, start=0)
        sTm = b2(DH, 384)
        mixT = b2(KC, TOK)

        landed = [ctx.enter_context(nc.semaphore(f"landed{s}")) for s in range(RING)]
        chunk_used = ev("chunk_used")
        phase_one = stream_of_phase_one(t)
        phase_two = stream_of_phase_two(t)
        moes = [
            dict(tag="m1", gate=t["w_gate"], up=t["w_up"], down=t["w_down"], ff=256, gains=1),
            dict(tag="m2", gate=t["expert_w_gate_2"], up=t["expert_w_up_2"], down=t["expert_w_down_2"], ff=512,
                 gains=3),
        ]
        TURN = {"m1": 1, "m2": 2}
        EARLIER = {"m1": 0, "m2": PAIRS}
        n = len(phase_one)
        for cfg, after in zip(moes, (phase_two, [])):
            cfg["per"] = len(pair_chunks(cfg["gate"], cfg["up"], cfg["down"], cfg["ff"], 0))
            cfg["base"] = n
            assert 2 * cfg["per"] % RING == 0
            n += PAIRS * cfg["per"]
            cfg["next"] = n
            n += len(after)

        def chunk_view(slot, shape):
            return ring[:, slot, 0:shape[0] * shape[1]].rearrange("p (a b) -> p a b", b=shape[1])

        two = moes[0]["next"]
        LAST_CHUNK = {
            ("zp", 3): 2, ("gcp", 4): 4, ("qp", 2): 5, ("kp", 8): 6, ("xip", 4): 8, ("gbp", 4): 10, ("pcp", 2): 12,
            ("pap", 2): 14, ("qdp", 4): two + 2, ("kdp", 4): two + 4, ("vdp", 2): two + 6, ("rp", 4): two + 8,
            ("vrp", 2): two + 10, ("grp", 2): two + 12, ("out2p", 2): two + 16,
        }

        LOOPS = ((0, 1), (2, PAIRS // 2 - 2), (PAIRS - 2, 1))

        def extra_rounds(eng, tag):
            extra = eng.value_load(rounds_i[0:1, TURN[tag] - 1:TURN[tag]], min_val=0, max_val=MAX_ROUNDS - 1)
            if tag == "m1":
                return extra, 0
            first = eng.value_load(rounds_i[0:1, 0:1], min_val=0, max_val=MAX_ROUNDS - 1)
            return extra, first * (PAIRS // 2)

        block = ctx.enter_context(nc.Block())

        @block.sync
        def _(sp):
            def load(n0, spec, turn, per_turn):
                src, shape = spec
                n_free = n0 - RING + 1
                if not isinstance(turn, int) or n_free + turn * per_turn > 0:
                    sp.wait_ge(chunk_used, turn * per_turn + n_free)
                sp.dma_start(chunk_view(n0 % RING, shape), src).then_inc(landed[n0 % RING], 16)

            for tt in range(TT):
                sp.dma_start(h[:, tt, :], t["x"][0, tt * P:(tt + 1) * P, :]).then_inc(ev(f"x_in{tt}"), 16)
            sp.dma_start(meta, t["meta_tokens"][:, :]).then_inc(ev("meta_in"), 16)
            for j, spec in enumerate(phase_one):
                load(j, spec, 0, 0)
            for cfg, rest in zip(moes, (phase_two, [])):
                tag = cfg["tag"]
                for p0, turns in LOOPS:
                    if turns == 1:
                        for k in range(2):
                            specs = pair_chunks(cfg["gate"], cfg["up"], cfg["down"], cfg["ff"], p0 + k)
                            for j, spec in enumerate(specs):
                                load(cfg["base"] + (p0 + k) * cfg["per"] + j, spec, 0, 0)
                        continue
                    with sp.Fori(0, turns) as i:
                        for k in range(2):
                            specs = pair_chunks(cfg["gate"], cfg["up"], cfg["down"], cfg["ff"], i * 2 + (p0 + k))
                            for j, spec in enumerate(specs):
                                load(cfg["base"] + (p0 + k) * cfg["per"] + j, spec, i, 2 * cfg["per"])
                sp.wait_ge(ev("rounds"), TURN[tag])
                extra, earlier_x = extra_rounds(sp, tag)
                with sp.If(extra > 0):
                    with sp.Fori(0, extra) as r:
                        with sp.Fori(0, PAIRS) as q:
                            specs = pair_chunks(cfg["gate"], cfg["up"], cfg["down"], cfg["ff"], q)
                            for j, (src, shape) in enumerate(specs):
                                if j % 2 == 0:
                                    sp.wait_ge(ev(f"{tag}_x_used"), (r * PAIRS + q) * cfg["per"] + j)
                                dst = spare[j % 2][:, 0:shape[0] * shape[1]].rearrange("p (a b) -> p a b", b=shape[1])
                                sp.dma_start(dst, src).then_inc(ev(f"{tag}_x_landed{j % 2}"), 16)
                for j, spec in enumerate(rest):
                    load(cfg["next"] + j, spec, 0, 0)
            for tt in range(TT):
                sp.wait_ge(ev("result"), tt + 1)
                sp.dma_start(out[0, tt * P:(tt + 1) * P, :], xs[:, tt, :]).then_inc(ev("stored"), 16)
            sp.wait_ge(ev("stored"), 16 * TT)

        def load_router(eng, wg, bg, we, be):
            eng.dma_start(wr[:, :, 0:GROUPS], t[wg][0].rearrange("(p c) e -> p c e", c=KC)).then_inc(ev("wr"), 16)
            eng.dma_start(wr[:, :, GROUPS:36], t[we][0].rearrange("(p c) e -> p c e", c=KC)).then_inc(ev("wr"), 16)
            eng.dma_start(br[0:GROUPS, :], t[bg][0].rearrange("(e o) -> e o", o=1)).then_inc(ev("br"), 16)
            eng.dma_start(br[GROUPS:36, :], t[be][0].rearrange("(e o) -> e o", o=1)).then_inc(ev("br"), 16)

        @block.gpsimd
        def _(pool):
            def keep_where(v, op, fill, base, pattern, mult):
                return pool.affine_select(out=v, in_=v, compare_op=op, fill=fill, base=base, pattern=pattern,
                                          channel_multiplier=mult)

            pool.memset(ident[:, :], 0.0).then_inc(ev("g0"), 1)
            pool.memset(ones[:, :], 1.0).then_inc(ev("tables_ready"), 1)
            pool.memset(before[:, :], 1.0).then_inc(ev("g0"), 1)
            pool.memset(mask, 0.0).then_inc(ev("g0"), 1)
            pool.wait_ge(ev("g0"), 3)
            keep_where(ident[:, :], ALU.not_equal, 1.0, 0, [[-1, P]], 1).then_inc(ev("tables_ready"), 1)
            keep_where(before[:, :], ALU.is_ge, 0.0, -1, [[1, P]], -1).then_inc(ev("tables_ready"), 1)
            keep_where(mask, ALU.is_ge, NEG, META + P, [[-1, COLS]], 1).then_inc(ev("tables_ready"), 1)
            pool.iota(iota_i[:, :], pattern=[[1, CAP]], base=0, channel_multiplier=0).then_inc(ev("tables_ready"), 1)
            pool.iota(pos_i[:, 3:4], pattern=[[1, 1]], base=0, channel_multiplier=1).then_inc(ev("tables_ready"), 1)
            for j in range(ROPE // 2):
                f = np.float32(1.0) / np.float32(10000.0) ** np.float32(2.0 * j / ROPE)
                pool.memset(freq[:, j:j + 1], float(f)).then_inc(ev("tables_ready"), 1)

            for j, name in enumerate(("pre_ffn_norm", "attn_norm_g_2", "ffn_norm_g_2")):
                pool.dma_start(gk[:, j + 1, :], t[name][0].rearrange("(p c) -> p c", c=KC))\
                    .then_inc(ev("params_in"), 16)
            pool.dma_start(gq[:, :], t["q_norm"][0].rearrange("(p c) -> p c", c=2)).then_inc(ev("params_in"), 16)
            pool.dma_start(gkv[:, :], t["kv_norm"][0].rearrange("(p c) -> p c", c=1)).then_inc(ev("params_in"), 16)
            pool.dma_start(rows[0:12, :], t["conv_w"][0].rearrange("w (c p) -> (w c) p", p=P))\
                .then_inc(ev("params_in"), 16)
            pool.dma_start(rows[12:16, :], t["attn_out_norm"][0].rearrange("(c p) -> c p", p=P))\
                .then_inc(ev("params_in"), 16)
            pool.dma_start(rows[16:20, :], t["conv_out_norm"][0].rearrange("(c p) -> c p", p=P))\
                .then_inc(ev("params_in"), 16)
            pool.dma_start(rows[20:21, :], t["da_subln_g_2"]).then_inc(ev("params_in"), 16)
            for j, name in enumerate(("da_lambda_q1_2", "da_lambda_q2_2", "da_lambda_k1_2", "da_lambda_k2_2")):
                pool.dma_start(lams[:, j, :], t[name].broadcast_to([P, DD])).then_inc(ev("lams_in"), 16)

            def squares_sum(src, dst, waits, tag, done):
                n = 0 if tag == "conv" else 2 * CC - 2
                for c in range(CC):
                    pool.wait_ge(*waits[c])
                    pool.tensor_tensor(sq[:, 2, :] if c else dst, src[:, c, :], src[:, c, :], ALU.mult)\
                        .then_inc(ev("sq_step"), 1)
                    n += 1
                    pool.wait_ge(ev("sq_step"), n)
                    if c:
                        add = pool.tensor_tensor(dst, dst, sq[:, 2, :], ALU.add)
                        if c == CC - 1:
                            add.then_inc(ev(done), 1)
                            pool.wait_ge(*nth(done, 1))
                        else:
                            add.then_inc(ev("sq_step"), 1)
                            n += 1
                            pool.wait_ge(ev("sq_step"), n)

            squares_sum(conv, sq[:, 0, :], [(ev("conv_ready"), c + 1) for c in range(CC)], "conv", "conv_sq_ready")
            squares_sum(attnT, sq[:, 1, :], [(ev("attnT_raw"), TT)] * CC, "attn", "attn_sq_ready")

            def split_tokens(tag):
                for tt in range(TT):
                    pool.wait_ge(ev("xs_ready"), {"m1": 4, "m2": 8}[tag] + tt)
                    pool.tensor_copy(xs_high[:, tt, :].bitcast(F32R), xs[:, tt, :]).then_inc(ev("xs_high"), 1)
                    pool.wait_ge(ev("xs_high"), 2 * TURN[tag] - 1 + tt)
                    pool.tensor_tensor(xs_low[:, tt, :].bitcast(F32R), xs[:, tt, :], xs_high[:, tt, :], ALU.subtract)\
                        .then_inc(ev("xs_low"), 1)

            pool.wait_ge(*nth("mixed1", TT))
            pool.iota(dist_i, pattern=[[-1, TOK]], base=P, channel_multiplier=1).then_inc(ev("dist_i_ready"), 1)
            split_tokens("m1")
            pool.wait_ge(ev("dist_ready"), 1)
            pool.iota(dist_i, pattern=[[1, TOK]], base=0, channel_multiplier=-1).then_inc(ev("lag_i_ready"), 1)
            pool.wait_ge(ev("decay_raw"), DH)
            keep_where(decay, ALU.is_ge, 0.0, 0, [[0, DH], [1, TOK]], -1).then_inc(ev("decay_ready"), 1)
            split_tokens("m2")

        def products_done(cfg, n, j, sfx=""):
            if sfx:
                return ev(f"{cfg['tag']}_x_used"), n * cfg["per"] + j
            return chunk_used, n * cfg["per"] + (cfg["base"] + j)

        def moe_scalar(act, cfg):
            tag, ff, per = cfg["tag"], cfg["ff"], cfg["per"]
            gates = KC * ff // CH * 2

            def pair(n, m, sfx=""):
                act.wait_ge(*products_done(cfg, m, gates, sfx))
                act.activation(sil[:, 0:ff], ps[:, 4, 0:ff], ACT.Silu).then_inc(ev(f"sil{sfx}"), 1)
                act.wait_ge(ev(f"hTp{sfx}"), n + 1)
                act.activation(hT[:, 0:ff // P, :], ps[:, 6, 0:ff].rearrange("p (c s) -> p c s", s=P), ACT.Copy)\
                    .then_inc(ev(f"hT{sfx}"), 1)
                act.wait_ge(*products_done(cfg, m, per, sfx))
                act.activation(y[:, 512:1024], ps[:, 7, :], ACT.Copy, scale=slot_weight).then_inc(ev(f"y1{sfx}"), 1)

            for p0, turns in LOOPS:
                first = EARLIER[tag] + p0
                if turns == 1:
                    for k in range(2):
                        pair(first + k, p0 + k)
                else:
                    with act.Fori(0, turns) as i:
                        for k in range(2):
                            pair(i * 2 + (first + k), i * 2 + (p0 + k))
            act.wait_ge(ev("rounds"), TURN[tag])
            extra, earlier_x = extra_rounds(act, tag)
            with act.If(extra > 0):
                with act.Fori(0, extra) as r:
                    with act.Fori(0, PAIRS) as q:
                        pair(earlier_x * 2 + (r * PAIRS + q), r * PAIRS + q, "_x")
            act.activation(ahead[:, TURN[tag] - 1:TURN[tag]], eps, ACT.Sqrt)
            act.wait_ge(ev("experts_summed"), earlier_x * 2 + extra * PAIRS + TURN[tag])

        def moe_vector(dve, cfg, chain):
            tag, ff, per = cfg["tag"], cfg["ff"], cfg["per"]
            ups = KC * ff // CH * 4

            def expert_cols(v, pair):
                return v[:, :, bass.ds(2 * pair, 2)].unsqueeze(3).broadcast_to([P, TT, 2, CAP])

            def slots():
                return slot_no[:, :].unsqueeze(1).unsqueeze(1).broadcast_to([P, TT, 2, CAP])

            def four(v):
                return v.rearrange("p t (e s) -> p t e s", e=2)

            def build_onehot(q, g, sfx=""):
                if not isinstance(g, int) or g > 0:
                    dve.wait_ge(ev(f"xgp{sfx}"), g * 4)
                dve.tensor_tensor(onehot.bitcast(F32R).rearrange("p t (e s) -> p t e s", e=4),
                                  posm[:, :, bass.ds(4 * q, 4)].unsqueeze(3).broadcast_to([P, TT, 4, CAP]),
                                  slot_no[:, :].unsqueeze(1).unsqueeze(1).broadcast_to([P, TT, 4, CAP]), ALU.is_equal)\
                    .then_inc(ev(f"onehot{sfx}"), 1)

            def build_weighted(pair, n, sfx=""):
                if not isinstance(n, int) or n > 0:
                    dve.wait_ge(ev(f"scatp{sfx}"), n)
                dve.tensor_tensor(four(wonehot), expert_cols(posm, pair), slots(), ALU.is_equal)\
                    .then_inc(ev(f"wraw{sfx}"), 1)
                dve.wait_ge(ev(f"wraw{sfx}"), n + 1)
                dve.tensor_tensor(four(wonehot), four(wonehot), expert_cols(comb, pair), ALU.mult)\
                    .then_inc(ev(f"wonehot{sfx}"), 1)

            def take_gathered(g, sfx=""):
                for b in range(4):
                    dve.wait_ge(ev(f"xgp{sfx}"), g * 4 + (b + 1))
                    gain = gk[:, cfg["gains"], 2 * b:2 * b + 2].unsqueeze(2).broadcast_to([P, 2, 2 * P])
                    dve.tensor_tensor(xgT[:, 2 * b:2 * b + 2, :],
                                      ps[:, 6 + b % 2, :].rearrange("p (c s) -> p c s", s=2 * P),
                                      gain, ALU.mult).then_inc(ev(f"xg{sfx}"), 1)

            def hidden(n, m, sfx=""):
                dve.wait_ge(ev(f"sil{sfx}"), n + 1)
                dve.wait_ge(*products_done(cfg, m, ups, sfx))
                dve.tensor_tensor(hs[:, 0:ff], sil[:, 0:ff], ps[:, 5, 0:ff], ALU.mult).then_inc(ev(f"h{sfx}"), 1)

            def take_scatter(n, sfx=""):
                dve.wait_ge(ev(f"scatp{sfx}"), n + 1)
                dve.tensor_reduce(slot_weight, ps[:, 7, 0:256], AX, ALU.max).then_inc(ev(f"scat{sfx}"), 1)
                dve.tensor_scalar(scat.bitcast(F32R), ps[:, 7, 0:256].rearrange("p (t s) -> p t s", s=P), 0.0, None,
                                  ALU.is_gt)\
                    .then_inc(ev(f"scat{sfx}"), 1)

            def take_y(n, sfx=""):
                dve.wait_ge(ev(f"y0p{sfx}"), n + 1)
                dve.wait_ge(ev(f"scat{sfx}"), n * 2 + 2)
                dve.tensor_scalar(y[:, 0:512], ps[:, 6, :], slot_weight, None, ALU.mult).then_inc(ev(f"y0{sfx}"), 1)
                for half in range(2):
                    v, high, low = (u_[:, 512 * half:512 * half + 512] for u_ in (y, y_high, y_low))
                    dve.wait_ge(ev(f"y{half}{sfx}"), n + 1)
                    dve.tensor_copy(high.bitcast(F32R), v).then_inc(ev(f"y_parts{sfx}"), 1)
                    dve.wait_ge(ev(f"y_parts{sfx}"), n * 4 + (2 * half + 1))
                    dve.tensor_tensor(low.bitcast(F32R), v, high, ALU.subtract).then_inc(ev(f"y_parts{sfx}"), 1)

            def two_pairs(q, last):
                for odd in range(2):
                    p = q * 2 + odd
                    n = q * 2 + (EARLIER[tag] + odd)
                    build_weighted(p, n)
                    if odd and not last:
                        build_onehot(q + 1, q + (EARLIER[tag] // 2 + 1))
                    hidden(n, p)
                    if odd and not last:
                        take_gathered(q + (EARLIER[tag] // 2 + 1))
                    take_scatter(n)
                    take_y(n)

            build_onehot(0, EARLIER[tag] // 2)
            count_rounds(dve, tag, chain)
            take_gathered(EARLIER[tag] // 2)
            two_pairs(0, False)
            with dve.Fori(0, PAIRS // 2 - 2) as i:
                two_pairs(i + 1, False)
            two_pairs(PAIRS // 2 - 1, True)
            dve.wait_ge(ev("rounds"), TURN[tag])
            extra, earlier_x = extra_rounds(dve, tag)
            with dve.If(extra > 0):
                with dve.Fori(0, extra) as r:
                    dve.wait_ge(ev("experts_summed"), TURN[tag])
                    dve.tensor_scalar(slot_no[:, :], slot_no[:, :], float(CAP), None, ALU.add)\
                        .then_inc(ev(f"{tag}_slots"), 1)
                    with dve.Fori(0, PAIRS // 2) as q:
                        dve.wait_ge(ev(f"{tag}_slots"), r + 1)
                        g = earlier_x + (r * (PAIRS // 2) + q)
                        build_onehot(q, g, "_x")
                        take_gathered(g, "_x")
                        for odd in range(2):
                            n = g * 2 + odd
                            build_weighted(q * 2 + odd, n, "_x")
                            hidden(n, r * PAIRS + (q * 2 + odd), "_x")
                            take_scatter(n, "_x")
                            take_y(n, "_x")
            dve.wait_ge(ev("experts_summed"), earlier_x * 2 + extra * PAIRS + TURN[tag])

        def moe_tensor(pe, cfg):
            tag, ff, per = cfg["tag"], cfg["ff"], cfg["per"]
            fc = ff // P
            rows_ = CH // ff

            def gather(g, part, sfx="", free=None):
                if part == 0:
                    pe.wait_ge(ev(f"onehot{sfx}"), g + 1)
                for b in range(2):
                    if free is not None:
                        pe.wait_ge(ev(f"y{b}"), free + 1)
                    if part == 1:
                        pe.wait_ge(ev(f"xg{sfx}"), g * 4 + (b + 1))
                    for c in range(2):
                        feature = 4 * part + 2 * b + c
                        for k, v in enumerate((xs_high, xs_low)):
                            for tt in range(TT):
                                mm = pe.matmul(ps[:, 6 + b, c * 2 * P:(c + 1) * 2 * P],
                                               v[:, tt, feature::KC].bitcast(F32R), onehot[:, tt, :].bitcast(F32R),
                                               start=(k + tt == 0), stop=(k + tt == 2))
                    mm.then_inc(ev(f"xgp{sfx}"), 1)

            def gates_and_ups(get, used, g, odd, sfx=""):
                pe.wait_ge(ev(f"xg{sfx}"), g * 4 + 4)
                j = 0
                for which in range(2):
                    for k0 in range(0, KC, rows_):
                        chunks = get(j, (rows_, ff))
                        for k in range(rows_):
                            for e in range(2):
                                mm = pe.matmul(ps[CAP * e:CAP * e + CAP, 4 + which, 0:ff],
                                               xgT[:, k0 + k, P * odd + CAP * e:P * odd + CAP * e + CAP], chunks[e][:, k, :],
                                               start=(k0 + k == 0), stop=(k0 + k == KC - 1), skip_group_check=True)
                                if k == rows_ - 1:
                                    mm.then_inc(used, 1)
                        j += 2
                return j

            def turn_hidden(n, sfx=""):
                pe.wait_ge(ev(f"h{sfx}"), n + 1)
                for c in range(fc):
                    tr = pe.transpose(ps[:, 6, c * P:(c + 1) * P], hs[:, c:ff:fc], ident[:, :])
                tr.then_inc(ev(f"hTp{sfx}"), 1)

            def turn_weights(n, sfx=""):
                pe.wait_ge(ev(f"wonehot{sfx}"), n + 1)
                for tt in range(TT):
                    tr = pe.transpose(ps[:, 7, tt * P:(tt + 1) * P], wonehot[:, tt, :], ident[:, :])
                tr.then_inc(ev(f"scatp{sfx}"), 1)

            def down(get, used, j, n, sfx=""):
                pe.wait_ge(ev(f"hT{sfx}"), n + 1)
                for c0 in range(0, fc, 2):
                    chunks = get(j, (2, D))
                    for half in range(2):
                        if half == 1 and c0 == 0:
                            pe.wait_ge(ev(f"scat{sfx}"), n * 2 + 2)
                        for k in range(2):
                            for e in range(2):
                                mm = pe.matmul(ps[CAP * e:CAP * e + CAP, 6 + half, :],
                                               hT[:, c0 + k, CAP * e:CAP * e + CAP],
                                               chunks[e][:, k, 512 * half:512 * half + 512],
                                               start=(c0 + k == 0), stop=(c0 + k == fc - 1), skip_group_check=True)
                                if half == 1 and k == 1:
                                    mm.then_inc(used, 1)
                        if half == 0 and c0 + 2 == fc:
                            mm.then_inc(ev(f"y0p{sfx}"), 1)
                    j += 2

            def scatter(n, half, first, last, sfx=""):
                pe.wait_ge(ev(f"y_parts{sfx}"), n * 4 + (2 * half + 2))
                for part, v in enumerate((y_high, y_low)):
                    for tt in range(TT):
                        mm = pe.matmul(ps[:, 2 * tt + half, :], scat[:, tt, :].bitcast(F32R),
                                       v[:, 512 * half:512 * half + 512].bitcast(F32R),
                                       start=first and part == 0, stop=last and part == 1, skip_group_check=True)
                return mm

            def two_pairs(q, q_first, turn, first, last):
                def getter(odd):
                    n0 = cfg["base"] + (2 * q_first + odd) * per

                    def get(j, shape):
                        views = []
                        for e in range(2):
                            slot, lap = (n0 + j + e) % RING, (n0 + j + e) // RING
                            pe.wait_ge(landed[slot], turn * (16 * (2 * per // RING)) + 16 * (lap + 1))
                            views.append(chunk_view(slot, shape))
                        return views
                    return get

                g = q + EARLIER[tag] // 2
                for odd in range(2):
                    n = q * 2 + (EARLIER[tag] + odd)
                    first_pair, ahead = first and not odd, odd and not last
                    if not first_pair:
                        done = q * 2 + (EARLIER[tag] + odd - 1)
                    opens = tag == "m2" and first and odd
                    j = gates_and_ups(getter(odd), chunk_used, g, odd)
                    if ahead:
                        gather(g + 1, 0, free=q * 2 + EARLIER[tag])
                    if not first_pair:
                        scatter(done, 0, opens, False)
                    if ahead:
                        gather(g + 1, 1)
                        pe.wait_ge(ev("xg"), g * 4 + 7)
                    turn_hidden(n)
                    if not first_pair:
                        scatter(done, 1, opens, False)
                    if ahead:
                        pe.wait_ge(ev("xg"), g * 4 + 8)
                    turn_weights(n)
                    down(getter(odd), chunk_used, j, n)

            pe.wait_ge(ev("xs_low"), TT * TURN[tag])
            for part in range(2):
                gather(EARLIER[tag] // 2, part)
            two_pairs(0, 0, 0, True, False)
            with pe.Fori(0, PAIRS // 2 - 2) as i:
                two_pairs(i + 1, 1, i, False, False)
            two_pairs(PAIRS // 2 - 1, PAIRS // 2 - 1, 0, False, True)
            for half in range(2):
                mm = scatter(EARLIER[tag] + PAIRS - 1, half, False, True)
            mm.then_inc(ev("experts_summed"), 1)

            pe.wait_ge(ev("rounds"), TURN[tag])
            extra, earlier_x = extra_rounds(pe, tag)
            with pe.If(extra > 0):
                with pe.Fori(0, extra) as r:
                    with pe.Fori(0, PAIRS // 2) as q:
                        g = earlier_x + (r * (PAIRS // 2) + q)
                        used = ev(f"{tag}_x_used")
                        for part in range(2):
                            gather(g, part, "_x")
                        for odd in range(2):
                            n = g * 2 + odd

                            def get(j, shape):
                                turn = r * PAIRS + (q * 2 + odd)
                                for e in range(2):
                                    pe.wait_ge(ev(f"{tag}_x_landed{e}"), (turn * (per // 2) + (j // 2 + 1)) * 16)
                                return [spare[e][:, 0:shape[0] * shape[1]].rearrange("p (a b) -> p a b", b=shape[1])
                                        for e in range(2)]

                            j = gates_and_ups(get, used, g, odd, "_x")
                            turn_hidden(n, "_x")
                            turn_weights(n, "_x")
                            down(get, used, j, n, "_x")
                            for half in range(2):
                                mm = scatter(n, half, False, True, "_x")
                            mm.then_inc(ev("experts_summed"), 1)

        def route(dve, tag, chain):
            A = lg[:, :, 0:GROUPS]
            E = lg[:, :, GROUPS:36]

            def over(v, n):
                return v.unsqueeze(2).broadcast_to([P, TT, n])

            def first_of(values, top, hit, ids, lowest, mask_out, n):
                chain(dve.tensor_tensor(hit, values, over(top, n), ALU.is_ge))
                chain(dve.scalar_tensor_tensor(hit, hit, -64.0, ids, ALU.mult, ALU.add))
                chain(dve.tensor_reduce(lowest, hit, AX, ALU.min))
                chain(dve.tensor_tensor(mask_out, hit, over(lowest, n), ALU.is_equal))

            ids4 = iota[:, 0:GROUPS].unsqueeze(1).broadcast_to([P, TT, GROUPS])
            ids32 = iota[:, 0:EXPERTS].unsqueeze(1).broadcast_to([P, TT, EXPERTS])
            dve.wait_ge(ev("router_pe"), 3 * TURN[tag] - 1)
            chain(dve.tensor_copy(lg, ps[:, 7, 0:72].rearrange("p (t e) -> p t e", t=TT)))
            chain(dve.tensor_reduce(r_gmax, A, AX, ALU.max))
            dve.tensor_tensor(r_gd, A, over(r_gmax, GROUPS), ALU.subtract).then_inc(ev("router_diff"), 1)
            first_of(A, r_gmax, r_geq, ids4, r_gi, r_gm, GROUPS)
            chain(dve.tensor_scalar(r_pen, r_gm, 1.0, 1e30, ALU.subtract, ALU.mult))

            def grouped(v):
                return v.rearrange("p t (g e) -> p t g e", g=GROUPS)

            def per_group(v):
                return v.unsqueeze(3).broadcast_to([P, TT, GROUPS, PER_GROUP])

            chain(dve.tensor_tensor(grouped(em), grouped(E), per_group(r_gm), ALU.mult))
            chain(dve.tensor_tensor(grouped(em), grouped(em), per_group(r_pen), ALU.add))
            chain(dve.tensor_reduce(r_m1, em, AX, ALU.max))
            first_of(em, r_m1, e_t, ids32, r_i1, mask1, EXPERTS)
            chain(dve.scalar_tensor_tensor(em, mask1, -2e30, em, ALU.mult, ALU.add))
            chain(dve.tensor_reduce(r_m2, em, AX, ALU.max))
            dve.tensor_tensor(r_dd, r_m2, r_m1, ALU.subtract).then_inc(ev("router_diff"), 1)
            first_of(em, r_m2, e_t, ids32, r_i2, mask2, EXPERTS)
            dve.tensor_tensor(routed, mask1, mask2, ALU.add).then_inc(ev("routed"), 1)
            dve.wait_ge(ev("router_exp"), 2 * TURN[tag] - 1)
            chain(dve.tensor_reduce(r_gsum, r_ge, AX, ALU.add))
            chain(dve.reciprocal(r_gw, r_gsum))
            dve.wait_ge(ev("router_exp"), 2 * TURN[tag])
            chain(dve.tensor_scalar(r_e1, r_e, 1.0, None, ALU.add))
            chain(dve.reciprocal(r_w1, r_e1))
            chain(dve.tensor_tensor(r_w1, r_w1, r_gw, ALU.mult))
            chain(dve.tensor_tensor(r_w2, r_w1, r_e, ALU.mult))
            chain(dve.tensor_tensor(comb, mask1, over(r_w1, EXPERTS), ALU.mult))
            chain(dve.tensor_tensor(e_t, mask2, over(r_w2, EXPERTS), ALU.mult))
            chain(dve.tensor_tensor(comb, comb, e_t, ALU.add))

        def place(dve, tag, chain):
            dve.wait_ge(ev("router_pe"), 3 * TURN[tag])
            pos = ps[:, 7, 128:192].rearrange("p (t e) -> p t e", t=TT)
            chain(dve.scalar_tensor_tensor(posm, pos, 1.0, routed, ALU.add, ALU.mult))
            dve.tensor_scalar(posm, posm, -1.0, None, ALU.add).then_inc(ev("placed"), 1)
            dve.tensor_copy(slot_no[:, :], iota[:, :]).then_inc(ev("placed"), 1)
            dve.tensor_reduce(r_c, ps[:, 7, 192:224], AX, ALU.max).then_inc(ev("placed"), 1)
            dve.wait_ge(ev("placed"), 3 * TURN[tag])

        def count_rounds(dve, tag, chain):
            for k in range(1, MAX_ROUNDS):
                chain(dve.tensor_scalar(rnd[:, k - 1:k], r_c, float(CAP * k), None, ALU.is_gt))
            chain(dve.tensor_reduce(rnd[:, 3:4], rnd[:, 0:3], AX, ALU.add))
            dve.tensor_copy(rounds_i[:, TURN[tag] - 1:TURN[tag]], rnd[:, 3:4]).then_inc(ev("rounds"), 1)

        def route_scalar(act, tag):
            act.wait_ge(ev("router_pe"), 3 * TURN[tag] - 2)
            act.activation(lgT[0:36, :], ps[0:36, 6, 0:TOK], ACT.Identity, bias=br[:, :]).then_inc(ev("lgT"), 1)
            act.wait_ge(ev("router_diff"), 2 * TURN[tag] - 1)
            act.activation(r_ge, r_gd, ACT.Exp).then_inc(ev("router_exp"), 1)
            act.wait_ge(ev("router_diff"), 2 * TURN[tag])
            act.activation(r_e, r_dd, ACT.Exp).then_inc(ev("router_exp"), 1)

        def logits(pe, tag, tt):
            pe.wait_ge(ev("wr"), 32 * TURN[tag])
            for k in range(KC):
                mm = pe.matmul(ps[0:36, 6, tt * P:(tt + 1) * P], wr[:, k, :], xT[:, k, META + tt * P:META + (tt + 1) * P],
                               start=(k == 0), stop=(k == KC - 1))
            if tt:
                mm.then_inc(ev("router_pe"), 1)

        def turn_logits(pe, tag):
            pe.wait_ge(ev("lgT"), TURN[tag])
            for tt in range(TT):
                tr = pe.transpose(ps[:, 7, 36 * tt:36 * tt + 36], lgT[0:36, tt * P:(tt + 1) * P], ident[0:36, 0:36])
            tr.then_inc(ev("router_pe"), 1)

        def positions_of(pe, tag):
            pe.wait_ge(ev("routed"), TURN[tag])
            r0, r1 = routed[:, 0, :], routed[:, 1, :]
            pe.matmul(ps[:, 7, 128:160], before[:, :], r0, start=True, stop=True)
            pe.matmul(ps[:, 7, 160:192], before[:, :], r1, start=True, stop=False)
            pe.matmul(ps[:, 7, 160:192], ones[:, :], r0, start=False, stop=True)
            pe.matmul(ps[:, 7, 192:224], ones[:, :], r0, start=True, stop=False)
            pe.matmul(ps[:, 7, 192:224], ones[:, :], r1, start=False, stop=True).then_inc(ev("router_pe"), 1)

        STAGES_ROWS = {"n0": (0, 1), "o1": (3, 2), "n1": (4, 2), "o2": (7, 1), "n2": (9, 1), "n3": (11, 1), "o4": (13, 1)}

        def nth_row(tag, tt):
            return STAGES_ROWS[tag][0] + STAGES_ROWS[tag][1] * tt + 1
        STAGES_XS = {"n0": 0, "n1": 3, "n2": 5, "n3": 7}
        STAGES_TURNED = {"n0": 0, "n1": KC, "n2": KC + 4, "n3": KC + 8}
        STAGES_XT_V = {"n0": 0, "n1": KC // 2, "n2": KC // 2 + 3, "n3": KC // 2 + 6}
        STAGES_XT_S = {"n0": 0, "n1": KC // 2, "n2": KC // 2 + 4, "n3": KC // 2 + 8}
        TURN_BANKS = {"n1": (2, 3, 4, 5), "n2": (4, 5, 6, 7), "n3": (5, 6, 7, 0)}

        def mean_square(act, tag, tt, src, junk, wait, parts=P):
            act.wait_ge(*wait)
            act.activation(junk, src, ACT.Square, scale=D ** -0.5, accum_out=mean_sq[0:parts, tt:tt + 1])\
                .then_inc(ev("mean_sq"), 1)
            act.wait_ge(ev("mean_sq"), nth_row(tag, tt))
            act.activation(root[0:parts, tt:tt + 1], mean_sq[0:parts, tt:tt + 1], ACT.Sqrt, bias=eps[0:parts, :])\
                .then_inc(ev("root"), 1)

        def one_over(dve, tag, tt, chain, parts=P):
            dve.wait_ge(ev("root"), nth_row(tag, tt))
            chain(dve.reciprocal(rstd[0:parts, tt:tt + 1], root[0:parts, tt:tt + 1]))

        def turn_first_tokens(pe):
            for tt in range(TT):
                pe.wait_ge(ev("xs_ready"), STAGES_XS["n0"] + tt + 1)
                for k in range(KC):
                    pe.transpose(ps[:, k, META + tt * P:META + (tt + 1) * P], xs[:, tt, k::KC], ident[:, :])
            pe.wait_ge(ev("xs_ready"), STAGES_XS["n0"] + TT + 1)
            for k in range(KC):
                pe.transpose(ps[:, k, 0:META], metan[:, k::KC], ident[0:META, 0:META]).then_inc(ev("turned"), 1)
            pe.wait_ge(ev("xT_scalar"), KC // 2)
            pe.wait_ge(ev("xT_vector"), KC // 2)

        def take_first_turned(eng, parity):
            for k in range(parity, KC, 2):
                eng.wait_ge(ev("turned"), k + 1)
                if parity:
                    eng.activation(xT[:, k, :], ps[:, k, 0:COLS], ACT.Copy, scale=gk[:, 0, k:k + 1])\
                        .then_inc(ev("xT_scalar"), 1)
                else:
                    eng.tensor_scalar(xT[:, k, :], ps[:, k, 0:COLS], gk[:, 0, k:k + 1], None, ALU.mult)\
                        .then_inc(ev("xT_vector"), 1)

        def turn_tokens(pe, tag, tt):
            pe.wait_ge(ev("xs_ready"), STAGES_XS[tag] + tt + 1)
            for k in range(KC):
                tr = pe.transpose(ps[:, TURN_BANKS[tag][2 * tt + k // 4], k % 4 * P:(k % 4 + 1) * P], xs[:, tt, k::KC],
                                  ident[:, :])
                if k % 4 == 3:
                    tr.then_inc(ev("turned"), 1)

        def take_turned(dve, tag, g, tt):
            for b in range(2 - tt):
                dve.wait_ge(ev("turned"), STAGES_TURNED[tag] + 2 * tt + b + 1)
                dve.tensor_tensor(xT[:, 4 * b:4 * b + 4, META + tt * P:META + (tt + 1) * P],
                                  ps[:, TURN_BANKS[tag][2 * tt + b], :].rearrange("p (k t) -> p k t", k=4),
                                  gk[:, g, 4 * b:4 * b + 4].unsqueeze(2).broadcast_to([P, 4, P]), ALU.mult)\
                    .then_inc(ev("xT_vector"), 1)

        def take_last_turned(act, tag, g):
            act.wait_ge(ev("turned"), STAGES_TURNED[tag] + 4)
            for k in range(4, KC):
                act.activation(xT[:, k, META + P:COLS], ps[:, TURN_BANKS[tag][3], (k - 4) * P:(k - 3) * P], ACT.Copy,
                               scale=gk[:, g, k:k + 1]).then_inc(ev("xT_scalar"), 1)

        def turned(pe, tag, tt):
            pe.wait_ge(ev("xT_vector"), STAGES_XT_V[tag] + 2 + tt)
            if tt:
                pe.wait_ge(ev("xT_scalar"), STAGES_XT_S[tag] + 4)

        TWO_PI_HI = 6.28125
        TWO_PI_MID = 0.0019350051879882812
        TWO_PI_LO = 3.01991598e-07
        ROUNDER = 12582912.0
        SC_KEYS = [META + P, COLS]
        conv_banks = [1, 6, 7, 0]

        @block.scalar
        def _(act):
            for tt in range(TT):
                act.dma_start(pos_i[:, tt:tt + 1], t["positions"][0, tt * P:(tt + 1) * P].rearrange("(p o) -> p o", o=1))\
                    .then_inc(ev("pos_in"), 16)
            act.dma_start(gk[:, 0, :], t["pre_mix_norm"][0].rearrange("(p c) -> p c", c=KC)).then_inc(ev("gain0_in"), 16)

            act.wait_ge(ev("consts"), 1)
            act.activation(ahead[:, 2:3], eps, ACT.Sqrt)
            for tt in range(TT):
                mean_square(act, "n0", tt, h[:, tt, :], xs[:, tt, :], (ev(f"x_in{tt}"), 16))
            mean_square(act, "n0", 2, meta, metan, (ev("meta_in"), 16), META)
            act.wait_ge(ev("gain0_in"), 16)
            take_first_turned(act, 1)

            act.wait_ge(ev("ang_ready"), 2)
            act.activation(sn[:, :, ROPE // 2:ROPE], ang, ACT.Sin).then_inc(ev("sin_ready"), 1)
            act.activation(cs[:, :, 0:ROPE // 2], turns_, ACT.Sin, bias=half_pi, scale=-1.0).then_inc(ev("cos_ready"), 1)

            for tt in range(TT):
                act.wait_ge(ev("zp"), tt + 1)
                junk = qs.rearrange("p t h d -> p (t h d)")
                act.activation(junk[:, tt * QL:(tt + 1) * QL], ps[:, tt, 0:QL], ACT.Square, scale=QL ** -0.5,
                               accum_out=zss[:, 2 * tt:2 * tt + 1]).then_inc(ev("zss"), 1)
                act.activation(junk[:, (4 + tt) * KVL:(5 + tt) * KVL], ps[:, tt, QL:QL + KVL], ACT.Square, scale=KVL ** -0.5,
                               accum_out=zss[:, 2 * tt + 1:2 * tt + 2]).then_inc(ev("zss"), 1)
            act.wait_ge(*nth("zp", 3))
            act.activation(junk[0:META, 6 * KVL:7 * KVL], ps[0:META, 2, 0:KVL], ACT.Square, scale=KVL ** -0.5,
                           accum_out=zss[0:META, 4:5]).then_inc(ev("zss"), 1)
            act.wait_ge(ev("zss"), 5)
            act.activation(zroot, zss, ACT.Sqrt, bias=eps).then_inc(ev("zroot"), 1)

            act.dma_start(gain_row[:, :], t["post_mix_norm"].broadcast_to([P, D])).then_inc(ev("gain_row"), 16)
            load_router(act, "w_group_router", "b_group_router", "w_expert_router", "b_expert_router")
            for c in range(CC):
                act.wait_ge(*nth("gcp", c + 1))
                act.activation(gc[:, c, :], ps[:, 3 + c, 0:COLS], ACT.Copy).then_inc(ev("gc_ready"), 1)
            act.wait_ge(*nth("krp", 1))
            act.activation(kT[NOPE:QK, :, :], ps[0:ROPE, 1, 0:COLS].unsqueeze(1).broadcast_to([ROPE, HEADS, COLS]),
                           ACT.Copy).then_inc(ev("kr_ready"), 1)
            for hh in range(HEADS):
                act.wait_ge(*nth("kp", hh + 1))
                act.activation(kT[0:NOPE, hh, :], ps[0:NOPE, conv_banks[hh % 4], 0:COLS], ACT.Copy)\
                    .then_inc(ev("kT_ready"), 1)
            for j, bank in enumerate((5, 2, 3, 4)):
                act.wait_ge(ev("qTp"), j + 1)
                tt, h0 = j // 2, 4 * (j % 2)
                act.activation(qT[0:QK, h0:h0 + 4, tt * P:(tt + 1) * P],
                               ps[0:QK, bank, :].rearrange("p (h c) -> p h c", h=4), ACT.Copy)\
                    .then_inc(ev("qT_ready"), 1)
            def exps(g):
                act.wait_ge(*nth("nmax", g + 1))
                b_ = g % 2
                for j in range(4):
                    row = pr[:, b_, j, 0:SC_KEYS[g // 2]]
                    act.activation(row, row, ACT.Exp, bias=nmax[:, 4 * b_ + j:4 * b_ + j + 1],
                                   accum_out=prow[:, 4 * b_ + j:4 * b_ + j + 1]).then_inc(ev("pexp"), 1)

            def take_second_block(g):
                if g >= 2:
                    act.wait_ge(ev("pTp"), g + 1)
                    act.activation(pT[:, 1, :, :], ps[:, 7, :].rearrange("p (h c) -> p h c", h=4), ACT.Copy)\
                        .then_inc(ev("pT7"), 1)

            exps(0)
            for g in range(4):
                if g < 3:
                    exps(g + 1)
                take_second_block(g)
                act.wait_ge(ev("cols_ready"), 1)
                act.wait_ge(ev("conv_ready"), g + 1)
                act.activation(u[:, g, 0:TOK], conv[:, g, :], ACT.Copy, scale=cols[:, 16 + g:17 + g])\
                    .then_inc(ev("convG_ready"), 1)
            act.wait_ge(ev("attnT_raw"), 2)
            for c in range(CC):
                act.activation(gc[:, c, 0:TOK], attnT[:, c, :], ACT.Copy, scale=cols[:, 12 + c:13 + c])\
                    .then_inc(ev("attnG_ready"), 1)
            act.wait_ge(ev("fine_ms"), 1)
            act.activation(fine_root, ps[:, 1, 0:4], ACT.Sqrt, bias=eps).then_inc(ev("fine_root"), 1)
            act.wait_ge(ev("fine_r"), 1)
            act.wait_ge(*nth("pcp", 2))
            for tt in range(TT):
                for half in range(2):
                    act.activation(mix[:, tt, 512 * half:512 * half + 512], ps[:, 2 + 2 * tt + half, :],
                                   ACT.Copy, scale=fine_r[:, 0, tt:tt + 1]).then_inc(ev("mixc"), 1)
            for tt in range(TT):
                mean_square(act, "o1", tt, mix[:, tt, :], xs[:, tt, :], (ev("mixa"), tt + 1))
                mean_square(act, "n1", tt, h[:, tt, :], xs[:, tt, :], nth("mixed1", tt + 1))
            act.wait_ge(ev("params_in"), 144)
            act.dma_start(gain_row[:, :], t["post_ffn_norm"].broadcast_to([P, D])).then_inc(ev("gain_row"), 16)
            take_last_turned(act, "n1", 1)
            act.wait_ge(ev("br"), 32)
            route_scalar(act, "m1")
            for tt in range(TT):
                act.wait_ge(chunk_used, 16)
                act.activation(sil[:, 256 * tt:256 * tt + 256], ps[:, 4 + tt, 0:256], ACT.Silu).then_inc(ev("sh_sil"), 1)
            act.wait_ge(ev("sh_hTp"), 1)
            act.activation(hT, ps[:, 6, :].rearrange("p (c s) -> p c s", s=P), ACT.Copy).then_inc(ev("sh_hT"), 1)
            act.wait_ge(ev("lag_ready"), 1)
            for hh in range(DH):
                act.activation(decay[:, hh, :], dist, ACT.Exp, scale=LN_GAMMA[hh]).then_inc(ev("decay_raw"), 1)
            act.wait_ge(ev("lam_a"), 1)
            act.activation(lam_b, lam_a, ACT.Exp).then_inc(ev("lam_b"), 1)
            act.wait_ge(ev("router_pe"), 1)
            load_router(act, "router_group_w_2", "router_group_b_2", "router_expert_w_2", "router_expert_b_2")
            moe_scalar(act, moes[0])

            for tt in range(TT):
                mean_square(act, "o2", tt, ps[:, 2 * tt:2 * tt + 2, :], xs[:, tt, :].rearrange("p (a b) -> p a b", a=2),
                            (ev("experts_summed"), 1))
            for tt in range(TT):
                mean_square(act, "n2", tt, h[:, tt, :], xs[:, tt, :], nth("h_two", tt + 1))
            act.wait_ge(*nth("h_two", TT))
            act.dma_start(gain_row[:, :], t["final_norm_g_2"].rearrange("(a n) -> a n", a=1).broadcast_to([P, D]))\
                .then_inc(ev("gain_row"), 16)
            take_last_turned(act, "n2", 2)
            for c in range(DH):
                act.wait_ge(*nth("kdp", c + 1))
                act.activation(kdT[:, c, :], ps[:, 4 + c, 0:TOK], ACT.Copy).then_inc(ev("kd_ready"), 1)
            for tt in range(TT):
                act.wait_ge(*nth("vdp", tt + 1))
                act.activation(vda[:, tt, :], ps[:, tt, :], ACT.Copy).then_inc(ev("vd_ready"), 1)

            def exps2(tile, src):
                act.wait_ge(*nth("nmax2", tile + 1))
                for j in range(8):
                    act.activation(src[:, j, :], src[:, j, :], ACT.Exp, bias=nmax[:, j:j + 1],
                                   accum_out=prow[:, j:j + 1]).then_inc(ev("pexp2"), 1)

            exps2(0, sd0)
            for c in range(4):
                act.wait_ge(*nth("rp", c + 1))
                act.activation(rT[:, c, :], ps[:, c, 0:TOK], ACT.Copy).then_inc(ev("r_ready"), 1)
            exps2(1, sd1)
            for tt in range(TT):
                act.wait_ge(*nth("vrp", tt + 1))
                act.activation(vr[:, tt, :], ps[:, 4 + tt, :], ACT.Copy).then_inc(ev("vr_ready"), 1)
            for j in range(3):
                act.wait_ge(ev("aTp"), j + 1)
                act.activation(aT[:, j, :, :], ps[:, j, :].rearrange("p (h c) -> p h c", h=DH), ACT.Copy)\
                    .then_inc(ev("aT_ready"), 1)
            n = 0
            for tt in range(TT):
                for kind, bank in ((0, 1 + 2 * tt), (1, 2 + 2 * tt)):
                    act.wait_ge(ev("odp" if kind == 0 else "orp"), tt + 1)
                    for hh in range(DH):
                        junk = sd1.rearrange("p a b -> p (a b)")[:, n * DV:(n + 1) * DV]
                        act.activation(junk, ps[:, bank, hh * DV:(hh + 1) * DV], ACT.Square, scale=DV ** -0.5,
                                       accum_out=hss[:, tt, 4 * kind + hh:4 * kind + hh + 1]).then_inc(ev("hss"), 1)
                        n += 1
                    act.wait_ge(ev("hss"), n)
                    act.activation(hroot[:, tt, 4 * kind:4 * kind + 4], hss[:, tt, 4 * kind:4 * kind + 4], ACT.Sqrt,
                                   bias=eps).then_inc(ev("hroot"), 1)
            for tt in range(TT):
                act.wait_ge(*nth("grp", tt + 1))
                act.activation(gr[:, tt, :], ps[:, 6 + tt, :], ACT.Silu).then_inc(ev("gr_ready"), 1)
            for j, (tt, kind) in enumerate(((0, 0), (0, 1), (1, 0), (1, 1))):
                act.wait_ge(ev("mTp"), j + 1)
                dst = mixT[:, 4 * kind:4 * kind + 4, tt * P:(tt + 1) * P]
                src = ps[:, 5 + j if j < 3 else 0, :].rearrange("p (h c) -> p h c", h=DH)
                if kind == 0:
                    act.activation(dst, src, ACT.Copy, scale=cols[:, 20:21]).then_inc(ev("mT_ready"), 1)
                else:
                    act.activation(dst, src, ACT.Copy).then_inc(ev("mT_ready"), 1)
            for tt in range(TT):
                mean_square(act, "n3", tt, h[:, tt, :], xs[:, tt, :], nth("mixed2", tt + 1))
            take_last_turned(act, "n3", 3)
            act.wait_ge(ev("br"), 64)
            route_scalar(act, "m2")
            moe_scalar(act, moes[1])
            for tt in range(TT):
                mean_square(act, "o4", tt, h[:, tt, :], xs[:, tt, :], nth("h_four", tt + 1))

        @block.vector
        def _(dve):
            count = [0]

            def chain(ins):
                count[0] += 1
                ins.then_inc(ev("vector_chain"), 1)
                dve.wait_ge(ev("vector_chain"), count[0])

            chain(dve.memset(eps, EPS))
            chain(dve.memset(half_pi, float(np.pi / 2)))
            chain(dve.memset(zss, 1.0))
            chain(dve.memset(inv512, 1.0 / 512.0))
            dve.memset(mean_sq, 1.0).then_inc(ev("consts"), 1)

            for tt in range(TT):
                one_over(dve, "n0", tt, chain)
                dve.tensor_scalar(xs[:, tt, :], h[:, tt, :], rstd[:, tt:tt + 1], None, ALU.mult).then_inc(ev("xs_ready"), 1)
            one_over(dve, "n0", 2, chain, META)
            dve.tensor_scalar(metan, meta, rstd[0:META, 2:3], None, ALU.mult).then_inc(ev("xs_ready"), 1)
            dve.wait_ge(ev("gain0_in"), 16)
            take_first_turned(dve, 0)
            dve.wait_ge(ev("pos_in"), 32)
            chain(dve.tensor_copy(posf[:, 0:2], pos_i[:, 0:2]))
            chain(dve.tensor_scalar(posf[:, 0:2], posf[:, 0:2], float(META), None, ALU.add))
            dve.wait_ge(ev("tables_ready"), 6 + ROPE // 2)
            chain(dve.tensor_copy(posf[:, 2:3], pos_i[:, 3:4]))
            dve.wait_ge(ev("tables_ready"), 6 + ROPE // 2)
            half = ROPE // 2
            chain(dve.tensor_tensor(ang, posf.unsqueeze(2).broadcast_to([P, 3, half]),
                                    freq.unsqueeze(1).broadcast_to([P, 3, half]), ALU.mult))
            chain(dve.tensor_scalar(turns_, ang, float(1 / (2 * np.pi)), None, ALU.mult))
            chain(dve.tensor_scalar(turns_, turns_, ROUNDER, None, ALU.add))
            chain(dve.tensor_scalar(turns_, turns_, ROUNDER, None, ALU.subtract))
            for part in (TWO_PI_HI, TWO_PI_MID, TWO_PI_LO):
                chain(dve.scalar_tensor_tensor(ang, turns_, -part, ang, ALU.mult, ALU.add))
            chain(dve.tensor_scalar(ang, ang, 3.1415925, -3.1415925, ALU.min, ALU.max))
            chain(dve.tensor_scalar(turns_, ang, -1.0, None, ALU.mult))
            dve.tensor_tensor(turns_, turns_, ang, ALU.max).then_inc(ev("ang_ready"), 2)
            dve.wait_ge(ev("tables_ready"), 6 + ROPE // 2)
            chain(dve.tensor_copy(iota[:, :], iota_i[:, :]))

            dve.wait_ge(*nth("sin_ready", 1))
            chain(dve.tensor_scalar(sn[:, :, 0:half], sn[:, :, half:ROPE], -1.0, None, ALU.mult))
            dve.wait_ge(*nth("cos_ready", 1))
            chain(dve.tensor_copy(cs[:, :, half:ROPE], cs[:, :, 0:half]))

            dve.wait_ge(ev("zroot"), 1)
            chain(dve.reciprocal(zr, zroot))
            for tt in range(TT):
                dve.tensor_scalar(zq[:, tt, 0:QL], ps[:, tt, 0:QL], zr[:, 2 * tt:2 * tt + 1], None, ALU.mult)\
                    .then_inc(ev("zq_ready"), 1)
                dve.tensor_scalar(zq[:, tt, QL:QL + KVL], ps[:, tt, QL:QL + KVL], zr[:, 2 * tt + 1:2 * tt + 2], None,
                                  ALU.mult).then_inc(ev("zq_ready"), 1)
            dve.tensor_scalar(zq[0:META, 2, QL:QL + KVL], ps[0:META, 2, 0:KVL], zr[0:META, 4:5], None, ALU.mult)\
                .then_inc(ev("zq_ready"), 1)

            def rotate(dst, src, parts, tile, done):
                n_ = src.shape[1]
                tmp = rtmp[0:parts, 0:n_, :]

                def angles(v):
                    return v[0:parts, tile, :].unsqueeze(1).broadcast_to([parts, n_, v.shape[2]])
                chain(dve.tensor_tensor(dst, src, angles(cs), ALU.mult))
                chain(dve.tensor_tensor(tmp[:, :, 0:half], src[:, :, half:ROPE], angles(sn[:, :, 0:half]), ALU.mult))
                chain(dve.tensor_tensor(tmp[:, :, half:ROPE], src[:, :, 0:half], angles(sn[:, :, half:ROPE]), ALU.mult))
                dve.tensor_tensor(dst, dst, tmp, ALU.add).then_inc(done, 1)

            for tile in range(3):
                parts, bank, at = (P, tile, QL + KVL) if tile < TT else (META, 2, KVL)
                rotate(kr[0:parts, tile:tile + 1, :], ps[0:parts, bank, at:at + ROPE].unsqueeze(1), parts, tile,
                       ev("kr_turned"))
                dve.wait_ge(ev("kr_turned"), tile + 1)
            dve.wait_ge(ev("colsp"), 1)
            dve.tensor_copy(cols[:, :], ps[:, 2, 0:21]).then_inc(ev("cols_ready"), 1)
            dve.wait_ge(ev("cols_ready"), 1)
            chain(dve.tensor_scalar(cols[:, 20:21], cols[:, 20:21], 1.0 - LAMBDA_INIT, None, ALU.mult))
            dve.wait_ge(ev("params_in"), 144)
            dve.wait_ge(*nth("cqp", 1))
            for c in range(2):
                dve.tensor_scalar(cqT[:, c, :], ps[:, 7, c * TOK:(c + 1) * TOK], gq[:, c:c + 1], None, ALU.mult)\
                    .then_inc(ev("cqT_ready"), 1)
            dve.wait_ge(*nth("ckvp", 1))
            dve.tensor_scalar(ckvT, ps[:, 0, 0:COLS], gkv[:, 0:1], None, ALU.mult).then_inc(ev("ckvT_ready"), 1)
            for tt in range(TT):
                dve.wait_ge(*nth("qp", tt + 1))
                src = ps[:, 2 + 2 * tt:4 + 2 * tt, :].rearrange("p a b -> p (a b)")[:, 0:HEADS * QK]\
                    .rearrange("p (h d) -> p h d", h=HEADS)
                dve.tensor_copy(qs[:, tt, :, 0:NOPE], src[:, :, 0:NOPE]).then_inc(ev("qs_ready"), 1)
                rotate(qs[:, tt, :, NOPE:QK], src[:, :, NOPE:QK], P, tt, ev("qs_ready"))
                dve.wait_ge(ev("qs_ready"), 2 * tt + 2)
            for kb in range(3):
                parts = P if kb < 2 else META
                dve.wait_ge(*nth("vp", kb + 1))
                dve.tensor_copy(vtok[0:parts, kb, :], ps[0:parts, [6, 7, 0][kb], :]).then_inc(ev("v_ready"), 1)
            for c in range(CC):
                dve.wait_ge(*nth("xip", c + 1))
                dve.wait_ge(ev("gc_ready"), c + 1)
                dve.tensor_tensor(u[:, c, :], ps[:, conv_banks[c], 0:COLS], gc[:, c, :], ALU.mult).then_inc(ev("u_ready"), 1)
                dve.wait_ge(ev("u_ready"), c + 1)
                chain(dve.tensor_scalar(conv[:, c, :], u[:, c, META - 2:COLS - 2], cols[:, c:c + 1], None, ALU.mult))
                for w in (1, 2):
                    chain(dve.scalar_tensor_tensor(conv[:, c, :], u[:, c, META - 2 + w:COLS - 2 + w],
                                                   cols[:, 4 * w + c:4 * w + c + 1], conv[:, c, :], ALU.mult, ALU.add))

            dve.wait_ge(ev("tables_ready"), 6 + ROPE // 2)

            def mask_and_max(g):
                b_, keys = g % 2, SC_KEYS[g // 2]
                dve.wait_ge(ev("scp"), g + 1)
                if g >= 2:
                    dve.wait_ge(ev("pTp"), g - 1)
                m_ = mask[:, COLS - keys:COLS].unsqueeze(1).broadcast_to([P, 4, keys])
                dve.scalar_tensor_tensor(pr[:, b_, :, 0:keys], ps[:, 2:6, 0:keys], A_SCALE, m_, ALU.mult, ALU.add)\
                    .then_inc(ev("masked"), 1)
                dve.wait_ge(ev("masked"), g + 1)
                dve.tensor_reduce(nmax[:, 4 * b_:4 * b_ + 4], pr[:, b_, :, 0:keys], AX, ALU.max, negate=True)\
                    .then_inc(ev("nmax"), 1)

            mask_and_max(0)
            for g in range(4):
                tt = g // 2
                b_, keys = g % 2, SC_KEYS[tt]
                if g < 3:
                    mask_and_max(g + 1)
                dve.wait_ge(*nth("pexp", 4 * g + 4))
                sums = prow[:, 4 * b_:4 * b_ + 4]
                chain(dve.reciprocal(sums, sums))
                dve.tensor_tensor(pr[:, b_, :, 0:keys], pr[:, b_, :, 0:keys],
                                  sums.unsqueeze(2).broadcast_to([P, 4, keys]), ALU.mult).then_inc(ev("p_ready"), 1)
                dve.wait_ge(ev("pTp"), g + 1)
                dve.tensor_copy(pT[:, 0, :, :], ps[:, 6, :].rearrange("p (h c) -> p h c", h=4)).then_inc(ev("pT_ready"), 1)
                dve.tensor_copy(pT[0:META, 1 + tt, :, :] if tt == 0 else pT[0:META, 2, :, :],
                                ps[0:META, 2:6, COLS:COLS + P]).then_inc(ev("pT_ready"), 1)
                dve.wait_ge(*nth("gbp", g + 1))
                dve.tensor_tensor(conv[:, g, :], ps[:, 0, 0:TOK], conv[:, g, :], ALU.mult).then_inc(ev("conv_ready"), 1)
                if g % 2:
                    dve.wait_ge(ev("atp"), tt + 1)
                    dve.tensor_copy(attnT[:, :, tt * P:(tt + 1) * P], ps[:, 1, :].rearrange("p (c t) -> p c t", c=4))\
                        .then_inc(ev("attnT_raw"), 1)
            dve.wait_ge(ev("fine_root"), 1)
            dve.reciprocal(fine_r.rearrange("p a b -> p (a b)"), fine_root).then_inc(ev("fine_r"), 1)
            dve.wait_ge(ev("fine_r"), 1)
            dve.wait_ge(ev("mixc"), 4)
            dve.wait_ge(ev("gain_row"), 16)
            for tt in range(TT):
                dve.wait_ge(*nth("pap", tt + 1))
                part = mix[:, tt, :].rearrange("p (a b) -> p a b", a=2)
                dve.scalar_tensor_tensor(part, ps[:, (6, 0)[tt]:(8, 2)[tt], :], fine_r[:, 1, tt:tt + 1], part,
                                         ALU.mult, ALU.add).then_inc(ev("mixa"), 1)
                if tt:
                    take_turned(dve, "n1", 1, 0)
                one_over(dve, "o1", tt, chain)
                chain(dve.scalar_tensor_tensor(mix[:, tt, :], mix[:, tt, :], rstd[:, tt:tt + 1], gain_row[:, :],
                                               ALU.mult, ALU.mult))
                dve.tensor_tensor(h[:, tt, :], h[:, tt, :], mix[:, tt, :], ALU.add).then_inc(ev("mixed1"), 1)
                one_over(dve, "n1", tt, chain)
                dve.tensor_scalar(xs[:, tt, :], h[:, tt, :], rstd[:, tt:tt + 1], None, ALU.mult).then_inc(ev("xs_ready"), 1)
            take_turned(dve, "n1", 1, 1)
            route(dve, "m1", chain)
            for tt in range(TT):
                dve.wait_ge(ev("sh_sil"), tt + 1)
                dve.wait_ge(chunk_used, 16)
                dve.tensor_tensor(hs[:, 256 * tt:256 * tt + 256], sil[:, 256 * tt:256 * tt + 256],
                                  ps[:, 4 + tt, 256:512], ALU.mult).then_inc(ev("sh_h"), 1)
            place(dve, "m1", chain)
            dve.wait_ge(*nth("dist_i_ready", 1))
            chain(dve.tensor_copy(dist, dist_i))
            chain(dve.tensor_scalar(decay[:, 0, 0:P], dist[:, 0:P], 1.0, None, ALU.mult))
            chain(dve.tensor_copy(decay[:, 0, P:TOK], dist[:, P:TOK]))
            chain(dve.scalar_tensor_tensor(dist[:, P:TOK], decay[:, 0, P:TOK], -1.0, decay[:, 0, P:TOK], ALU.mult, ALU.max))
            chain(dve.memset(dist[0:64, P + 64:TOK], 1e33))
            for hh in range(DH):
                chain(dve.tensor_scalar(bias[:, hh, :], dist, -SLOPES[hh], None, ALU.mult))
            dve.tensor_copy(rnd[:, 0:1], eps).then_inc(ev("dist_ready"), 1)
            dve.wait_ge(*nth("lag_i_ready", 1))
            dve.tensor_copy(dist, dist_i).then_inc(ev("lag_ready"), 1)
            dve.wait_ge(ev("lams_in"), 64)
            chain(dve.tensor_tensor(lams[:, 0:2, :], lams[:, 0:2, :], lams[:, 2:4, :], ALU.mult))
            dve.tensor_reduce(lam_a, lams[:, 0:2, :], AX, ALU.add).then_inc(ev("lam_a"), 1)
            dve.wait_ge(ev("lam_b"), 1)
            chain(dve.scalar_tensor_tensor(lam, lam_b[:, 0:1], LAMBDA_INIT, lam_b[:, 1:2], ALU.add, ALU.subtract))
            moe_vector(dve, moes[0], chain)

            dve.wait_ge(ev("gain_row"), 32)
            for tt in range(TT):
                one_over(dve, "o2", tt, chain)
                chain(dve.scalar_tensor_tensor(xs[:, tt, :].rearrange("p (a b) -> p a b", a=2), ps[:, 2 * tt:2 * tt + 2, :],
                                               rstd[:, tt:tt + 1], gain_row[:, :].rearrange("p (a b) -> p a b", a=2),
                                               ALU.mult, ALU.mult))
                dve.tensor_tensor(h[:, tt, :], h[:, tt, :], xs[:, tt, :], ALU.add).then_inc(ev("h_two"), 1)
            for tt in range(TT):
                one_over(dve, "n2", tt, chain)
                dve.tensor_scalar(xs[:, tt, :], h[:, tt, :], rstd[:, tt:tt + 1], None, ALU.mult).then_inc(ev("xs_ready"), 1)
            for tt in range(TT):
                take_turned(dve, "n2", 2, tt)
            for c in range(DH):
                dve.wait_ge(*nth("qdp", c + 1))
                dve.tensor_copy(qdT[:, c, :], ps[:, c, 0:TOK]).then_inc(ev("qd_ready"), 1)
            dve.wait_ge(ev("sc2p"), 1)
            for mp in range(2):
                dve.scalar_tensor_tensor(sd0[:, 4 * mp:4 * mp + 4, :], ps[:, 2 + mp, :].rearrange("p (h k) -> p h k", h=DH),
                                         DD ** -0.5, bias[:, :, P:TOK], ALU.mult, ALU.add).then_inc(ev("biased0"), 1)
            dve.wait_ge(*nth("biased0", 2))
            dve.tensor_reduce(nmax, sd0, AX, ALU.max, negate=True).then_inc(ev("nmax2"), 1)
            dve.wait_ge(ev("sc2p"), 2)
            for mp in range(2):
                dve.scalar_tensor_tensor(sd1[:, 4 * mp:4 * mp + 4, :],
                                         ps[:, 4 + 2 * mp:6 + 2 * mp, :].rearrange("p a (h k) -> p (a h) k", h=2),
                                         DD ** -0.5, bias, ALU.mult, ALU.add).then_inc(ev("biased1"), 1)
            dve.wait_ge(*nth("biased1", 2))

            def combine(sd, tile, keys):
                dve.wait_ge(*nth("pexp2", 8 * tile + 8))
                chain(dve.reciprocal(prow, prow))
                chain(dve.tensor_scalar(prow[:, 4:8], prow[:, 4:8], lam, None, ALU.mult))
                chain(dve.tensor_tensor(sd, sd, prow.unsqueeze(2).broadcast_to([P, 8, keys]), ALU.mult))
                dve.tensor_tensor(sd[:, 0:4, :], sd[:, 0:4, :], sd[:, 4:8, :], ALU.subtract).then_inc(ev("a_ready"), 1)
                dve.wait_ge(ev("a_ready"), tile + 1)

            combine(sd0, 0, P)
            dve.tensor_reduce(nmax, sd1, AX, ALU.max, negate=True).then_inc(ev("nmax2"), 1)
            combine(sd1, 1, TOK)
            dve.wait_ge(ev("decay_ready"), 1)
            for hh in range(DH):
                dve.wait_ge(ev("rsp"), hh + 1)
                bank = [5, 6, 7, 0][hh]
                dve.scalar_tensor_tensor(sTm[:, hh, 0:TOK], ps[:, bank, 0:TOK], DD ** -0.5, decay[:, hh, :],
                                         ALU.mult, ALU.mult).then_inc(ev("rs_ready"), 1)
                dve.scalar_tensor_tensor(sTm[:, hh, TOK:384], ps[:, bank, TOK:384], DD ** -0.5, decay[:, hh, 0:P],
                                         ALU.mult, ALU.mult).then_inc(ev("rs_ready"), 1)
            n = 0
            for tt in range(TT):
                for kind, bank in ((0, 1 + 2 * tt), (1, 2 + 2 * tt)):
                    n += 1
                    dve.wait_ge(ev("hroot"), n)
                    r_ = hrs[:, tt, 4 * kind:4 * kind + 4]
                    chain(dve.reciprocal(r_, hroot[:, tt, 4 * kind:4 * kind + 4]))
                    dst = (on_da, on_r)[kind][:, tt, :]
                    hd = dst.rearrange("p (h e) -> p h e", h=DH)
                    last = dve.tensor_tensor(hd, ps[:, bank, :].rearrange("p (h e) -> p h e", h=DH),
                                             r_.unsqueeze(2).broadcast_to([P, DH, DV]), ALU.mult)
                    if kind:
                        chain(last)
                        dve.wait_ge(*nth("gr_ready", tt + 1))
                        last = dve.tensor_tensor(dst, dst, gr[:, tt, :], ALU.mult)
                    last.then_inc(ev("on_ready"), 1)
            for tt in range(TT):
                dve.wait_ge(*nth("out2p", tt + 1))
                hv = h[:, tt, :].rearrange("p (a b) -> p a b", a=2)
                dve.tensor_tensor(hv, ps[:, 1 + 2 * tt:3 + 2 * tt, :], hv, ALU.add).then_inc(ev("mixed2"), 1)
                if tt:
                    take_turned(dve, "n3", 3, 0)
                one_over(dve, "n3", tt, chain)
                dve.tensor_scalar(xs[:, tt, :], h[:, tt, :], rstd[:, tt:tt + 1], None, ALU.mult).then_inc(ev("xs_ready"), 1)
            take_turned(dve, "n3", 3, 1)
            route(dve, "m2", chain)
            place(dve, "m2", chain)
            moe_vector(dve, moes[1], chain)
            for tt in range(TT):
                hv = h[:, tt, :].rearrange("p (a b) -> p a b", a=2)
                dve.tensor_tensor(hv, ps[:, 2 * tt:2 * tt + 2, :], hv, ALU.add).then_inc(ev("h_four"), 1)
            dve.wait_ge(ev("gain_row"), 48)
            for tt in range(TT):
                one_over(dve, "o4", tt, chain)
                dve.scalar_tensor_tensor(xs[:, tt, :], h[:, tt, :], rstd[:, tt:tt + 1], gain_row[:, :],
                                         ALU.mult, ALU.mult).then_inc(ev("result"), 1)

        @block.tensor
        def _(pe):
            def chunk(n, spec):
                pe.wait_ge(landed[n % RING], 16 * (n // RING + 1))
                return chunk_view(n % RING, spec[1])

            pe.wait_ge(ev("tables_ready"), 6 + ROPE // 2)
            turn_first_tokens(pe)

            for j in range(2):
                w = chunk(j, phase_one[j])
                for tile in range(3):
                    parts, lo, c0 = (P, META + tile * P, 0) if tile < TT else (META, 0, QL)
                    for k in range(4):
                        mm = pe.matmul(ps[0:parts, tile, 0:ZC - c0], xT[:, 4 * j + k, lo:lo + parts], w[:, k, c0:ZC],
                                       start=(j == 0 and k == 0), stop=(j == 1 and k == 3))
                    if j == 1 and tile < TT:
                        mm.then_inc(ev("zp"), 1)
                mm.then_inc(chunk_used, 1)

            def features(n, c, bank, cols_, done, ks=range(KC)):
                ws = [chunk(n, ((), (4, 512))), chunk(n + 1, ((), (4, 512)))]
                for k in ks:
                    mm = pe.matmul(ps[:, bank, 0:cols_], ws[k // 4][:, k % 4, c * P:(c + 1) * P],
                                   xT[:, k, COLS - cols_:COLS], start=(k == 0), stop=(k == KC - 1), skip_group_check=True)
                    if c == 3 and k % 4 == 3:
                        mm.then_inc(chunk_used, 1)
                if c < 3 and k == KC - 1:
                    mm.then_inc(done, 1)

            def by_feature(n, banks, cols_, done, before_bank=None):
                for c in range(4):
                    if before_bank:
                        pe.wait_ge(*before_bank(c))
                    features(n, c, banks[c], cols_, done)

            by_feature(2, [3, 4, 5, 6], COLS, ev("gcp"))
            pe.wait_ge(ev("zq_ready"), 5)
            pe.wait_ge(ev("kr_turned"), 3)
            pe.wait_ge(ev("params_in"), 144)
            pe.transpose(ps[:, 2, 0:21], rows[:, :], ident[0:21, 0:21]).then_inc(ev("colsp"), 1)
            for c in range(2):
                for tt in range(TT):
                    tr = pe.transpose(ps[:, 7, c * TOK + tt * P:c * TOK + (tt + 1) * P], zq[:, tt, c:QL:2], ident[:, :])
            tr.then_inc(ev("cqp"), 1)
            for tt in range(TT):
                pe.transpose(ps[:, 0, META + tt * P:META + (tt + 1) * P], zq[:, tt, QL:QL + KVL], ident[:, :])
            pe.transpose(ps[:, 0, 0:META], zq[0:META, 2, QL:QL + KVL], ident[0:META, 0:META]).then_inc(ev("ckvp"), 1)
            for tt in range(TT):
                pe.transpose(ps[0:ROPE, 1, META + tt * P:META + (tt + 1) * P], kr[:, tt, :], ident[:, :])
            pe.transpose(ps[0:ROPE, 1, 0:META], kr[0:META, 2, :], ident[0:META, 0:META]).then_inc(ev("krp"), 1)
            w = chunk(4, phase_one[4])
            pe.wait_ge(*nth("cqT_ready", 2))
            pe.wait_ge(ev("gc_ready"), 3)
            pe.wait_ge(ev("cols_ready"), 1)
            for tt in range(TT):
                for lo, hi in ((0, 512), (512, 768)):
                    for k in range(2):
                        mm = pe.matmul(ps[:, 2 + 2 * tt + lo // 512, 0:hi - lo], cqT[:, k, tt * P:(tt + 1) * P],
                                       w[:, k, lo:hi], start=(k == 0), stop=(k == 1))
                if tt == 0:
                    mm.then_inc(ev("qp"), 1)
            mm.then_inc(chunk_used, 1)
            w = chunk(5, phase_one[5])[:, 0, :].rearrange("p (h d) -> p h d", h=HEADS)
            pe.wait_ge(*nth("ckvT_ready", 1))
            pe.wait_ge(ev("gc_ready"), 4)
            for kb in range(3):
                parts = P if kb < 2 else META
                pe.matmul(ps[0:parts, [6, 7, 0][kb], :], ckvT[:, kb * P:kb * P + parts], w[:, :, NOPE:NOPE + VD],
                          start=True, stop=True).then_inc(ev("vp"), 1)
            for hh in range(HEADS):
                if hh == 0:
                    pe.wait_ge(*nth("kr_ready", 1))
                elif hh < 4:
                    pe.wait_ge(ev("v_ready"), hh)
                else:
                    pe.wait_ge(*nth("kT_ready", hh - 3))
                mm = pe.matmul(ps[0:NOPE, conv_banks[hh % 4], 0:COLS], w[:, hh, 0:NOPE], ckvT, start=True, stop=True)
                if hh < HEADS - 1:
                    mm.then_inc(ev("kp"), 1)
            mm.then_inc(chunk_used, 1)
            by_feature(6, conv_banks, COLS, ev("xip"), lambda c: nth("kT_ready", 5 + c))
            for j, bank in enumerate((5, 2, 3, 4)):
                tt, h0 = j // 2, 4 * (j % 2)
                if j == 0:
                    pe.wait_ge(ev("qs_ready"), 4)
                for hh in range(4):
                    tr = pe.transpose(ps[0:QK, bank, hh * P:(hh + 1) * P], qs[:, tt, h0 + hh, :], ident[:, :])
                tr.then_inc(ev("qTp"), 1)

            def scores(g):
                tt, h0 = g // 2, 4 * (g % 2)
                keys = SC_KEYS[tt]
                if g == 0:
                    pe.wait_ge(ev("qT_ready"), 4)
                else:
                    pe.wait_ge(ev("masked"), g)
                for hh in range(4):
                    mm = pe.matmul(ps[:, 2 + hh, 0:keys], qT[0:QK, h0 + hh, tt * P:(tt + 1) * P],
                                   kT[0:QK, h0 + hh, 0:keys], start=True, stop=True)
                mm.then_inc(ev("scp"), 1)

            GATE_FIRST = 5

            def weigh_values(g):
                tt, h0 = g // 2, 4 * (g % 2)
                blocks = [(0, P, 6, 0), (P, META, None, 1)] if tt == 0 else [(0, P, 6, 0), (P, P, 7, 1), (2 * P, META, None, 2)]
                pe.wait_ge(ev("p_ready"), g + 1)
                if g > 0:
                    pe.wait_ge(ev("pT_ready"), 2 * g)
                    if g == 3:
                        pe.wait_ge(ev("pT7"), 1)
                for lo, n_, bank, _ in blocks:
                    for hh in range(4):
                        dst = ps[0:n_, 2 + hh, COLS:COLS + P] if bank is None else ps[0:n_, bank, hh * P:(hh + 1) * P]
                        tr = pe.transpose(dst, pr[:, g % 2, hh, lo:lo + n_], ident[:, :])
                tr.then_inc(ev("pTp"), 1)
                features(8, g, 0, TOK, ev("gbp"), range(GATE_FIRST, KC))
                pe.wait_ge(ev("pT_ready"), 2 * g + 2)
                if tt:
                    pe.wait_ge(ev("pT7"), g - 1)
                if g == 2:
                    pe.wait_ge(ev("attnT_raw"), 1)
                for hh in range(4):
                    head = h0 + hh
                    half = NOPE * (head % 2)
                    for b_, (lo, n_, bank, at) in enumerate(blocks):
                        mm = pe.matmul(ps[half:half + VD, 1, (head // 2) * P:(head // 2 + 1) * P],
                                       vtok[0:n_, lo // P, head * VD:(head + 1) * VD], pT[0:n_, at, hh, :],
                                       start=(b_ == 0), stop=(b_ == len(blocks) - 1), skip_group_check=True)
                if g % 2:
                    mm.then_inc(ev("atp"), 1)

            scores(0)
            for g in range(4):
                if g < 3:
                    scores(g + 1)
                if g == 0:
                    pe.wait_ge(ev("u_ready"), 4)
                else:
                    pe.wait_ge(ev("conv_ready"), g)
                features(8, g, 0, TOK, ev("gbp"), range(0, GATE_FIRST))
                weigh_values(g)

            def project(n, lhs, out_bank, done, total, before_tile=None):
                for tt in range(TT):
                    if before_tile:
                        before_tile(tt)
                    for j in range(total // 2):
                        w_ = chunk(n + j, ((), (2, D)))
                        for k in range(2):
                            for half in range(2):
                                mm = pe.matmul(ps[:, out_bank(tt, half), :], lhs[:, 2 * j + k, tt * P:(tt + 1) * P],
                                               w_[:, k, 512 * half:512 * half + 512],
                                               start=(j + k == 0), stop=(2 * j + k == total - 1))
                        if tt:
                            mm.then_inc(chunk_used, 1)
                    if tt == 0:
                        mm.then_inc(done, 1)

            pe.wait_ge(ev("masked"), 4)
            pe.wait_ge(ev("convG_ready"), 4)
            project(10, u, lambda tt, half: 2 + 2 * tt + half, ev("pcp"), 4)
            pe.wait_ge(*nth("conv_sq_ready", 1))
            pe.wait_ge(*nth("attn_sq_ready", 1))
            pe.wait_ge(ev("attnT_raw"), 2)
            for i_ in range(2):
                for tt in range(TT):
                    mm = pe.matmul(ps[:, 1, 2 * i_ + tt:2 * i_ + tt + 1], sq[:, i_, tt * P:(tt + 1) * P], inv512,
                                   start=True, stop=True)
            mm.then_inc(ev("fine_ms"), 1)
            pe.wait_ge(ev("attnG_ready"), 4)
            pe.wait_ge(ev("fine_root"), 1)
            project(12, gc, lambda tt, half: [6, 7, 0, 1][2 * tt + half], ev("pap"), 4)

            pe.wait_ge(ev("mixc"), 4)
            for tt in range(TT):
                turn_tokens(pe, "n1", tt)
                turned(pe, "n1", tt)
                logits(pe, "m1", tt)
            turn_logits(pe, "m1")
            for which in range(2):
                w = chunk(14 + which, phase_one[14 + which])
                for tt in range(TT):
                    for k in range(KC):
                        mm = pe.matmul(ps[:, 4 + tt, 256 * which:256 * which + 256],
                                       xT[:, k, META + tt * P:META + (tt + 1) * P], w[:, k, :],
                                       start=(k == 0), stop=(k == KC - 1))
                mm.then_inc(chunk_used, 1)
            positions_of(pe, "m1")
            pe.wait_ge(ev("sh_h"), 2)
            for tt in range(TT):
                for c in range(2):
                    tr = pe.transpose(ps[:, 6, (2 * tt + c) * P:(2 * tt + c + 1) * P],
                                      hs[:, 256 * tt + c:256 * tt + 256:2], ident[:, :])
            tr.then_inc(ev("sh_hTp"), 1)
            w = chunk(16, phase_one[16])
            pe.wait_ge(ev("sh_hT"), 1)
            for tt in range(TT):
                for half in range(2):
                    for c in range(2):
                        mm = pe.matmul(ps[:, 2 * tt + half, :], hT[:, 2 * tt + c, :], w[:, c, 512 * half:512 * half + 512],
                                       start=(c == 0), stop=False, skip_group_check=True)
            mm.then_inc(chunk_used, 1)
            moe_tensor(pe, moes[0])

            pe.wait_ge(*nth("h_two", 2))
            for tt in range(TT):
                turn_tokens(pe, "n2", tt)
            turned(pe, "n2", 1)
            base2 = moes[0]["next"]

            def by_token(n, banks, done, wait=None):
                if wait:
                    pe.wait_ge(*wait)
                for tt in range(TT):
                    for j in range(2):
                        w_ = chunk(n + j, ((), (4, 512)))
                        for k in range(4):
                            mm = pe.matmul(ps[:, banks[tt], :], xT[:, 4 * j + k, META + tt * P:META + (tt + 1) * P],
                                           w_[:, k, :], start=(j + k == 0), stop=(j == 1 and k == 3))
                        if tt:
                            mm.then_inc(chunk_used, 1)
                    if tt == 0:
                        mm.then_inc(done, 1)

            by_feature(base2, [0, 1, 2, 3], TOK, ev("qdp"))
            by_feature(base2 + 2, [4, 5, 6, 7], TOK, ev("kdp"))
            by_token(base2 + 4, [0, 1], ev("vdp"), (ev("qd_ready"), 2))
            pe.wait_ge(ev("qd_ready"), 4)
            pe.wait_ge(*nth("kd_ready", 4))
            for hh in range(DH):
                for mp in range(2):
                    rows_ = slice(DD * mp, DD * mp + DD)
                    mm = pe.matmul(ps[:, 2 + mp, hh * P:(hh + 1) * P], qdT[rows_, hh, 0:P], kdT[rows_, hh, 0:P],
                                   start=True, stop=True)
            mm.then_inc(ev("sc2p"), 1)
            for hh in range(DH):
                for mp in range(2):
                    rows_ = slice(DD * mp, DD * mp + DD)
                    mm = pe.matmul(ps[:, 4 + 2 * mp + hh // 2, (hh % 2) * TOK:(hh % 2 + 1) * TOK],
                                   qdT[rows_, hh, P:TOK], kdT[rows_, hh, :], start=True, stop=True)
            mm.then_inc(ev("sc2p"), 1)
            by_feature(base2 + 6, [0, 1, 2, 3], TOK, ev("rp"),
                       lambda c: nth("vd_ready", c + 1) if c < 2 else nth("biased0", c - 1))
            by_token(base2 + 8, [4, 5], ev("vrp"), nth("biased1", 2))
            for j in range(3):
                pe.wait_ge(ev("a_ready"), 1 + (j > 0))
                pe.wait_ge(*nth("r_ready", 4))
                for hh in range(DH):
                    src = sd0[:, hh, :] if j == 0 else sd1[:, hh, (j - 1) * P:j * P]
                    tr = pe.transpose(ps[:, j, hh * P:(hh + 1) * P], src, ident[:, :])
                tr.then_inc(ev("aTp"), 1)
            for hh in range(DH):
                rows_ = slice(DD * (hh % 2), DD * (hh % 2) + DD)
                bank = [5, 6, 7, 0][hh]
                if hh == 0:
                    pe.wait_ge(*nth("vr_ready", 2))
                elif hh == 3:
                    pe.wait_ge(ev("aT_ready"), 1)
                pe.matmul(ps[:, bank, 0:TOK], rT[rows_, 2 + hh // 2, 0:P], rT[rows_, hh // 2, :], start=True, stop=True)
                pe.matmul(ps[:, bank, TOK:384], rT[rows_, 2 + hh // 2, P:TOK], rT[rows_, hh // 2, P:TOK],
                          start=True, stop=True).then_inc(ev("rsp"), 1)
            pe.wait_ge(ev("aT_ready"), 3)
            for tt in range(TT):
                for hh in range(DH):
                    ks = [(0, 0)] if tt == 0 else [(1, 0), (2, 1)]
                    for b_, (at, kt) in enumerate(ks):
                        mm = pe.matmul(ps[:, 1 + 2 * tt, hh * DV:(hh + 1) * DV], aT[:, at, hh, :],
                                       vda[:, kt, hh * DV:(hh + 1) * DV], start=(b_ == 0), stop=(b_ == len(ks) - 1))
                mm.then_inc(ev("odp"), 1)
                pe.wait_ge(ev("rs_ready"), 8)
                for hh in range(DH):
                    ks = [(0, 0)] if tt == 0 else [(P, 0), (TOK, 1)]
                    for b_, (at, kt) in enumerate(ks):
                        mm = pe.matmul(ps[:, 2 + 2 * tt, hh * DV:(hh + 1) * DV], sTm[:, hh, at:at + P],
                                       vr[:, kt, hh * DV:(hh + 1) * DV], start=(b_ == 0), stop=(b_ == len(ks) - 1))
                mm.then_inc(ev("orp"), 1)
            by_token(base2 + 10, [6, 7], ev("grp"))

            def turn_heads(tt):
                if tt:
                    pe.wait_ge(*nth("gr_ready", 2))
                for kind in range(2):
                    j = 2 * tt + kind
                    pe.wait_ge(ev("on_ready"), j + 1)
                    src = (on_da, on_r)[kind]
                    for c in range(DH):
                        tr = pe.transpose(ps[:, 5 + j if j < 3 else 0, c * P:(c + 1) * P], src[:, tt, c * P:(c + 1) * P],
                                          ident[:, :])
                    tr.then_inc(ev("mTp"), 1)
                pe.wait_ge(ev("mT_ready"), 2 * tt + 2)

            project(base2 + 12, mixT, lambda tt, half: 1 + 2 * tt + half, ev("out2p"), 8, turn_heads)
            for tt in range(TT):
                turn_tokens(pe, "n3", tt)
                turned(pe, "n3", tt)
                logits(pe, "m2", tt)
            turn_logits(pe, "m2")
            positions_of(pe, "m2")
            moe_tensor(pe, moes[1])


_INS = ['x', 'positions', 'meta_tokens', 'pre_mix_norm', 'w_in', 'q_norm', 'w_uq', 'kv_norm', 'w_ukv', 'conv_w',
        'attn_out_norm', 'conv_out_norm', 'w_out', 'post_mix_norm', 'pre_ffn_norm', 'w_group_router',
        'b_group_router', 'w_expert_router', 'b_expert_router', 'w_gate', 'w_up', 'w_down', 'w_sh_gate', 'w_sh_up',
        'w_sh_down', 'post_ffn_norm', 'attn_norm_g_2', 'w_in_2', 'da_lambda_q1_2', 'da_lambda_k1_2',
        'da_lambda_q2_2', 'da_lambda_k2_2', 'da_subln_g_2', 'w_out_2', 'ffn_norm_g_2', 'router_group_w_2',
        'router_group_b_2', 'router_expert_w_2', 'router_expert_b_2', 'expert_w_gate_2', 'expert_w_up_2',
        'expert_w_down_2', 'final_norm_g_2']
_OUTS = [((1, 256, 1024), 'float32')]


def kernel(**inputs):
    import numpy as _np
    import concourse.bacc as _bacc
    from concourse import mybir as _mybir
    from concourse.bass_utils import run_bass_kernel_spmd as _run

    nc = _bacc.Bacc("TRN2", target_bir_lowering=False, num_devices=1)
    arrays, tensors = {}, {}
    for name in _INS:
        a = _np.ascontiguousarray(inputs[name])
        arrays[f"in_{name}_dram"] = a
        tensors[name] = nc.dram_tensor(f"in_{name}_dram", a.shape, _mybir.dt.from_np(a.dtype), kind="ExternalInput").ap()
    shape, dtype = _OUTS[0]
    result = nc.dram_tensor("out_0_dram", shape, _mybir.dt.from_np(_np.dtype(dtype)), kind="ExternalOutput").ap()
    two_block_kernel(nc, tensors, result)
    r = _run(nc, [arrays], core_ids=[0])
    return r.results[0]["out_0_dram"]
```
